# Optimizing a Trainium2 kernel written in Bass

```python
import jax, jax.numpy as jnp
from jax import lax
import numpy as np
import math

D_MODEL = 1024
BATCH = 1
SEQ = 1024
DEPTH = 1

PLE_DIM = 256
EXPAND = 2
D_MIX = EXPAND * D_MODEL
D_HGRN = D_MIX // 2
D_FOX = D_MIX - D_HGRN
HGRN_HEAD_DIM = 128
HGRN_HEADS = D_HGRN // HGRN_HEAD_DIM
FOX_HEAD_DIM = 64
FOX_HEADS = D_FOX // FOX_HEAD_DIM
HGRN_CHUNK = 32
FOX_BLOCK = 128
NORM_EPS = 1e-6
D_IN = 4 * D_HGRN + 4 * D_FOX + FOX_HEADS
SPLIT_POINTS = tuple(D_HGRN * j for j in range(1, 5)) + tuple(4 * D_HGRN + D_FOX * j for j in range(1, 5))


def rmsnorm(x, w):
    xf = x.astype(jnp.float32)
    y = xf * lax.rsqrt(jnp.mean(xf * xf, axis=-1, keepdims=True) + NORM_EPS)
    return (y * w.astype(jnp.float32)).astype(x.dtype)

def hgrn_lower_bounds(logits):
    sm = jax.nn.softmax(logits.astype(jnp.float32), axis=0)
    c = jnp.cumsum(sm, axis=0)
    return c - c[0:1]

def hgrn2_branch(q, fz, i, lb, gn_w):
    B, S, _ = q.shape
    H, dk, C = HGRN_HEADS, HGRN_HEAD_DIM, HGRN_CHUNK
    N = S // C
    f32 = jnp.float32
    fz = fz.astype(f32)
    lb = lb.astype(f32)
    log_f = jnp.logaddexp(jnp.log(lb), jnp.log1p(-lb) + jax.nn.log_sigmoid(fz))
    k = (1.0 - lb) * jax.nn.sigmoid(-fz)

    def to_chunks(t):
        return t.astype(f32).reshape(B, N, C, H, -1).transpose(1, 0, 3, 2, 4)

    qc = to_chunks(q) * (dk ** -0.5)
    kc, vc, gc = to_chunks(k), to_chunks(i), to_chunks(log_f)
    causal = jnp.tril(jnp.ones((C, C), dtype=bool))[:, :, None]

    def step(state, xs):
        qb, kb, vb, gb = xs
        b = jnp.cumsum(gb, axis=2)
        diff = b[:, :, :, None, :] - b[:, :, None, :, :]
        decay = jnp.exp(jnp.where(causal, diff, -jnp.inf))
        scores = jnp.einsum('bhtd,bhsd,bhtsd->bhts', qb, kb, decay)
        o = (jnp.einsum('bhts,bhsv->bhtv', scores, vb)
             + jnp.einsum('bhtd,bhdv->bhtv', qb * jnp.exp(b), state))
        b_last = b[:, :, -1:, :]
        new_state = (jnp.exp(b_last[:, :, 0, :])[..., None] * state
                     + jnp.einsum('bhsd,bhsv->bhdv', kb * jnp.exp(b_last - b), vb))
        return new_state, o

    state0 = jnp.zeros((B, H, dk, vc.shape[-1]), f32)
    _, o = lax.scan(step, state0, (qc, kc, vc, gc))
    o = o.transpose(1, 0, 3, 2, 4).reshape(B, S, H, -1)
    o = o * lax.rsqrt(jnp.mean(o * o, axis=-1, keepdims=True) + NORM_EPS)
    o = o * gn_w.astype(f32).reshape(H, -1)
    return o.reshape(B, S, D_HGRN).astype(q.dtype)

def fox_branch(q, k, v, fz, fb):
    B, S, _ = q.shape
    H, d, Q = FOX_HEADS, FOX_HEAD_DIM, FOX_BLOCK
    f32 = jnp.float32

    def heads(t):
        return t.reshape(B, S, H, d).transpose(0, 2, 1, 3)

    q, k, v = heads(q), heads(k), heads(v)
    log_f = jax.nn.log_sigmoid(fz.astype(f32) + fb.astype(f32))
    F = jnp.cumsum(log_f, axis=1).transpose(0, 2, 1)
    scale = d ** -0.5
    outs = []
    for blk in range(S // Q):
        q0, q1 = blk * Q, (blk + 1) * Q
        qb = q[:, :, q0:q1]
        kb, vb = k[:, :, :q1], v[:, :, :q1]
        logits = (jnp.einsum('bhtd,bhsd->bhts', qb, kb).astype(f32) * scale
                  + F[:, :, q0:q1, None] - F[:, :, None, :q1])
        mask = jnp.arange(q0, q1)[:, None] >= jnp.arange(q1)[None, :]
        probs = jax.nn.softmax(jnp.where(mask, logits, -jnp.inf), axis=-1)
        outs.append(jnp.einsum('bhts,bhsd->bhtd', probs.astype(v.dtype), vb))
    o = jnp.concatenate(outs, axis=2)
    return o.transpose(0, 2, 1, 3).reshape(B, S, D_FOX)

def first_inputs(seed: int = 0) -> dict:
    key = jax.random.key(seed)
    ks = jax.random.split(key, 11)
    f32 = jnp.float32
    x = jax.random.normal(ks[0], (BATCH, SEQ, D_MODEL), f32)
    p = jax.random.normal(ks[1], (DEPTH, BATCH, SEQ, PLE_DIM), f32)
    norm_w = 1.0 + 0.1 * jax.random.normal(ks[2], (DEPTH, D_MODEL), f32)
    w_in = jax.random.normal(ks[3], (DEPTH, D_MODEL, D_IN), f32) * D_MODEL ** -0.5
    fox_fb = jax.random.uniform(ks[4], (DEPTH, FOX_HEADS), f32, 1.0, 4.0)
    hgrn_gn = 1.0 + 0.1 * jax.random.normal(ks[5], (DEPTH, D_HGRN), f32)
    hgrn_lb_logits = 0.5 * jax.random.normal(ks[6], (DEPTH, D_HGRN), f32)
    w_out = jax.random.normal(ks[7], (DEPTH, D_MIX, D_MODEL), f32) * D_MIX ** -0.5
    w_ple = jax.random.normal(ks[8], (DEPTH, PLE_DIM, D_MODEL), f32) * PLE_DIM ** -0.5
    w_ple_gate = jax.random.normal(ks[9], (DEPTH, D_MODEL, D_MODEL), f32) * D_MODEL ** -0.5
    final_norm_w = 1.0 + 0.1 * jax.random.normal(ks[10], (D_MODEL,), f32)
    return {"x": x, "p": p, "norm_w": norm_w, "w_in": w_in, "fox_fb": fox_fb,
            "hgrn_gn": hgrn_gn, "hgrn_lb_logits": hgrn_lb_logits, "w_out": w_out,
            "w_ple": w_ple, "w_ple_gate": w_ple_gate, "final_norm_w": final_norm_w}

def first_block(x, p, norm_w, w_in, fox_fb, hgrn_gn, hgrn_lb_logits, w_out, w_ple, w_ple_gate, final_norm_w):
    lb_all = hgrn_lower_bounds(hgrn_lb_logits)
    h = x
    for i in range(DEPTH):
        u = rmsnorm(h, norm_w[i])
        proj = jnp.einsum('bsd,de->bse', u, w_in[i])
        hq, hf, hi, hg, fq, fk, fv, fg, fz = jnp.split(proj, SPLIT_POINTS, axis=-1)
        y_h = hgrn2_branch(hq, hf, hi, lb_all[i], hgrn_gn[i]) * jax.nn.silu(hg)
        y_f = fox_branch(fq, fk, fv, fz, fox_fb[i]) * jax.nn.silu(fg)
        y = jnp.concatenate([y_h, y_f], axis=-1)
        h = h + jnp.einsum('bse,ed->bsd', y, w_out[i])
        ple = jnp.einsum('bsk,kd->bsd', p[i], w_ple[i])
        h = h + jax.nn.sigmoid(jnp.einsum('bsd,de->bse', h, w_ple_gate[i])) * ple
    return rmsnorm(h, final_norm_w)


DEPTH_2 = 2

GRID_W = 64
CTX_LEN = 256
N_MIXERS = 2
HEAD_DIM = 64
N_HEADS = D_MODEL // HEAD_DIM
A_KV_HEADS = 4
A_GROUPS = N_HEADS // A_KV_HEADS
A_WINDOW = 128
A_BLOCK = 128
A_INNER = N_HEADS * HEAD_DIM
A_KV_DIM = A_KV_HEADS * HEAD_DIM
A_IN_DIM = 2 * A_INNER + 2 * A_KV_DIM
B_KH_MAX = 8
B_KW = 16
B_QW = 16
B_REG_W = 2 * B_KW
B_INNER = N_HEADS * HEAD_DIM
B_IN_DIM = 4 * B_INNER
ROPE_BASE = 10000.0
LN_EPS = 1e-5
NEG_INF = -1e30
DEEPNORM_ALPHA = (2.0 * DEPTH_2) ** 0.25
DEEPNORM_BETA = (8.0 * DEPTH_2) ** -0.25
N_LAYERS_A = (DEPTH_2 + 1) // 2
N_LAYERS_B = DEPTH_2 // 2


def layer_norm(x, g, b):
    xf = x.astype(jnp.float32)
    mu = jnp.mean(xf, axis=-1, keepdims=True)
    var = jnp.mean(jnp.square(xf - mu), axis=-1, keepdims=True)
    y = (xf - mu) * lax.rsqrt(var + LN_EPS)
    return (y * g.astype(jnp.float32) + b.astype(jnp.float32)).astype(x.dtype)

def axial_rope_tables(n_tok):
    t = jnp.arange(n_tok)
    row = (t // GRID_W).astype(jnp.float32)
    col = (t % GRID_W).astype(jnp.float32)
    n_freq = HEAD_DIM // 4
    inv = ROPE_BASE ** (-jnp.arange(n_freq, dtype=jnp.float32) / n_freq)
    ang_r = row[:, None] * inv[None]
    ang_c = col[:, None] * inv[None]
    return (jnp.cos(ang_r), jnp.sin(ang_r), jnp.cos(ang_c), jnp.sin(ang_c))

def _rotate(x, cos, sin):
    a, b = jnp.split(x, 2, axis=-1)
    cos = cos[None, :, None, :].astype(x.dtype)
    sin = sin[None, :, None, :].astype(x.dtype)
    return jnp.concatenate([a * cos - b * sin, b * cos + a * sin], axis=-1)

def apply_axial_rope(x, rope):
    cos_r, sin_r, cos_c, sin_c = rope
    xr, xc = jnp.split(x, 2, axis=-1)
    return jnp.concatenate([_rotate(xr, cos_r, sin_r), _rotate(xc, cos_c, sin_c)], axis=-1)

def ctx_attention(q, k, v, sink):
    B, C = q.shape[0], q.shape[1]
    s = jnp.einsum('bqkgd,bckd->bkgqc', q, k).astype(jnp.float32) * (HEAD_DIM ** -0.5)
    if sink is not None:
        s_sink = jnp.broadcast_to(sink[None, :, :, None, None], s.shape[:-1] + (1,))
        p = jax.nn.softmax(jnp.concatenate([s, s_sink], axis=-1), axis=-1)[..., :C]
    else:
        p = jax.nn.softmax(s, axis=-1)
    o = jnp.einsum('bkgqc,bckd->bqkgd', p.astype(v.dtype), v)
    return o.reshape(B, C, -1)

def _split_a(p):
    return jnp.split(p, [A_INNER, A_INNER + A_KV_DIM, A_INNER + 2 * A_KV_DIM], axis=-1)

def mixer_a(u, uc, w_in, w_out, sink, rope, ctx_out):
    B, S, _ = u.shape
    C = uc.shape[1]
    scale = HEAD_DIM ** -0.5
    q, k, v, g = _split_a(u @ w_in)
    q = apply_axial_rope(q.reshape(B, S, N_HEADS, HEAD_DIM), rope).reshape(B, S, A_KV_HEADS, A_GROUPS, HEAD_DIM)
    k = apply_axial_rope(k.reshape(B, S, A_KV_HEADS, HEAD_DIM), rope)
    v = v.reshape(B, S, A_KV_HEADS, HEAD_DIM)
    qc, kc, vc, gc = _split_a(uc @ w_in)
    kc = kc.reshape(B, C, A_KV_HEADS, HEAD_DIM)
    vc = vc.reshape(B, C, A_KV_HEADS, HEAD_DIM)
    sink_l = sink.reshape(A_KV_HEADS, A_GROUPS).astype(jnp.float32)
    span = A_BLOCK + 2 * A_WINDOW
    pad = ((0, 0), (A_WINDOW, A_WINDOW), (0, 0), (0, 0))
    kp = jnp.pad(k, pad)
    vp = jnp.pad(v, pad)

    def block(bi):
        start = bi * A_BLOCK
        qb = lax.dynamic_slice_in_dim(q, start, A_BLOCK, axis=1)
        kb = lax.dynamic_slice_in_dim(kp, start, span, axis=1)
        vb = lax.dynamic_slice_in_dim(vp, start, span, axis=1)
        qi = start + jnp.arange(A_BLOCK)
        kj = start - A_WINDOW + jnp.arange(span)
        mask = (jnp.abs(qi[:, None] - kj[None, :]) <= A_WINDOW) & (kj >= 0)[None, :] & (kj < S)[None, :]
        s_lat = jnp.einsum('bqkgd,bjkd->bkgqj', qb, kb).astype(jnp.float32) * scale
        s_lat = jnp.where(mask, s_lat, NEG_INF)
        s_ctx = jnp.einsum('bqkgd,bckd->bkgqc', qb, kc).astype(jnp.float32) * scale
        s_sink = jnp.broadcast_to(sink_l[None, :, :, None, None], s_lat.shape[:-1] + (1,))
        p = jax.nn.softmax(jnp.concatenate([s_lat, s_ctx, s_sink], axis=-1), axis=-1)
        p_lat = p[..., :span].astype(v.dtype)
        p_ctx = p[..., span:span + C].astype(v.dtype)
        o = jnp.einsum('bkgqj,bjkd->bqkgd', p_lat, vb) + jnp.einsum('bkgqc,bckd->bqkgd', p_ctx, vc)
        return o.reshape(B, A_BLOCK, A_INNER)

    o = lax.map(block, jnp.arange(S // A_BLOCK))
    o = jnp.transpose(o, (1, 0, 2, 3)).reshape(B, S, A_INNER)
    y = (o * jax.nn.silu(g)) @ w_out
    if not ctx_out:
        return y, None
    oc = ctx_attention(qc.reshape(B, C, A_KV_HEADS, A_GROUPS, HEAD_DIM), kc, vc, sink_l)
    yc = (oc * jax.nn.silu(gc)) @ w_out
    return y, yc

def mixer_b(u, uc, w_in, w_out, rel_bias, ctx_out):
    B, S, _ = u.shape
    C = uc.shape[1]
    rows = S // GRID_W
    kh = min(B_KH_MAX, rows)
    scale = HEAD_DIM ** -0.5
    q, k, v, g = jnp.split(u @ w_in, 4, axis=-1)
    q = q.reshape(B, rows, GRID_W, N_HEADS, HEAD_DIM)
    k = k.reshape(B, rows, GRID_W, N_HEADS, HEAD_DIM)
    v = v.reshape(B, rows, GRID_W, N_HEADS, HEAD_DIM)
    qc, kc, vc, gc = jnp.split(uc @ w_in, 4, axis=-1)
    kc = kc.reshape(B, C, N_HEADS, HEAD_DIM)
    vc = vc.reshape(B, C, N_HEADS, HEAD_DIM)

    n_cb = GRID_W // B_QW
    c0 = np.arange(n_cb) * B_QW
    cs_blk = np.clip(c0 - B_KW // 2, 0, GRID_W - B_REG_W)
    key_col = cs_blk[:, None] + np.arange(B_REG_W)
    q_col = c0[:, None] + np.arange(B_QW)
    cs_q = np.clip(q_col - B_KW // 2, 0, GRID_W - B_KW)
    col_mask = (key_col[:, None, :] >= cs_q[:, :, None]) & (key_col[:, None, :] < cs_q[:, :, None] + B_KW)
    col_idx = np.clip(key_col[:, None, :] - q_col[:, :, None] + (B_KW - 1), 0, 2 * B_KW - 2)
    key_col = jnp.asarray(key_col, dtype=jnp.int32)
    col_idx = jnp.asarray(col_idx, dtype=jnp.int32)
    col_mask = jnp.asarray(col_mask)[:, :, None, :]
    bias_tab = rel_bias.astype(jnp.float32)

    def row_block(r):
        rs = jnp.clip(r - kh // 2, 0, rows - kh)
        q_r = lax.dynamic_index_in_dim(q, r, axis=1, keepdims=False).reshape(B, n_cb, B_QW, N_HEADS, HEAD_DIM)
        k_rows = lax.dynamic_slice_in_dim(k, rs, kh, axis=1)
        v_rows = lax.dynamic_slice_in_dim(v, rs, kh, axis=1)
        k_reg = k_rows[:, :, key_col]
        v_reg = v_rows[:, :, key_col]
        s = jnp.einsum('bnqhd,brnjhd->bhnqrj', q_r, k_reg).astype(jnp.float32) * scale
        row_idx = rs + jnp.arange(kh) - r + (B_KH_MAX - 1)
        bias = bias_tab[:, row_idx[:, None, None, None], col_idx[None]]
        s = s + jnp.transpose(bias, (0, 2, 3, 1, 4))[None]
        s = jnp.where(col_mask, s, NEG_INF).reshape(B, N_HEADS, n_cb, B_QW, kh * B_REG_W)
        s_ctx = jnp.einsum('bnqhd,bchd->bhnqc', q_r, kc).astype(jnp.float32) * scale
        p = jax.nn.softmax(jnp.concatenate([s, s_ctx], axis=-1), axis=-1)
        p_lat = p[..., :kh * B_REG_W].reshape(B, N_HEADS, n_cb, B_QW, kh, B_REG_W).astype(v.dtype)
        p_ctx = p[..., kh * B_REG_W:].astype(v.dtype)
        o = jnp.einsum('bhnqrj,brnjhd->bnqhd', p_lat, v_reg) + jnp.einsum('bhnqc,bchd->bnqhd', p_ctx, vc)
        return o.reshape(B, GRID_W, B_INNER)

    o = lax.map(row_block, jnp.arange(rows))
    o = jnp.transpose(o, (1, 0, 2, 3)).reshape(B, S, B_INNER)
    y = (o * jax.nn.silu(g)) @ w_out
    if not ctx_out:
        return y, None
    oc = ctx_attention(qc.reshape(B, C, N_HEADS, 1, HEAD_DIM), kc[:, :, :, :], vc, None)
    yc = (oc * jax.nn.silu(gc)) @ w_out
    return y, yc

def second_inputs(seed: int = 0) -> dict:
    key = jax.random.key(seed)
    ks = jax.random.split(key, 14)
    f32 = jnp.float32
    d = D_MODEL
    return {
        "x": jax.random.normal(ks[0], (BATCH, SEQ, d), f32),
        "c": jax.random.normal(ks[1], (BATCH, d), f32),
        "ctx": jax.random.normal(ks[2], (BATCH, CTX_LEN, d), f32),
        "c_ctx": jax.random.normal(ks[3], (d,), f32),
        "w_ada": jax.random.normal(ks[4], (DEPTH_2, d, 3 * d), f32) * d ** -0.5,
        "b_ada": 0.01 * jax.random.normal(ks[5], (DEPTH_2, 3 * d), f32),
        "ln_g": 1.0 + 0.05 * jax.random.normal(ks[6], (DEPTH_2, d), f32),
        "ln_b": 0.02 * jax.random.normal(ks[7], (DEPTH_2, d), f32),
        "a_w_in": jax.random.normal(ks[8], (N_LAYERS_A, d, A_IN_DIM), f32) * d ** -0.5,
        "a_w_out": jax.random.normal(ks[9], (N_LAYERS_A, A_INNER, d), f32) * (A_INNER ** -0.5 * DEEPNORM_BETA),
        "a_sink": 0.5 * jax.random.normal(ks[10], (N_LAYERS_A, N_HEADS), f32),
        "b_w_in": jax.random.normal(ks[11], (N_LAYERS_B, d, B_IN_DIM), f32) * d ** -0.5,
        "b_w_out": jax.random.normal(ks[12], (N_LAYERS_B, B_INNER, d), f32) * (B_INNER ** -0.5 * DEEPNORM_BETA),
        "b_rel_bias": 0.5 * jax.random.normal(ks[13], (N_LAYERS_B, N_HEADS, 2 * B_KH_MAX - 1, 2 * B_KW - 1), f32),
    }

def second_block(x, c, ctx, c_ctx, w_ada, b_ada, ln_g, ln_b, a_w_in, a_w_out, a_sink, b_w_in, b_w_out, b_rel_bias):
    S = x.shape[1]
    rope = axial_rope_tables(S)
    silu_c = jax.nn.silu(c)
    silu_cc = jax.nn.silu(c_ctx)
    h, hc = x, ctx
    for i in range(DEPTH_2):
        shift, scale, gate = jnp.split(silu_c @ w_ada[i] + b_ada[i], 3, axis=-1)
        shift_c, scale_c, gate_c = jnp.split(silu_cc @ w_ada[i] + b_ada[i], 3, axis=-1)
        ctx_out = i < DEPTH_2 - 1
        u = h * (1.0 + scale[:, None, :]) + shift[:, None, :]
        uc = hc * (1.0 + scale_c) + shift_c
        j = i // N_MIXERS
        if i % N_MIXERS == 0:
            y, yc = mixer_a(u, uc, a_w_in[j], a_w_out[j], a_sink[j], rope, ctx_out)
        else:
            y, yc = mixer_b(u, uc, b_w_in[j], b_w_out[j], b_rel_bias[j], ctx_out)
        h = layer_norm(DEEPNORM_ALPHA * h + gate[:, None, :] * y, ln_g[i], ln_b[i])
        if ctx_out:
            hc = layer_norm(DEEPNORM_ALPHA * hc + gate_c * yc, ln_g[i], ln_b[i])
    return h


def setup_inputs(seed=0):
    out = dict(first_inputs(seed))
    for name, value in second_inputs(seed + 1).items():
        if name != "x":
            out[name + "_2"] = value
    return out


def reference(
    x, p, norm_w, w_in, fox_fb, hgrn_gn, hgrn_lb_logits, w_out, w_ple, w_ple_gate, final_norm_w,
    c_2, ctx_2, c_ctx_2, w_ada_2, b_ada_2, ln_g_2, ln_b_2, a_w_in_2, a_w_out_2, a_sink_2,
    b_w_in_2, b_w_out_2, b_rel_bias_2,
):
    x = first_block(
        x, p, norm_w, w_in, fox_fb, hgrn_gn, hgrn_lb_logits, w_out, w_ple, w_ple_gate,
        final_norm_w,
    )
    return second_block(
        x, c_2, ctx_2, c_ctx_2, w_ada_2, b_ada_2, ln_g_2, ln_b_2, a_w_in_2, a_w_out_2, a_sink_2,
        b_w_in_2, b_w_out_2, b_rel_bias_2,
    )


_drawn_inputs = setup_inputs


def setup_inputs(seed=0):
    import zlib

    import numpy as np

    out = dict(_drawn_inputs(seed))
    spreads = {}
    factors = {'b_ada_2': 8.0, 'a_sink_2': 45.56, 'b_rel_bias_2': 4.457, 'ctx_2': 2.828}
    for name, (base, spread) in spreads.items():
        noise = np.random.default_rng([zlib.crc32(name.encode()), seed]).standard_normal(out[name].shape)
        drawn = base * np.exp(spread * noise) if base else spread * noise
        out[name] = __import__('jax').numpy.asarray(drawn.astype(out[name].dtype))
    for name, factor in factors.items():
        out[name] = (out[name] * factor).astype(out[name].dtype)
    return out
```

```python
from contextlib import ExitStack

import numpy as np
import concourse.bass as bass
from concourse import mybir

F32 = mybir.dt.float32
F32R = mybir.dt.float32r
ALU = mybir.AluOpType
ACT = mybir.ActivationFunctionType
AX = mybir.AxisListType.X
ds = bass.ds

P = 128
T = 1024
D = 1024
C = 256
TC = T + C
KT = D // P
CH = 512
PLE = 256
HG = 8
PAIRS = 8
HD = 64
HGRN_CHUNK = 32
LEVELS = 7
GRID_W = 64
BIG = -1e30
EPS = 1e-6
LN_EPS = 1e-5
ALPHA = (2.0 * 2) ** 0.25
ADA_UNITS = 48

V_NORM, V_GN, V_FINAL, V_LNG, V_LNB, V_BADA, V_LB, V_END = 0, 8, 16, 24, 40, 56, 104, 112
K_ID, K_TRI, K_WIN, K_COL, K_ROW, K_END = 0, 128, 256, 256 + 640, 256 + 640 + 64, 256 + 640 + 64 + 9

U_HGRN = 0
U_FZ = U_HGRN + 4 * HG
U_FOX = U_FZ + 2
U_OUT = U_FOX + 4 * PAIRS
U_PLE = U_OUT + 2 * KT
U_GATE = U_PLE + 2
U_A = U_GATE + KT
U_A_OUT = U_A + 20
U_B = U_A_OUT + KT
U_B_OUT = U_B + 4 * PAIRS
UNITS = U_B_OUT + KT
assert UNITS % 2 == 0


def build_program(nc, a, stop=99):
    ctx = ExitStack()

    def sb(name, shape, dt=F32, at=None):
        return (at or ctx).enter_context(nc.sbuf_tensor(name, shape, dt))

    def sem(name):
        return ctx.enter_context(nc.semaphore(name))

    with ctx:
        ps = ctx.enter_context(nc.psum_tensor("ps", [P, 8 * CH], F32))

        def bank(b, n=1):
            return ps[:, b * CH:(b + n) * CH]

        h_dram = nc.dram_tensor("residual", [KT, P, TC], F32).ap()
        y_dram = nc.dram_tensor("y_parts", [2, 16, P, TC], F32).ap()

        consts = sb("consts", [P, K_END])
        vecs = sb("vecs", [P, V_END])
        ident = consts[:, K_ID:K_ID + P]
        ada = sb("ada", [P, ADA_UNITS, 2])
        adv = sb("adv", [P, ADA_UNITS, 2])
        ones_mean = sb("ones_mean", [P, P])
        small = sb("small", [P, 8])
        raw = sb("raw", [P, 2, KT * P])
        w_hi = sb("w_hi", [P, 2, KT * P], F32R)
        w_lo = sb("w_lo", [P, 2, KT * P], F32R)

        def whi(slot, k):
            return w_hi[:, slot, k * P:(k + 1) * P]

        def wlo(slot, k):
            return w_lo[:, slot, k * P:(k + 1) * P]

        loaded = sem("loaded")
        x_loaded = sem("x_loaded")
        raw_loaded = [sem("raw_loaded0"), sem("raw_loaded1")]
        w_ready = sem("w_ready")
        w_used = sem("w_used")
        consts_set = sem("consts_set")

        block1 = ctx.enter_context(ExitStack())
        u_hi = sb("u_hi", [P, KT, T], F32R, block1)
        u_lo = sb("u_lo", [P, KT, T], F32R, block1)
        u_ready = sem("u_ready")

        def project(pe, n, slot, hi, lo, chunks, done, tiles=range(KT), first=0, start=True, stop=True, last=True):
            pe.wait_ge(w_ready, n + 1)
            for c, (cols, out, waits) in enumerate(chunks):
                for s, v in waits:
                    pe.wait_ge(s, v)
                for i, k in enumerate(tiles):
                    for p, (w, u) in enumerate(((whi, hi), (whi, lo), (wlo, hi))):
                        mm = pe.matmul(out, w(slot, k), u[:, first + i, cols],
                                       start=start and i == 0 and p == 0,
                                       stop=stop and i == len(tiles) - 1 and p == 2)
                mm.then_inc(w_used if last and c == len(chunks) - 1 else done, 1)

        def stream_loads(sp):
            for s in range(2):
                sp.dma_start(raw[:, s, :], a["w_stream"][s]).then_inc(raw_loaded[s], 16)

        def stream_loads_rest(sp):
            with sp.Fori(1, UNITS // 2) as i:
                for s in range(2):
                    sp.wait_ge(w_ready, i * 2 + (s - 1))
                    sp.dma_start(raw[:, s, :], a["w_stream"][ds(i * 2 + s, 1)].rearrange("a p n -> (a p) n")
                                 ).then_inc(raw_loaded[s], 16)

        def split_unit(pool, s):
            zero = small[:, 0:1].broadcast_to([P, KT * P])
            pool.tensor_tensor(w_hi[:, s, :], raw[:, s, :], zero, ALU.add)
            pool.drain()
            pool.tensor_tensor(w_lo[:, s, :], raw[:, s, :], w_hi[:, s, :].bitcast(F32),
                               ALU.subtract).then_inc(w_ready, 1)

        def stream_splits(pool):
            pool.wait_ge(consts_set, 1)
            for s in range(2):
                pool.wait_ge(raw_loaded[s], 16)
                split_unit(pool, s)
            with pool.Fori(1, UNITS // 2) as i:
                for s in range(2):
                    pool.wait_ge(raw_loaded[s], i * 16 + 16)
                    pool.wait_ge(w_used, i * 2 + (s - 1))
                    split_unit(pool, s)

        ph1 = ctx.enter_context(ExitStack())
        x_sb = sb("x_sb", [P, KT, T], at=ph1)
        sq1 = sb("sq1", [P, 2, T], at=ph1)
        rstd1 = sb("rstd1", [P, T], at=ph1)
        ph1.close()
        n1_sq = sem("n1_sq")
        n1_sum = sem("n1_sum")
        n1_sd = sem("n1_sd")
        n1_scaled = sem("n1_scaled")
        n1_hi = sem("n1_hi")

        def norm1_act(act):
            act.wait_ge(x_loaded, 16 * KT)
            act.wait_ge(consts_set, 1)
            for k in range(KT):
                if k >= 2:
                    act.wait_ge(n1_sum, k - 1)
                nc.scalar.activation(sq1[:, k % 2, :], x_sb[:, k, :], ACT.Square).then_inc(n1_sq, 1)
            act.wait_ge(n1_sum, KT)
            nc.scalar.activation(rstd1[:], bank(0, 2), ACT.Sqrt, bias=small[:, 1:2]).then_inc(n1_sd, 1)
            for k in range(KT):
                act.wait_ge(n1_scaled, k + 1)
                nc.scalar.copy(u_hi[:, k, :], x_sb[:, k, :]).then_inc(n1_hi, 1)

        def norm1_pe(pe):
            pe.wait_ge(consts_set, 1)
            for k in range(KT):
                pe.wait_ge(n1_sq, k + 1)
                for c in range(2):
                    mm = pe.matmul(bank(c), ones_mean[:], sq1[:, k % 2, c * CH:(c + 1) * CH],
                                   start=k == 0, stop=k == KT - 1)
                mm.then_inc(n1_sum, 1)

        def norm1_dve(dve):
            dve.memset(small[:, 0:1], 0.0)
            dve.memset(small[:, 1:2], EPS)
            dve.memset(small[:, 2:3], LN_EPS)
            dve.memset(ones_mean[:], 1.0 / D)
            dve.drain().then_inc(consts_set, 1)
            dve.wait_ge(loaded, 32)
            dve.wait_ge(n1_sd, 1)
            dve.reciprocal(rstd1[:], rstd1[:])
            dve.drain()
            for k in range(KT):
                dve.scalar_tensor_tensor(x_sb[:, k, :], x_sb[:, k, :], vecs[:, V_NORM + k:V_NORM + k + 1],
                                         rstd1[:], ALU.mult, ALU.mult).then_inc(n1_scaled, 1)
            for k in range(KT):
                dve.wait_ge(n1_hi, k + 1)
                dve.tensor_tensor(u_lo[:, k, :], x_sb[:, k, :], u_hi[:, k, :].bitcast(F32),
                                  ALU.subtract).then_inc(u_ready, 1)

        ph2 = ctx.enter_context(ExitStack())
        hgrn_masks = sb("hgrn_masks", [P, 2, T], at=ph2)
        z_f = sb("z_f", [P, T], at=ph2)
        t_a = sb("t_a", [P, T], at=ph2)
        t_g = sb("t_g", [P, T], at=ph2)
        k_t = sb("k_t", [P, T], at=ph2)
        q_t = sb("q_t", [P, T], at=ph2)
        i_t = sb("i_t", [P, T], at=ph2)
        b32 = sb("b32", [P, T], at=ph2)
        b128 = sb("b128", [P, T], at=ph2)
        off = sb("off", [P, 8, 4], at=ph2)
        tile_decay = sb("tile_decay", [P, 8], at=ph2)
        lev = sb("lev", [P, LEVELS, T], at=ph2)
        q_in = sb("q_in", [P, T], at=ph2)
        k_out = sb("k_out", [P, T], at=ph2)
        k_tok = sb("k_tok", [P, 8, P], at=ph2)
        i_tok = sb("i_tok", [P, 8, P], at=ph2)
        masked = sb("masked", [P, 8, P], at=ph2)
        scores = sb("scores", [P, 2, P], at=ph2)
        state = sb("state", [P, 2, P], at=ph2)
        silu_h = sb("silu_h", [P, T], at=ph2)
        o_n = sb("o_n", [P, T], at=ph2)
        ssq = sb("ssq", [P, 8], at=ph2)
        rs8 = sb("rs8", [P, 8], at=ph2)
        head_vec = sb("head_vec", [P, 4], at=ph2)
        lnom = sb("lnom", [P, 8], at=ph2)
        yh_hi = sb("yh_hi", [P, T], F32R, ph2)
        yh_lo = sb("yh_lo", [P, T], F32R, ph2)
        ph2.close()

        h_chunk = sem("h_chunk")
        h_z = sem("h_z")
        h_t2 = sem("h_t2")
        h_k = sem("h_k")
        h_q = sem("h_q")
        h_it = sem("h_it")
        h_tr = sem("h_tr")
        h_tok = sem("h_tok")
        h_e = sem("h_e")
        h_x = sem("h_x")
        h_kout = sem("h_kout")
        h_ops = sem("h_ops")
        h_sg = sem("h_sg")
        h_lv = sem("h_lv")
        h_sc = sem("h_sc")
        h_ds = sem("h_ds")
        h_s = sem("h_s")
        h_o = sem("h_o")
        h_sd = sem("h_sd")
        h_on = sem("h_on")
        h_yt = sem("h_yt")
        h_y = sem("h_y")
        h_hi = sem("h_hi")
        h_lo = sem("h_lo")
        h_spill = sem("h_spill")
        lb_set = sem("lb_set")
        lb_exp = sem("lb_exp")

        def hgrn_pe(pe):
            pe.wait_ge(u_ready, KT)
            with pe.Fori(0, HG) as h:
                n = h * 4 + U_HGRN

                def unit(j, b, waits):
                    project(pe, n + j, j % 2, u_hi, u_lo,
                            [(slice(c * CH, c * CH + CH), bank(b + c), waits if c == 0 else []) for c in range(2)],
                            h_chunk)

                unit(0, 0, [(h_sc, h * 8)])
                unit(1, 2, [])
                unit(2, 4, [(h_on, h)])
                unit(3, 0, [(h_z, h + 1)])
                pe.wait_ge(h_it, h + 1)
                pe.wait_ge(h_yt, h)
                for j in range(8):
                    mm = pe.transpose(ps[:, 6 * CH + j * P:6 * CH + (j + 1) * P], i_t[:, j * P:(j + 1) * P], ident)
                mm.then_inc(h_tr, 1)
                pe.wait_ge(h_ops, h + 1)

                def level_products(j):
                    if j == 0:
                        pe.wait_ge(h_sg, h + 1)
                    if j >= 2:
                        pe.wait_ge(h_sc, h * 8 + (j - 1))
                    t = slice(j * P, (j + 1) * P)
                    for lv in range(LEVELS + 1):
                        o = ps[:, (j % 2) * 2 * CH + lv * P:(j % 2) * 2 * CH + (lv + 1) * P]
                        if lv < LEVELS:
                            mm = pe.matmul(o, lev[:, lv, t], lev[:, lv, t], start=True, stop=True)
                        else:
                            mm = pe.matmul(o, k_t[:, t], q_t[:, t], start=True, stop=True)
                    mm.then_inc(h_lv, 1)

                level_products(0)
                pe.wait_ge(h_kout, h + 1)
                pe.wait_ge(h_tok, h * 2 + 1)
                for j in range(8):
                    mm = pe.transpose(ps[:, 6 * CH + j * P:6 * CH + (j + 1) * P], k_out[:, j * P:(j + 1) * P], ident)
                mm.then_inc(h_tr, 1)
                for j in range(8):
                    if j < 7:
                        level_products(j + 1)
                        if j == 0:
                            pe.wait_ge(h_tok, h * 2 + 2)
                        else:
                            pe.wait_ge(h_s, h * 7 + j)
                        pe.matmul(ps[:, 6 * CH:6 * CH + P], k_tok[:, j, :], i_tok[:, j, :],
                                  start=True, stop=True).then_inc(h_ds, 1)
                    pe.wait_ge(h_sc, h * 8 + (j + 1))
                    o = ps[:, 4 * CH + j * P:4 * CH + (j + 1) * P]
                    mm = pe.matmul(o, scores[:, j % 2, :], i_tok[:, j, :], start=True, stop=j == 0)
                    if j:
                        pe.wait_ge(h_s, h * 7 + j)
                        mm = pe.matmul(o, q_in[:, j * P:(j + 1) * P], state[:, j % 2, :], start=False, stop=True)
                    mm.then_inc(h_o, 1)
                pe.wait_ge(h_on, h + 1)
                for j in range(8):
                    mm = pe.transpose(ps[:, 6 * CH + j * P:6 * CH + (j + 1) * P], o_n[:, j * P:(j + 1) * P], ident)
                mm.then_inc(h_y, 1)

        def hgrn_act(act):
            act.wait_ge(lb_set, 1)
            act.dma_start(hgrn_masks[:], a["hgrn_masks"]).then_inc(loaded, 16)
            nc.scalar.activation(lnom[:], lnom[:], ACT.Exp).then_inc(lb_exp, 1)
            act.wait_ge(lb_set, 2)
            nc.scalar.activation(lnom[:], lnom[:], ACT.Ln, bias=1.0, scale=-1.0).then_inc(lb_exp, 1)
            with act.Fori(0, HG) as h:
                act.wait_ge(h_chunk, h * 4 + 1)
                act.wait_ge(w_used, h * 4 + 1)
                nc.scalar.copy(z_f[:], bank(0, 2))
                nc.scalar.activation(t_a[:], bank(0, 2), ACT.Abs)
                act.drain()
                nc.scalar.activation(t_a[:], t_a[:], ACT.Exp, scale=-1.0)
                act.drain()
                nc.scalar.activation(t_a[:], t_a[:], ACT.Ln, bias=1.0).then_inc(h_z, 1)
                act.wait_ge(h_t2, h + 1)
                nc.scalar.activation(k_t[:], t_a[:], ACT.Exp).then_inc(h_k, 1)
                for lv in range(LEVELS):
                    act.wait_ge(h_e, h * 9 + (lv + 1))
                    nc.scalar.activation(lev[:, lv, :], lev[:, lv, :], ACT.Exp).then_inc(h_x, 1)
                act.wait_ge(h_e, h * 9 + 9)
                nc.scalar.activation(q_in[:], b128[:], ACT.Exp).then_inc(h_x, 1)
                nc.scalar.activation(k_out[:], k_out[:], ACT.Exp)
                nc.scalar.activation(tile_decay[:], b128[:].rearrange("p (j t) -> p j t", j=8)[:, :, P - 1],
                                     ACT.Exp).then_inc(h_x, 1)
                act.wait_ge(h_chunk, h * 4 + 2)
                act.wait_ge(w_used, h * 4 + 2)
                nc.scalar.activation(q_t[:], bank(2, 2), ACT.Copy, scale=float(P) ** -0.5).then_inc(h_q, 1)
                act.wait_ge(h_chunk, h * 4 + 3)
                act.wait_ge(w_used, h * 4 + 3)
                nc.scalar.copy(i_t[:], bank(4, 2)).then_inc(h_it, 1)
                act.wait_ge(h_chunk, h * 4 + 4)
                act.wait_ge(w_used, h * 4 + 4)
                nc.scalar.activation(silu_h[:], bank(0, 2), ACT.Silu).then_inc(h_sg, 1)
                act.wait_ge(h_tr, h * 2 + 1)
                nc.scalar.copy(i_tok[:].rearrange("p j t -> p (j t)"), bank(6, 2)).then_inc(h_tok, 1)
                act.wait_ge(h_tr, h * 2 + 2)
                nc.scalar.copy(k_tok[:].rearrange("p j t -> p (j t)"), bank(6, 2)).then_inc(h_tok, 1)
                for j in range(8):
                    if j % 4 == 0:
                        act.wait_ge(h_o, h * 8 + (j + 4))
                    nc.scalar.activation(q_in[:, j * P:(j + 1) * P], ps[:, 4 * CH + j * P:4 * CH + (j + 1) * P],
                                         ACT.Square, accum_out=ssq[:, j:j + 1])
                act.drain()
                nc.scalar.activation(ssq[:], ssq[:], ACT.Sqrt, bias=small[:, 1:2], scale=1.0 / P).then_inc(h_sd, 1)
                act.wait_ge(h_yt, h + 1)
                act.wait_ge(h_spill, h * 32)
                nc.scalar.copy(yh_hi[:], o_n[:]).then_inc(h_hi, 1)
                act.wait_ge(h_lo, h + 1)
                for part, src in ((0, yh_hi), (1, yh_lo)):
                    act.dma_start(y_dram[part, ds(h, 1), :, 0:T].rearrange("a p t -> (a p) t"), src[:].bitcast(F32)
                                  ).then_inc(h_spill, 16)

        def hgrn_dve(dve):
            lb_in = vecs[:, V_LB:V_LB + 8]
            dve.wait_ge(u_ready, KT)
            dve.tensor_tensor(lnom[:], lb_in, lb_in, ALU.subtract).then_inc(lb_set, 1)
            dve.wait_ge(lb_exp, 1)
            dve.reciprocal(ssq[:], lnom[:])
            dve.drain()
            dve.tensor_tensor(lnom[:], lnom[:], ssq[:], ALU.mult)
            dve.drain()
            dve.tensor_tensor(lnom[:], lnom[:], lnom[:], ALU.subtract)
            dve.drain().then_inc(lb_set, 1)
            dve.wait_ge(lb_exp, 2)
            dve.wait_ge(loaded, 48)
            with dve.Fori(0, HG) as h:
                dve.tensor_copy(head_vec[:, 0:1], vecs[:, ds(h + V_GN, 1)])
                dve.tensor_copy(head_vec[:, 1:2], lnom[:, ds(h, 1)])
                dve.drain()
                dve.wait_ge(h_z, h + 1)
                dve.scalar_tensor_tensor(t_g[:], z_f[:], 0.0, t_a[:], ALU.min, ALU.subtract)
                dve.drain()
                dve.tensor_tensor(t_a[:], t_g[:], z_f[:], ALU.subtract)
                dve.tensor_scalar(t_g[:], t_g[:], head_vec[:, 1:2], None, ALU.add)
                dve.drain()
                dve.tensor_scalar(t_a[:], t_a[:], head_vec[:, 1:2], None, ALU.add).then_inc(h_t2, 1)
                dve.tensor_tensor_scan(b32[:], hgrn_masks[:, 1, :], t_g[:], 0.0, ALU.mult, ALU.add)
                dve.drain()
                tot = b32[:].rearrange("p (j c t) -> p j c t", c=4, t=32)[:, :, :, 31]
                dve.memset(off[:, :, 0], 0.0)
                dve.tensor_copy(off[:, :, 1], tot[:, :, 0])
                dve.tensor_tensor(off[:, :, 2], tot[:, :, 0], tot[:, :, 1], ALU.add)
                dve.drain()
                dve.tensor_tensor(off[:, :, 3], off[:, :, 2], tot[:, :, 2], ALU.add)
                dve.drain()
                dve.tensor_tensor(b128[:].rearrange("p (c t) -> p c t", t=32),
                                  b32[:].rearrange("p (c t) -> p c t", t=32),
                                  off[:].rearrange("p j c -> p (j c)").unsqueeze(2).broadcast_to([P, 32, 32]), ALU.add)
                dve.drain()
                for lv in range(LEVELS):
                    H = 1 << lv
                    b = (b32 if 2 * H <= HGRN_CHUNK else b128)[:].rearrange("p (g r t) -> p g r t", r=2, t=H)
                    e = lev[:, lv, :].rearrange("p (g r t) -> p g r t", r=2, t=H)
                    mid = b[:, :, 0, H - 1:H].broadcast_to([P, T // (2 * H), H])
                    dve.tensor_tensor(e[:, :, 0, :], mid, b[:, :, 0, :], ALU.subtract)
                    dve.tensor_tensor(e[:, :, 1, :], b[:, :, 1, :], mid, ALU.subtract).then_inc(h_e, 1)
                bt = b128[:].rearrange("p (j t) -> p j t", t=P)
                dve.tensor_tensor(k_out[:].rearrange("p (j t) -> p j t", t=P),
                                  bt[:, :, P - 1:P].broadcast_to([P, 8, P]), bt, ALU.subtract).then_inc(h_e, 2)
                dve.wait_ge(h_k, h + 1)
                for lv in range(LEVELS):
                    H = 1 << lv
                    e = lev[:, lv, :].rearrange("p (g r t) -> p g r t", r=2, t=H)
                    k = k_t[:].rearrange("p (g r t) -> p g r t", r=2, t=H)
                    dve.wait_ge(h_x, h * 9 + (lv + 1))
                    dve.tensor_tensor(e[:, :, 0, :], e[:, :, 0, :], k[:, :, 0, :], ALU.mult)
                dve.wait_ge(h_x, h * 9 + 9)
                dve.tensor_tensor(k_out[:], k_out[:], k_t[:], ALU.mult).then_inc(h_kout, 1)
                dve.wait_ge(h_q, h + 1)
                dve.tensor_tensor(q_in[:], q_in[:], q_t[:], ALU.mult)
                for lv in range(LEVELS):
                    H = 1 << lv
                    e = lev[:, lv, :].rearrange("p (g r t) -> p g r t", r=2, t=H)
                    q = q_t[:].rearrange("p (g r t) -> p g r t", r=2, t=H)
                    dve.tensor_tensor(e[:, :, 1, :], e[:, :, 1, :], q[:, :, 1, :], ALU.mult)
                dve.drain().then_inc(h_ops, 1)

                def tile_scores(j):
                    dve.drain()
                    dve.wait_ge(h_lv, h * 8 + (j + 1))
                    if j >= 2:
                        dve.wait_ge(h_o, h * 8 + (j - 1))
                    dve.tensor_tensor(masked[:].rearrange("p l t -> p (l t)"), bank((j % 2) * 2, 2),
                                      hgrn_masks[:, 0, :], ALU.mult)
                    dve.drain()
                    dve.tensor_reduce(scores[:, j % 2, :], masked[:].rearrange("p l t -> p t l"), AX,
                                      ALU.add).then_inc(h_sc, 1)

                tile_scores(0)
                for j in range(7):
                    tile_scores(j + 1)
                    if j:
                        dve.drain()
                    dve.wait_ge(h_ds, h * 7 + (j + 1))
                    if j == 0:
                        dve.tensor_copy(state[:, 1, :], ps[:, 6 * CH:6 * CH + P]).then_inc(h_s, 1)
                    else:
                        dve.wait_ge(h_o, h * 8 + j)
                        dve.scalar_tensor_tensor(state[:, (j + 1) % 2, :], state[:, j % 2, :],
                                                 tile_decay[:, j:j + 1], ps[:, 6 * CH:6 * CH + P],
                                                 ALU.mult, ALU.add).then_inc(h_s, 1)
                dve.wait_ge(h_sd, h + 1)
                dve.reciprocal(rs8[:], ssq[:])
                dve.drain()
                dve.tensor_tensor(o_n[:].rearrange("p (j t) -> p j t", t=P),
                                  bank(4, 2).rearrange("p (j t) -> p j t", t=P),
                                  rs8[:].unsqueeze(2).broadcast_to([P, 8, P]), ALU.mult).then_inc(h_on, 1)
                dve.wait_ge(h_y, h + 1)
                dve.scalar_tensor_tensor(o_n[:], bank(6, 2), head_vec[:, 0:1], silu_h[:],
                                         ALU.mult, ALU.mult).then_inc(h_yt, 1)
                dve.wait_ge(h_hi, h + 1)
                dve.tensor_tensor(yh_lo[:], o_n[:], yh_hi[:].bitcast(F32), ALU.subtract).then_inc(h_lo, 1)

        class Attention:

            def __init__(self, name, blocks, halves, width, keys, q_cols, v_blocks, area):
                self.blocks, self.halves, self.name = blocks, halves, name
                self.NA = 2 * len(blocks)
                self.groups = []
                for u in range(self.NA):
                    n = len(blocks[u // 2]["chunks"])
                    self.groups += [(u, c, min(c + 4, n)) for c in range(0, n, 4)]
                self.NG = len(self.groups)
                assert self.NG % 2 == 0
                self.NH = len(halves)
                self.q2 = [sb(f"{name}_q2_{i}", [P, q_cols], F32R, area) for i in range(2)]
                self.l = sb(f"{name}_l", [P, 2, width], at=area)
                self.pt = sb(f"{name}_pt", [P, 2, CH], at=area)
                self.nm = sb(f"{name}_nm", [P, self.NA, 2], at=area)
                self.o_s = sb(f"{name}_o", [P, CH], at=area)
                self.r_s = sb(f"{name}_r", [P, CH], at=area)
                self.silu = sb(f"{name}_silu", [P, q_cols], at=area)
                self.y = sb(f"{name}_y", [P, q_cols], at=area)
                self.y_hi = sb(f"{name}_y_hi", [P, q_cols], F32R, area)
                self.y_lo = sb(f"{name}_y_lo", [P, q_cols], F32R, area)
                self.scored = sem(f"{name}_scored")
                self.shifted = sem(f"{name}_shifted")
                self.exped = sem(f"{name}_exped")
                self.turned = sem(f"{name}_turned")
                self.out_of = [sem(f"{name}_copied_act"), sem(f"{name}_copied_dve")]
                self.valued = sem(f"{name}_valued")
                self.left = sem(f"{name}_left")
                self.gated = sem(f"{name}_gated")
                self.hi_done = sem(f"{name}_hi_done")
                self.lo_done = sem(f"{name}_lo_done")
                self.spilled = sem(f"{name}_spilled")
                self.chunk = sem(f"{name}_chunk")
                self.steps = self.sequence()

            def sequence(self):
                steps, last = [("S", 0)], None

                def value(g):
                    steps.append(("V", g))
                    u = self.groups[g][0]
                    if g == self.NG - 1 or self.groups[g + 1][0] != u:
                        for hf, bs in enumerate(self.halves):
                            if u // 2 == bs[-1]:
                                steps.append(("O", hf, u % 2))
                                if u % 2:
                                    steps.append(("F", hf))

                for g, (u, c0, _) in enumerate(self.groups):
                    if c0 == 0 and u + 1 < self.NA:
                        steps.append(("S", u + 1))
                    steps.append(("T", g))
                    if last is not None:
                        value(last)
                    last = g
                value(last)
                return steps

            def half_of(self, block):
                return next(i for i, bs in enumerate(self.halves) if block in bs)

            def pe(self, pe, it, k2a, k2b, v, before_scores, before_turn, before_value):
                for step in self.steps:
                    if step[0] == "S":
                        u = step[1]
                        blk = self.blocks[u // 2]
                        pe.wait_ge(self.shifted, it * self.NA + max(u - 1, 0))
                        for s, w in before_scores(u):
                            pe.wait_ge(s, w)
                        q = self.q2[u % 2][:, blk["b"] * P:(blk["b"] + 1) * P]
                        for pc, kc, n in blk["runs"]:
                            o = ps[:, (u % 2) * 2 * CH + pc:(u % 2) * 2 * CH + pc + n]
                            pe.matmul(o, q, k2a[u % 2][:, kc:kc + n], start=True, stop=False)
                            mm = pe.matmul(o, q, k2b[u % 2][:, kc:kc + n], start=False, stop=True)
                        mm.then_inc(self.scored, 1)
                    elif step[0] == "T":
                        g = step[1]
                        u, c0, c1 = self.groups[g]
                        pe.wait_ge(self.exped, it * self.NA + (u + 1))
                        pe.wait_ge(self.out_of[g % 2], it * (self.NG // 2) + g // 2)
                        for s, w in before_turn(g):
                            pe.wait_ge(s, w)
                        for c in range(c0, c1):
                            pc, n, _ = self.blocks[u // 2]["chunks"][c]
                            mm = pe.transpose(ps[0:n, (4 + g % 2) * CH + (c - c0) * P:(4 + g % 2) * CH + (c - c0 + 1) * P],
                                              self.l[:, u % 2, pc:pc + n], ident)
                        mm.then_inc(self.turned, 1)
                    elif step[0] == "V":
                        g = step[1]
                        u, c0, c1 = self.groups[g]
                        blk, hd = self.blocks[u // 2], u % 2
                        pe.wait_ge(self.out_of[g % 2], it * (self.NG // 2) + (g // 2 + 1))
                        hf = self.half_of(u // 2)
                        if u // 2 == self.halves[hf][0] and c0 == 0:
                            pe.wait_ge(self.left, it * (2 * self.NH) + max(2 * (hf - 1) + hd + 1, 0) if hf else
                                       it * (2 * self.NH))
                            for s, w in before_value(hf):
                                pe.wait_ge(s, w)
                        o0 = (6 + hd) * CH + (u // 2 - self.halves[hf][0]) * P
                        for c in range(c0, c1):
                            _, n, vb = blk["chunks"][c]
                            mm = pe.matmul(ps[:, o0:o0 + P], v[hd][0:n, vb, :],
                                           self.pt[0:n, g % 2, (c - c0) * P:(c - c0 + 1) * P],
                                           start=c == 0, stop=c == len(blk["chunks"]) - 1)
                        mm.then_inc(self.valued, 1)

            def last_group(self, u):
                return max(g for g, x in enumerate(self.groups) if x[0] == u)

            def act(self, act, it):
                for step in self.steps:
                    if step[0] == "S":
                        u = step[1]
                        w = self.blocks[u // 2]["width"]
                        act.wait_ge(self.shifted, it * self.NA + (u + 1))
                        nc.scalar.activation(self.l[:, u % 2, 0:w], self.l[:, u % 2, 0:w], ACT.Exp, scale=-1.0,
                                             bias=self.nm[:, u, 1:2]).then_inc(self.exped, 1)
                    elif step[0] == "T" and step[1] % 2 == 0:
                        self.copy_group(act, it, step[1], nc.scalar.copy)
                    elif step[0] == "O":
                        hf, hd = step[1:]
                        u = 2 * self.halves[hf][-1] + hd
                        n = len(self.halves[hf]) * P
                        act.wait_ge(self.valued, it * self.NG + (self.last_group(u) + 1))
                        act.wait_ge(self.gated, it * self.NH + hf)
                        o = ps[:, (6 + hd) * CH:(6 + hd) * CH + n]
                        own, other = slice(hd * HD, hd * HD + HD), slice(HD - hd * HD, P - hd * HD)
                        nc.scalar.copy(self.o_s[own, 0:n], o[own])
                        nc.scalar.copy(self.r_s[own, 0:n], o[other]).then_inc(self.left, 1)

            def copy_group(self, eng, it, g, copy):
                u, c0, c1 = self.groups[g]
                eng.wait_ge(self.turned, it * self.NG + (g + 1))
                eng.wait_ge(self.valued, it * self.NG + max(g - 1, 0))
                src = ps[:, (4 + g % 2) * CH:(4 + g % 2) * CH + CH]
                full = [c for c in range(c0, c1) if self.blocks[u // 2]["chunks"][c][1] == P]
                if len(full) < c1 - c0:
                    n = self.blocks[u // 2]["chunks"][c1 - 1][1]
                    k = (c1 - 1 - c0) * P
                    ins = copy(self.pt[0:n, g % 2, k:k + P], src[0:n, k:k + P])
                if full:
                    ins = copy(self.pt[:, g % 2, 0:len(full) * P], src[:, 0:len(full) * P])
                ins.then_inc(self.out_of[g % 2], 1)

            def dve(self, dve, it, start, masks):
                for step in self.steps:
                    if step[0] == "S":
                        u = step[1]
                        blk = self.blocks[u // 2]
                        dve.wait_ge(self.turned, it * self.NG + (self.last_group(u - 2) + 1 if u >= 2 else 0))
                        dve.wait_ge(self.scored, it * self.NA + (u + 1))
                        start(u, self.nm[:, u, 0:1])
                        segs = masks(u)
                        dve.drain()
                        for i, (p0, n, mask) in enumerate(segs):
                            if i:
                                dve.drain()
                            end = i == len(segs) - 1
                            ins = dve.tensor_tensor_reduce(
                                self.l[:, u % 2, p0:p0 + n],
                                ps[:, (u % 2) * 2 * CH + p0:(u % 2) * 2 * CH + p0 + n], mask, -1.0,
                                self.nm[:, u, 0:1], ALU.add, ALU.min,
                                self.nm[:, u, 1:2] if end else self.nm[:, u, 0:1])
                        ins.then_inc(self.shifted, 1)
                    elif step[0] == "T" and step[1] % 2 == 1:
                        self.copy_group(dve, it, step[1], dve.tensor_copy)
                    elif step[0] == "F":
                        hf = step[1]
                        n = len(self.halves[hf]) * P
                        t0 = self.blocks[self.halves[hf][0]]["b"] * P
                        dve.drain()
                        dve.wait_ge(self.left, it * (2 * self.NH) + (2 * hf + 2))
                        dve.reciprocal(self.r_s[:, 0:n], self.r_s[:, 0:n])
                        dve.tensor_tensor(self.o_s[:, 0:n], self.o_s[:, 0:n], self.silu[:, t0:t0 + n], ALU.mult)
                        dve.drain()
                        dve.tensor_tensor(self.y[:, t0:t0 + n], self.o_s[:, 0:n], self.r_s[:, 0:n],
                                          ALU.mult).then_inc(self.gated, 1)

            def finish_act(self, act, it, y_index, cols):
                act.wait_ge(self.gated, it * self.NH + self.NH)
                act.wait_ge(self.spilled, it * 32)
                nc.scalar.copy(self.y_hi[:], self.y[:]).then_inc(self.hi_done, 1)
                act.wait_ge(self.lo_done, it + 1)
                for part, src in ((0, self.y_hi), (1, self.y_lo)):
                    act.dma_start(y_dram[part, ds(y_index, 1), :, 0:cols].rearrange("a p t -> (a p) t"),
                                  src[:].bitcast(F32)).then_inc(self.spilled, 16)

            def finish_dve(self, dve, it):
                dve.wait_ge(self.hi_done, it + 1)
                dve.tensor_tensor(self.y_lo[:], self.y[:], self.y_hi[:].bitcast(F32),
                                  ALU.subtract).then_inc(self.lo_done, 1)

        def rows_of(hd):
            return slice(hd * HD, hd * HD + HD)

        ph3 = ctx.enter_context(ExitStack())
        fox_blocks = [{"b": b, "width": (b + 1) * P,
                       "runs": [(c, c, min(CH, (b + 1) * P - c)) for c in range(0, (b + 1) * P, CH)],
                       "chunks": [(c * P, P, c) for c in range(b + 1)]} for b in range(8)]
        fox = Attention("fox", fox_blocks, [[0, 1, 2, 3], [4, 5, 6, 7]], T, T, T, 8, ph3)
        fx_k2a = [sb(f"fx_k2a{i}", [P, T], F32R, ph3) for i in range(2)]
        fx_k2b = [sb(f"fx_k2b{i}", [P, T], F32R, ph3) for i in range(2)]
        fx_v = [sb(f"fx_v{i}", [P, 8, P], at=ph3) for i in range(2)]
        fx_vt = sb("fx_vt", [P, T], at=ph3)
        nf = sb("nf", [P, T], at=ph3)
        nf_t = sb("nf_t", [P, T], at=ph3)
        fb = sb("fb", [16, 1], at=ph3)
        nf_b = sb("nf_b", [P, 2, T], at=ph3)
        nf_tri = sb("nf_tri", [P, 2, P], at=ph3)
        cond = sb("cond", [P, 2, D], at=ph3)
        ada_w = sb("ada_w", [P, 3, D], at=ph3)
        ada_acc = sb("ada_acc", [P, 12], at=ph3)
        ph3.close()

        fb_loaded = sem("fb_loaded")
        fz_shift = sem("fz_shift")
        fz_act = sem("fz_act")
        fz_done = sem("fz_done")
        nf_stored = sem("nf_stored")
        nf_loaded = sem("nf_loaded")
        f_hi = sem("f_hi")
        f_lo = sem("f_lo")
        f_v = sem("f_v")
        f_g = sem("f_g")
        f_vt = sem("f_vt")
        f_vc = sem("f_vc")
        cond_set = sem("cond_set")
        ada_loaded = sem("ada_loaded")
        ada_done = sem("ada_done")
        area3 = sem("area3")
        nf_dram = nc.dram_tensor("nf_rows", [16, T], F32).ap()

        def fz_pe(pe):
            pe.wait_ge(h_yt, HG)
            pe.wait_ge(h_sc, 8 * HG)
            project(pe, U_FZ, 0, u_hi, u_lo, [(slice(c * CH, c * CH + CH), bank(c), []) for c in range(2)], h_chunk)
            pe.wait_ge(w_ready, U_FZ + 2)
            pe.drain().then_inc(w_used, 1)

        def fz_act_part(act):
            act.wait_ge(h_spill, 32 * HG)
            act.dma_start(fb[:], a["fox_fb"]).then_inc(fb_loaded, 16)
            for i in range(2):
                act.dma_start(cond[:, i, :], a["cond"][i:i + 1, :].broadcast_to([P, D])).then_inc(fb_loaded, 16)
            act.wait_ge(h_chunk, 4 * HG + 1)
            act.wait_ge(w_used, U_FZ + 1)
            act.wait_ge(fb_loaded, 48)
            r = slice(0, 16)
            nc.scalar.activation(nf_t[r], ps[r, 0:T], ACT.Identity, bias=fb[:, 0:1])
            nc.scalar.activation(nf[r], ps[r, 0:T], ACT.Abs, bias=fb[:, 0:1])
            act.drain()
            nc.scalar.activation(nf[r], nf[r], ACT.Exp, scale=-1.0)
            act.drain()
            nc.scalar.activation(nf[r], nf[r], ACT.Ln, bias=1.0).then_inc(fz_act, 1)
            nc.scalar.activation(cond[:].rearrange("p a b -> p (a b)"), cond[:].rearrange("p a b -> p (a b)"),
                                 ACT.Silu).then_inc(cond_set, 1)
            act.wait_ge(fz_done, 1)
            act.dma_start(nf_dram, nf[r]).then_inc(nf_stored, 16)
            act.wait_ge(nf_stored, 16)

        def fz_dve(dve):
            dve.wait_ge(h_spill, 32 * HG)
            for i in range(2):
                dve.memset(fx_v[i][:], 1.0)
            dve.memset(nf_b[0:16, 0, :], 1.0)
            dve.drain().then_inc(area3, 1)
            dve.wait_ge(fz_act, 1)
            r = slice(0, 16)
            dve.scalar_tensor_tensor(nf_t[r], nf_t[r], 0.0, nf[r], ALU.min, ALU.subtract)
            dve.drain()
            dve.tensor_tensor_scan(nf[r], nf_b[r, 0, :], nf_t[r], 0.0, ALU.mult, ALU.subtract)
            dve.drain().then_inc(fz_done, 1)

        def fox_pe(pe):
            with pe.Fori(0, PAIRS) as it:
                n = it * 4 + U_FOX

                def unit(j, b, waits):
                    project(pe, n + j, j % 2, u_hi, u_lo,
                            [(slice(c * CH, c * CH + CH), bank(b + c), waits if c == 0 else []) for c in range(2)],
                            fox.chunk)

                unit(0, 0, [(fox.shifted, it * fox.NA), (fz_act, 1)])
                unit(1, 2, [])
                unit(2, 4, [(fox.out_of[i], it * (fox.NG // 2)) for i in range(2)])
                unit(3, 0, [(f_lo, it * 2 + 1)])
                pe.wait_ge(f_v, it + 1)
                pe.wait_ge(fox.left, it * (2 * fox.NH))
                for j in range(8):
                    mm = pe.transpose(ps[:, 6 * CH + j * P:6 * CH + (j + 1) * P], fx_vt[:, j * P:(j + 1) * P], ident)
                mm.then_inc(f_vt, 1)
                fox.pe(pe, it, fx_k2a, fx_k2b, fx_v,
                       lambda u: [(f_lo, it * 2 + 2), (f_g, it + 1)] if u == 0 else [],
                       lambda g: [],
                       lambda hf: [(f_vc, it + 1)] if hf == 0 else [])

        def fox_act(act):
            act.wait_ge(area3, 1)
            with act.Fori(0, PAIRS) as it:
                act.wait_ge(fox.shifted, it * fox.NA)
                for hd in range(2):
                    act.dma_start(nf_b[:, hd, :], nf_dram[ds(it * 2 + hd, 1), :].broadcast_to([P, T])
                                  ).then_inc(nf_loaded, 16)

                def load_ada(half):
                    act.wait_ge(ada_done, it * 2 + half)
                    for j in range(3):
                        act.dma_start(ada_w[:, j, :], a["w_ada"][ds(it * 6 + (3 * half + j), 1)
                                                                 ].rearrange("a p n -> (a p) n")
                                      ).then_inc(ada_loaded, 16)

                load_ada(0)
                act.wait_ge(fox.chunk, it * 4 + 1)
                act.wait_ge(w_used, it * 4 + (U_FOX + 1))
                for hd in range(2):
                    ins = nc.scalar.activation(fox.q2[hd][0:HD, :], bank(0, 2)[rows_of(hd)], ACT.Copy, scale=HD ** -0.5)
                ins.then_inc(f_hi, 1)
                act.wait_ge(fox.chunk, it * 4 + 2)
                act.wait_ge(w_used, it * 4 + (U_FOX + 2))
                for hd in range(2):
                    for half in range(2):
                        ins = nc.scalar.copy(fx_k2a[hd][rows_of(half), :], bank(2, 2)[rows_of(hd)])
                ins.then_inc(f_hi, 1)
                load_ada(1)
                act.wait_ge(fox.chunk, it * 4 + 3)
                act.wait_ge(w_used, it * 4 + (U_FOX + 3))
                nc.scalar.copy(fx_vt[:], bank(4, 2)).then_inc(f_v, 1)
                act.wait_ge(fox.chunk, it * 4 + 4)
                act.wait_ge(w_used, it * 4 + (U_FOX + 4))
                nc.scalar.activation(fox.silu[:], bank(0, 2), ACT.Silu).then_inc(f_g, 1)
                act.wait_ge(f_vt, it + 1)
                vt = bank(6, 2).rearrange("p (j t) -> p j t", t=P)
                nc.scalar.copy(fx_v[0][:, :, 0:HD], vt[:, :, 0:HD])
                nc.scalar.copy(fx_v[1][:, :, HD:P], vt[:, :, HD:P]).then_inc(f_vc, 1)
                fox.act(act, it)
                fox.finish_act(act, it, it + 8, T)

        def fox_dve(dve):
            dve.wait_ge(cond_set, 1)
            with dve.Fori(0, PAIRS) as it:
                dve.wait_ge(fox.turned, it * fox.NG)

                def dot_ada(half):
                    for j in range(3):
                        for i in range(2):
                            k = 6 * half + 2 * j + i
                            dve.wait_ge(ada_loaded, it * 96 + 48 * (half + 1))
                            dve.memset(ada_acc[:, k:k + 1], 0.0)
                            dve.drain()
                            ins = dve.tensor_tensor_reduce(fox.l[:, i, :], ada_w[:, j, :], cond[:, i, :], 1.0,
                                                           ada_acc[:, k:k + 1], ALU.mult, ALU.add,
                                                           ada_acc[:, k:k + 1])
                    ins.then_inc(ada_done, 1)

                dot_ada(0)
                dve.wait_ge(f_hi, it * 2 + 1)
                for hd in range(2):
                    ins = dve.scalar_tensor_tensor(fox.q2[hd][HD:P, :], bank(0, 2)[rows_of(hd)], HD ** -0.5,
                                                   fox.q2[hd][0:HD, :].bitcast(F32), ALU.mult, ALU.subtract)
                ins.then_inc(f_lo, 1)
                dve.wait_ge(f_hi, it * 2 + 2)
                for hd in range(2):
                    for half in range(2):
                        ins = dve.tensor_tensor(fx_k2b[hd][rows_of(half), :], bank(2, 2)[rows_of(hd)],
                                                fx_k2a[hd][0:HD, :].bitcast(F32), ALU.subtract)
                ins.then_inc(f_lo, 1)
                dot_ada(1)
                dve.drain()
                dve.tensor_copy(ada[:].rearrange("p u i -> p (u i)")[:, ds(it * 12, 12)], ada_acc[:])
                dve.drain()
                dve.wait_ge(nf_loaded, it * 32 + 32)

                def masks(u):
                    b, hd = u // 2, u % 2
                    dve.tensor_tensor(nf_tri[:, hd, :], nf_b[:, hd, b * P:(b + 1) * P],
                                      consts[:, K_TRI:K_TRI + P], ALU.add)
                    return ([(0, b * P, nf_b[:, hd, 0:b * P])] if b else []) + [(b * P, P, nf_tri[:, hd, :])]

                fox.dve(dve, it, lambda u, nm: dve.memset(nm, 3e38), masks)
                fox.finish_dve(dve, it)

        block1.close()
        ph4 = ctx.enter_context(ExitStack())
        y_hi = sb("y_hi", [P, 16, T], F32R, ph4)
        y_lo = sb("y_lo", [P, 16, T], F32R, ph4)
        h_area = ctx.enter_context(ExitStack())
        h_sb = sb("h_sb", [P, KT, T], at=h_area)
        x_in = sb("x_in", [P, 2, T], at=h_area)
        ctx_in = sb("ctx_in", [P, KT, C], at=h_area)
        h_area.close()
        ph4.close()
        y4_loaded = sem("y4_loaded")
        x4_loaded = sem("x4_loaded")
        o_chunk = sem("o_chunk")
        o_added = sem("o_added")

        ph4b = ctx.enter_context(ExitStack())
        r_hi = sb("r_hi", [P, KT, T], F32R, ph4b)
        r_lo = sb("r_lo", [P, KT, T], F32R, ph4b)
        ple = sb("ple", [P, KT, T], at=ph4b)
        p_hi = sb("p_hi", [P, 2, T], F32R, ph4b)
        p_lo = sb("p_lo", [P, 2, T], F32R, ph4b)
        sig = sb("sig", [P, 2, T], at=ph4b)
        ph4b.close()
        p_loaded = sem("p_loaded")
        p_hi_set = sem("p_hi_set")
        p_lo_set = sem("p_lo_set")
        h_hi_set = sem("h_hi_set")
        h_lo_set = sem("h_lo_set")
        ple_chunk = sem("ple_chunk")
        ple_done = sem("ple_done")
        g_chunk = sem("g_chunk")
        g_sig = sem("g_sig")
        g_added = sem("g_added")

        def two_chunks(b, waits):
            return [(slice(c * CH, c * CH + CH), bank(b + c), waits if c == 0 else []) for c in range(2)]

        def out1_pe(pe):
            pe.wait_ge(y4_loaded, 16 * 32)
            with pe.Fori(0, KT // 2) as i:
                for m in range(2):
                    n = i * 4 + (U_OUT + 2 * m)
                    free = [(o_added, i * 2 + (m - 1))] if m else [(o_added, i * 2)]
                    project(pe, n, 0, y_hi, y_lo, two_chunks(2 * m, free), o_chunk, stop=False)
                    project(pe, n + 1, 1, y_hi, y_lo, two_chunks(2 * m, []), o_chunk, first=KT, start=False)

        def out1_act(act):
            act.wait_ge(fox.spilled, 32 * PAIRS)
            act.wait_ge(fox.valued, PAIRS * fox.NG)
            for k in range(2 * KT):
                for part, dst in ((0, y_hi), (1, y_lo)):
                    act.dma_start(dst[:, k, :].bitcast(F32), y_dram[part, k, :, 0:T]).then_inc(y4_loaded, 16)
            with act.Fori(0, KT // 2) as i:
                for m in range(2):
                    act.wait_ge(o_added, i * 2)
                    act.dma_start(x_in[:, m, :], a["x_t"][:, ds(i * 2 + m, 1), :].rearrange("p a t -> p (a t)")
                                  ).then_inc(x4_loaded, 16)

        def out1_dve(dve):
            with dve.Fori(0, KT // 2) as i:
                for m in range(2):
                    dve.wait_ge(x4_loaded, i * 32 + 32)
                    dve.wait_ge(o_chunk, i * 4 + (2 * m + 2))
                    dve.wait_ge(w_used, i * 4 + (U_OUT + 2 * m + 2))
                    dve.tensor_tensor(h_sb[:, ds(i * 2 + m, 1), :].rearrange("p a t -> p (a t)"),
                                      bank(2 * m, 2), x_in[:, m, :], ALU.add).then_inc(o_added, 1)

        def ple_pe(pe):
            pe.wait_ge(p_lo_set, 1)
            for half in range(2):
                for m in range(4):
                    j = 4 * half + m
                    free = [(ple_done, j - 1)] if j >= 2 else [(o_added, KT)]
                    project(pe, U_PLE + half, half, p_hi, p_lo, two_chunks(2 * (m % 2), free), ple_chunk,
                            tiles=(2 * m, 2 * m + 1), last=m == 3)

        def gate_pe(pe):
            pe.wait_ge(h_lo_set, KT)
            pe.wait_ge(ple_done, KT)
            with pe.Fori(0, KT // 2) as i:
                for m in range(2):
                    free = [(g_sig, i * 2 + (m - 1))] if m else [(g_sig, i * 2)]
                    project(pe, i * 2 + (U_GATE + m), m, r_hi, r_lo, two_chunks(2 * m, free), g_chunk)

        def ple_act(act):
            act.wait_ge(o_added, KT)
            act.dma_start(x_in[:], a["p_t"]).then_inc(p_loaded, 16)
            act.wait_ge(p_loaded, 16)
            nc.scalar.copy(p_hi[:], x_in[:]).then_inc(p_hi_set, 1)
            for k in range(KT):
                nc.scalar.copy(r_hi[:, k, :], h_sb[:, k, :]).then_inc(h_hi_set, 1)
            for m in range(KT):
                act.wait_ge(ple_chunk, 2 * (m + 1) - (m + 1) // 4)
                act.wait_ge(w_used, U_PLE + (m + 1) // 4)
                nc.scalar.copy(ple[:, m, :], bank(2 * (m % 2), 2)).then_inc(ple_done, 1)
            with act.Fori(0, KT // 2) as i:
                for m in range(2):
                    act.wait_ge(g_added, i * 2)
                    act.wait_ge(g_chunk, i * 2 + (m + 1))
                    act.wait_ge(w_used, i * 2 + (U_GATE + m + 1))
                    nc.scalar.activation(sig[:, m, :], bank(2 * m, 2), ACT.Sigmoid).then_inc(g_sig, 1)

        def ple_dve(dve):
            dve.wait_ge(p_hi_set, 1)
            dve.tensor_tensor(p_lo[:], x_in[:], p_hi[:].bitcast(F32), ALU.subtract).then_inc(p_lo_set, 1)
            for k in range(KT):
                dve.wait_ge(h_hi_set, k + 1)
                dve.tensor_tensor(r_lo[:, k, :], h_sb[:, k, :], r_hi[:, k, :].bitcast(F32),
                                  ALU.subtract).then_inc(h_lo_set, 1)
            dve.wait_ge(ple_done, KT)
            with dve.Fori(0, KT // 2) as i:
                for m in range(2):
                    dve.wait_ge(g_sig, i * 2 + (m + 1))
                    row = lambda t: t[:, ds(i * 2 + m, 1), :].rearrange("p a t -> p (a t)")
                    dve.tensor_tensor(sig[:, m, :], sig[:, m, :], row(ple), ALU.mult)
                    dve.drain()
                    dve.tensor_tensor(row(h_sb), row(h_sb), sig[:, m, :], ALU.add).then_inc(g_added, 1)

        ph4c = ctx.enter_context(ExitStack())
        sq4 = sb("sq4", [P, 2, T], at=ph4c)
        rstd4 = sb("rstd4", [P, T], at=ph4c)
        ph4c.close()
        n4_sq = sem("n4_sq")
        n4_sum = sem("n4_sum")
        n4_sd = sem("n4_sd")
        n4_h = sem("n4_h")
        h_stored = sem("h_stored")
        ctx_loaded = sem("ctx_loaded")

        def norm4_act(act):
            act.wait_ge(g_added, KT)
            act.dma_start(ctx_in[:], a["ctx_t"]).then_inc(ctx_loaded, 16)
            for k in range(KT):
                if k >= 2:
                    act.wait_ge(n4_sum, k - 1)
                nc.scalar.activation(sq4[:, k % 2, :], h_sb[:, k, :], ACT.Square).then_inc(n4_sq, 1)
            act.wait_ge(n4_sum, KT)
            nc.scalar.activation(rstd4[:], bank(0, 2), ACT.Sqrt, bias=small[:, 1:2]).then_inc(n4_sd, 1)
            for k in range(KT):
                act.wait_ge(n4_h, k + 1)
                act.dma_start(h_dram[k, :, 0:T], h_sb[:, k, :]).then_inc(h_stored, 16)
            act.wait_ge(ctx_loaded, 16)
            act.dma_start(h_dram[:, :, T:TC].rearrange("k p t -> p k t"), ctx_in[:]).then_inc(h_stored, 16)

        def norm4_pe(pe):
            for k in range(KT):
                pe.wait_ge(n4_sq, k + 1)
                for c in range(2):
                    mm = pe.matmul(bank(c), ones_mean[:], sq4[:, k % 2, c * CH:(c + 1) * CH],
                                   start=k == 0, stop=k == KT - 1)
                mm.then_inc(n4_sum, 1)

        def norm4_dve(dve):
            dve.wait_ge(n4_sd, 1)
            dve.reciprocal(rstd4[:], rstd4[:])
            dve.drain()
            for k in range(KT):
                dve.scalar_tensor_tensor(h_sb[:, k, :], h_sb[:, k, :], vecs[:, V_FINAL + k:V_FINAL + k + 1],
                                         rstd4[:], ALU.mult, ALU.mult).then_inc(n4_h, 1)

        ada_set = sem("ada_set")

        def ada_dve(dve):
            dve.tensor_tensor(adv[:], ada[:], vecs[:, V_BADA:V_BADA + ADA_UNITS].unsqueeze(2)
                              .broadcast_to([P, ADA_UNITS, 2]), ALU.add)
            dve.drain()
            for l in range(2):
                sc = adv[:, 24 * l + 8:24 * l + 16, :]
                dve.tensor_scalar(sc, sc, 1.0, None, ALU.add)
            dve.drain().then_inc(ada_set, 1)

        class Layer:

            def __init__(self, l, name, n_out, cols, first=None):
                self.l, self.name, self.n_out, self.cols = l, name, n_out, cols
                self.chunks = [(0, CH), (CH, CH), (T, C)][:3 if cols == TC else 2]
                area = ctx.enter_context(ExitStack())
                self.yh = sb(f"{name}_out_yh", [P, KT, cols], F32R, area)
                self.yl = sb(f"{name}_out_yl", [P, KT, cols], F32R, area)
                self.h = sb(f"{name}_h", [P, KT, cols], at=area)
                self.res = sb(f"{name}_res", [P, 2, cols], at=area)
                self.gate = sb(f"{name}_gate", [P, 2, 2], at=area)
                self.tmp = sb(f"{name}_tmp", [P, 2, cols], at=area)
                area.close()
                area = ctx.enter_context(ExitStack())
                self.sq = sb(f"{name}_sq", [P, 2, cols], at=area)
                self.mean = sb(f"{name}_mean", [P, cols], at=area)
                self.rstd = sb(f"{name}_rstd", [P, cols], at=area)
                assert 4 * 4 * cols <= 2 * 4 * KT * cols
                area.close()
                self.base = l * KT
                if first is None:
                    self.y_loaded = sem("layer_y_loaded")
                    self.res_loaded = sem("layer_res_loaded")
                    self.chunk = sem("layer_chunk")
                    self.gated = sem("layer_gated")
                    self.added = sem("layer_added")
                    self.mean_sum = sem("layer_mean_sum")
                    self.centred = sem("layer_centred")
                    self.sq_set = sem("layer_sq_set")
                    self.sq_sum = sem("layer_sq_sum")
                    self.sd = sem("layer_sd")
                    self.normed = sem("layer_normed")
                else:
                    self.y_loaded = first.y_loaded
                    self.res_loaded = first.res_loaded
                    self.chunk = first.chunk
                    self.gated = first.gated
                    self.added = first.added
                    self.mean_sum = first.mean_sum
                    self.centred = first.centred
                    self.sq_set = first.sq_set
                    self.sq_sum = first.sq_sum
                    self.sd = first.sd
                    self.normed = first.normed

            def span(self, b, waits=()):
                return [(slice(t, t + n), ps[:, b * CH + t:b * CH + t + n], waits if t == 0 else [])
                        for t, n in self.chunks]

            def flat(self, b):
                return ps[:, b * CH:b * CH + self.cols]

            def pe(self, pe, mixer):
                pe.wait_ge(self.y_loaded, 16 * 2 * (self.base + KT))
                n = len(self.chunks)
                with pe.Fori(0, KT // 2) as i:
                    for m in range(2):
                        project(pe, i * 2 + (self.n_out + m), m, self.yh, self.yl,
                                self.span(3 * m, [(self.gated, i * 2 + (self.base + max(m - 1, 0)))]), self.chunk)
                for k in range(KT):
                    if k == 0:
                        pe.wait_ge(self.added, self.base + KT)
                    for t, w in self.chunks:
                        mm = pe.matmul(ps[:, t:t + w], ones_mean[:], self.h[:, k, t:t + w],
                                       start=k == 0, stop=k == KT - 1)
                mm.then_inc(self.mean_sum, 1)
                for k in range(KT):
                    pe.wait_ge(self.sq_set, self.base + k + 1)
                    for t, w in self.chunks:
                        mm = pe.matmul(ps[:, 3 * CH + t:3 * CH + t + w], ones_mean[:], self.sq[:, k % 2, t:t + w],
                                       start=k == 0, stop=k == KT - 1)
                    mm.then_inc(self.sq_sum, 1)

            def act(self, act, mixer):
                act.wait_ge(mixer.spilled, 32 * PAIRS)
                act.wait_ge(mixer.valued, PAIRS * mixer.NG)
                for k in range(KT):
                    for part, dst in ((0, self.yh), (1, self.yl)):
                        act.dma_start(dst[:, k, :].bitcast(F32), y_dram[part, k, :, 0:self.cols]
                                      ).then_inc(self.y_loaded, 16)
                with act.Fori(0, KT // 2) as i:
                    for m in range(2):
                        act.wait_ge(self.added, i * 2 + self.base)
                        act.dma_start(self.res[:, m, :], h_dram[ds(i * 2 + m, 1), :, 0:self.cols]
                                      .rearrange("a p t -> (a p) t")).then_inc(self.res_loaded, 16)
                for k in range(KT):
                    act.wait_ge(self.centred, self.base + k + 1)
                    if k >= 2:
                        act.wait_ge(self.sq_sum, self.base + k - 1)
                    nc.scalar.activation(self.sq[:, k % 2, :], self.h[:, k, :], ACT.Square).then_inc(self.sq_set, 1)
                act.wait_ge(self.sq_sum, self.base + KT)
                nc.scalar.activation(self.rstd[:], self.flat(3), ACT.Sqrt, bias=small[:, 2:3]).then_inc(self.sd, 1)

            def dve(self, dve):
                l = self.l
                with dve.Fori(0, KT // 2) as i:
                    for m in range(2):
                        dve.tensor_copy(self.gate[:, m, :],
                                        adv[:, ds(i * 2 + (24 * l + 16 + m), 1), :].rearrange("p a i -> p (a i)"))
                        dve.drain()
                        dve.wait_ge(self.chunk, (i * 2 + (m + 1)) * (len(self.chunks) - 1) + 2 * self.base)
                        dve.wait_ge(w_used, i * 2 + (self.n_out + m + 1))
                        ins = dve.tensor_scalar(self.tmp[:, m, 0:T], ps[:, 3 * m * CH:3 * m * CH + T],
                                                self.gate[:, m, 0:1], None, ALU.mult)
                        if self.cols > T:
                            ins = dve.tensor_scalar(self.tmp[:, m, T:], ps[:, 3 * m * CH + T:3 * m * CH + TC],
                                                    self.gate[:, m, 1:2], None, ALU.mult)
                        ins.then_inc(self.gated, 1)
                        dve.drain()
                        dve.wait_ge(self.res_loaded, i * 32 + (16 * self.base + 32))
                        dve.scalar_tensor_tensor(self.h[:, ds(i * 2 + m, 1), :].rearrange("p a t -> p (a t)"),
                                                 self.res[:, m, :], ALPHA, self.tmp[:, m, :], ALU.mult, ALU.add
                                                 ).then_inc(self.added, 1)
                dve.wait_ge(self.mean_sum, l + 1)
                dve.tensor_copy(self.mean[:], self.flat(0))
                dve.drain()
                for k in range(KT):
                    dve.tensor_tensor(self.h[:, k, :], self.h[:, k, :], self.mean[:], ALU.subtract
                                      ).then_inc(self.centred, 1)
                dve.wait_ge(self.sd, l + 1)
                dve.reciprocal(self.rstd[:], self.rstd[:])
                dve.drain()
                for k in range(KT):
                    g = vecs[:, V_LNG + 8 * l + k:V_LNG + 8 * l + k + 1]
                    b = vecs[:, V_LNB + 8 * l + k:V_LNB + 8 * l + k + 1]
                    dve.scalar_tensor_tensor(self.h[:, k, :], self.h[:, k, :], g, self.rstd[:], ALU.mult, ALU.mult)
                    dve.drain()
                    dve.tensor_scalar(self.h[:, k, :], self.h[:, k, :], b, None, ALU.add).then_inc(self.normed, 1)

        class Modulated:

            def __init__(self, l, name, h_of, first=None):
                self.l, self.h_of = l, h_of
                self.area = ctx.enter_context(ExitStack())
                self.hi = sb(f"{name}_u_hi", [P, KT, TC], F32R, self.area)
                self.lo = sb(f"{name}_u_lo", [P, KT, TC], F32R, self.area)
                self.base = l * KT
                if first is None:
                    self.made = sem("u_made")
                    self.hi_set = sem("u_hi_set")
                    self.lo_set = sem("u_lo_set")
                else:
                    self.made, self.hi_set, self.lo_set = first.made, first.hi_set, first.lo_set

            def act(self, act):
                for k in range(KT):
                    act.wait_ge(self.made, self.base + k + 1)
                    nc.scalar.copy(self.hi[:, k, :], self.u[:, k % 2, :]).then_inc(self.hi_set, 1)

            def dve(self, dve):
                def low(k):
                    dve.wait_ge(self.hi_set, self.base + k + 1)
                    dve.tensor_tensor(self.lo[:, k, :], self.u[:, k % 2, :], self.hi[:, k, :].bitcast(F32),
                                      ALU.subtract).then_inc(self.lo_set, 1)
                for k in range(KT):
                    if k >= 2:
                        dve.drain()
                    for i, (t, n) in enumerate(((0, T), (T, C))):
                        ins = dve.tensor_scalar(self.u[:, k % 2, t:t + n], self.h_of(k, i),
                                                adv[:, 24 * self.l + 8 + k, i:i + 1], adv[:, 24 * self.l + k, i:i + 1],
                                                ALU.mult, ALU.add)
                    ins.then_inc(self.made, 1)
                    if k:
                        low(k - 1)
                low(KT - 1)

        mod_a = Modulated(0, "wa", lambda k, i: ctx_in[:, k, :] if i else h_sb[:, k, :])
        with ExitStack() as above:
            mod_a.u = sb("wa_u", [P, 2, TC], at=above)

        def window_block(b):
            if b >= 8:
                lo, hi = 0, 0
            else:
                lo, hi = max(b - 1, 0), min(b + 2, 8)
            n = (hi - lo) * P
            runs = [(0, lo * P, n)] if n else []
            for p0 in range(n, n + C, P if n % CH == 3 * P else C):
                runs.append((p0, T + p0 - n, P if n % CH == 3 * P else C))
            chunks = [(c * P, P, lo + c) for c in range(hi - lo)]
            chunks += [(n + c * P, P, 8 + c) for c in range(2)] + [(n + C, 1, 10)]
            return {"b": b, "width": n + C + 1, "runs": runs, "chunks": chunks, "lat": n}

        ph6 = ctx.enter_context(ExitStack())
        wa = Attention("wa", [window_block(b) for b in range(10)], [[0, 1, 2, 3], [4, 5, 6, 7], [8, 9]],
                       3 * P + C + 1, TC, TC, 11, ph6)
        wa_k2a = [sb(f"wa_k2a{i}", [P, TC], F32R, ph6) for i in range(2)]
        wa_k2b = [sb(f"wa_k2b{i}", [P, TC], F32R, ph6) for i in range(2)]
        wa_v = [[sb(f"wa_v{i}{o}", [P, 11, P], at=ph6) for o in range(2)] for i in range(2)]
        rope = sb("rope", [P, 2, T], at=ph6)
        nsink = sb("nsink", [P, 16], at=ph6)
        head_sink = sb("head_sink", [P, 2], at=ph6)
        ph6.close()
        wa_shuf = wa.l[:].rearrange("p s w -> p (s w)")[:, 0:T]
        a_loaded = sem("a_loaded")
        a_set = sem("a_set")
        a_copied = sem("a_copied")
        a_turned = sem("a_turned")
        a_hi = sem("a_hi")
        a_lo = sem("a_lo")
        a_vt = sem("a_vt")
        a_vc = sem("a_vc")
        a_g = sem("a_g")

        def wa_pe(pe):
            pe.wait_ge(mod_a.lo_set, KT)
            with pe.Fori(0, 2) as j:
                def unit(i, b, waits):
                    project(pe, j * 10 + (U_A + i), i % 2, mod_a.hi, mod_a.lo,
                            layer_a.span(b, waits), wa.chunk)

                unit(0, 0, [(wa.shifted, j * (4 * wa.NA))])
                unit(1, 3, [(wa.out_of[i], j * (4 * wa.NG // 2)) for i in range(2)])
                pe.wait_ge(a_copied, j * 6 + 2)
                for t in range(10):
                    mm = pe.transpose(ps[:, t * P:(t + 1) * P], wa.y[:, t * P:(t + 1) * P], ident)
                mm.then_inc(a_vt, 1)
                for g in range(4):
                    it = j * 4 + g
                    unit(2 + 2 * g, 0, [(wa.shifted, it * wa.NA), (a_vc, j + 1)])
                    unit(3 + 2 * g, 3, [(wa.out_of[i], it * (wa.NG // 2)) for i in range(2)])
                    wa.pe(pe, it, [wa_k2a[g // 2]] * 2, [wa_k2b[g // 2]] * 2, wa_v[g // 2],
                          lambda u: [(a_lo, j * 5 + (g + 2)), (a_g, it + 1)] if u == 0 else [],
                          lambda g: [],
                          lambda hf: [])

        def wa_act(act):
            act.wait_ge(mod_a.lo_set, KT)
            act.wait_ge(h_stored, 16 * (KT + 1))
            act.dma_start(rope[:], a["rope"]).then_inc(a_loaded, 16)
            act.dma_start(nsink[:], a["a_sink"].broadcast_to([P, 16])).then_inc(a_loaded, 16)
            with act.Fori(0, 2) as j:
                def copied(i, b, scale=1.0):
                    act.wait_ge(wa.chunk, j * 20 + 2 * (i + 1))
                    act.wait_ge(w_used, j * 10 + (U_A + i + 1))
                    return nc.scalar.activation(wa.y[:], layer_a.flat(b), ACT.Copy, scale=scale
                                                ).then_inc(a_copied, 1)

                copied(0, 0)
                act.wait_ge(a_turned, j * 5 + 1)
                for kk in range(2):
                    for half in range(2):
                        ins = nc.scalar.copy(wa_k2a[kk][rows_of(half), :], wa.y[rows_of(kk), :])
                ins.then_inc(a_hi, 1)
                act.wait_ge(a_lo, j * 5 + 1)
                copied(1, 3)
                act.wait_ge(a_vt, j + 1)
                vt = ps[:, 0:TC].rearrange("p (j t) -> p j t", t=P)
                for kk in range(2):
                    for o in range(2):
                        ins = nc.scalar.copy(wa_v[kk][o][:, 0:10, rows_of(o)], vt[:, :, rows_of(kk)])
                ins.then_inc(a_vc, 1)
                for g in range(4):
                    it = j * 4 + g
                    copied(2 + 2 * g, 0, HD ** -0.5)
                    act.wait_ge(a_turned, j * 5 + (g + 2))
                    for hd in range(2):
                        ins = nc.scalar.copy(wa.q2[hd][rows_of(hd), :], wa.y[rows_of(hd), :])
                    ins.then_inc(a_hi, 1)
                    act.wait_ge(wa.chunk, j * 20 + 2 * (4 + 2 * g))
                    act.wait_ge(w_used, j * 10 + (U_A + 4 + 2 * g))
                    nc.scalar.activation(wa.silu[:], layer_a.flat(3), ACT.Silu).then_inc(a_g, 1)
                    wa.act(act, it)
                    wa.finish_act(act, it, it, TC)

        def wa_dve(dve):
            dve.wait_ge(h_stored, 16 * (KT + 1))
            dve.wait_ge(a_loaded, 32)
            for kk in range(2):
                for o in range(2):
                    v = wa_v[kk][o]
                    dve.memset(v[:, 0:10, :], 1.0)
                    dve.memset(v[0:1, 10, rows_of(o)], 0.0)
                    dve.memset(v[0:1, 10, rows_of(1 - o)], 1.0)
            dve.tensor_scalar(nsink[:], nsink[:], -1.0, None, ALU.mult)
            dve.drain().then_inc(a_set, 1)
            with dve.Fori(0, 2) as j:
                def rotate(i, n, it):
                    dve.drain()
                    dve.wait_ge(wa.turned, it * wa.NG)
                    dve.wait_ge(a_copied, j * 6 + i)
                    dve.tensor_copy(head_sink[:], nsink[:, ds(n, 2)])
                    dve.stream_shuffle(wa_shuf, wa.y[:, 0:T], [(x + 16) % 32 for x in range(32)])
                    dve.drain()
                    dve.tensor_tensor(wa.y[:, 0:T], wa.y[:, 0:T], rope[:, 0, :], ALU.mult)
                    dve.tensor_tensor(wa_shuf, wa_shuf, rope[:, 1, :], ALU.mult)
                    dve.drain()
                    dve.tensor_tensor(wa.y[:, 0:T], wa.y[:, 0:T], wa_shuf, ALU.add).then_inc(a_turned, 1)

                rotate(1, j * 8, j * 4)
                dve.wait_ge(a_hi, j * 5 + 1)
                for kk in range(2):
                    r = rows_of(kk)
                    for half in range(2):
                        ins = dve.tensor_tensor(wa_k2b[kk][rows_of(half), :], wa.y[r, :],
                                                wa_k2a[kk][r, :].bitcast(F32), ALU.subtract)
                ins.then_inc(a_lo, 1)
                for g in range(4):
                    it = j * 4 + g
                    rotate(3 + g, it * 2, it)
                    dve.wait_ge(a_hi, j * 5 + (g + 2))
                    for hd in range(2):
                        r = rows_of(hd)
                        ins = dve.tensor_tensor(wa.q2[hd][rows_of(1 - hd), :], wa.y[r, :],
                                                wa.q2[hd][r, :].bitcast(F32), ALU.subtract)
                    ins.then_inc(a_lo, 1)
                    dve.drain()

                    def masks(u):
                        blk = wa.blocks[u // 2]
                        b, n, w = blk["b"], blk["lat"], blk["width"]
                        dve.tensor_copy(wa.l[:, u % 2, w - 1:w], head_sink[:, u % 2:u % 2 + 1])
                        win = consts[:, K_WIN:K_WIN + 3 * P + C]
                        if b == 7:
                            return [(0, n, win[:, 0:n]), (n, C, win[:, 3 * P:])]
                        return [(0, n + C, win[:, 3 * P - n:])]

                    wa.dve(dve, it, lambda u, nm: dve.tensor_copy(nm, head_sink[:, u % 2:u % 2 + 1]), masks)
                    wa.finish_dve(dve, it)

        mod_a.area.close()
        layer_a = Layer(0, "la", U_A_OUT, TC)
        mod_b = Modulated(1, "nb", lambda k, i: layer_a.h[:, k, T:TC] if i else layer_a.h[:, k, 0:T], mod_a)
        with ExitStack() as above:
            sb("layer_a_h_place", [P, KT, TC], at=above)
            mod_b.u = sb("nb_u", [P, 2, TC], at=above)

        def near_block(b):
            rs = min(max(2 * b - 4, 0), 8)
            n = (9 if 2 <= b <= 5 else 8) * GRID_W
            chunks = [(c * P, P, 8 + c) for c in range(2)]
            chunks += [(C + c * P, min(P, n - c * P), rs // 2 + c) for c in range((n + P - 1) // P)]
            return {"b": b, "width": C + n, "chunks": chunks, "first_row": rs - 2 * b,
                    "runs": [(0, T, C), (C, rs * GRID_W, CH - C), (CH, rs * GRID_W + CH - C, n + C - CH)]}

        ph7 = ctx.enter_context(ExitStack())
        nb = Attention("nb", [near_block(b) for b in range(8)], [[0, 1, 2, 3], [4, 5, 6, 7]],
                       C + 9 * GRID_W, T, T, 10, ph7)
        nb_k2a = [sb(f"nb_k2a{i}", [P, TC], F32R, ph7) for i in range(2)]
        nb_k2b = [sb(f"nb_k2b{i}", [P, TC], F32R, ph7) for i in range(2)]
        nb_v = [sb(f"nb_v{i}", [P, 10, P], at=ph7) for i in range(2)]
        nb_bias = sb("nb_bias", [P, 2, 14 * GRID_W], at=ph7)
        nb_mid = sb("nb_mid", [P, 2, C + 9 * GRID_W], at=ph7)
        ph7.close()
        mod_b.area.close()
        nb_vt = nb.l[:].rearrange("p s w -> p (s w)")[:, 0:TC]
        b_loaded = sem("b_loaded")
        b_set = sem("b_set")
        b_hi = sem("b_hi")
        b_lo = sem("b_lo")
        b_v = sem("b_v")
        b_vt = sem("b_vt")
        b_vc = sem("b_vc")
        b_g = sem("b_g")
        layer_b = Layer(1, "lb", U_B_OUT, T, layer_a)

        def nb_pe(pe):
            pe.wait_ge(mod_b.lo_set, 2 * KT)
            with pe.Fori(0, PAIRS) as it:
                n = it * 4 + U_B
                project(pe, n, 0, mod_b.hi, mod_b.lo, two_chunks(0, [(nb.shifted, it * nb.NA)]), nb.chunk)
                project(pe, n + 1, 1, mod_b.hi, mod_b.lo,
                        layer_a.span(3, [(nb.out_of[i], it * (nb.NG // 2)) for i in range(2)]), nb.chunk)
                project(pe, n + 2, 0, mod_b.hi, mod_b.lo, layer_a.span(0, [(b_lo, it * 2 + 1)]), nb.chunk)
                project(pe, n + 3, 1, mod_b.hi, mod_b.lo, two_chunks(3, [(b_lo, it * 2 + 2)]), nb.chunk)
                pe.wait_ge(b_v, it + 1)
                for t in range(10):
                    mm = pe.transpose(ps[:, t * P:(t + 1) * P], nb_vt[:, t * P:(t + 1) * P], ident)
                mm.then_inc(b_vt, 1)
                nb.pe(pe, it, nb_k2a, nb_k2b, nb_v,
                      lambda u: [(b_vc, it + 1), (b_g, it + 1)] if u == 0 else [],
                      lambda g: [],
                      lambda hf: [])

        def nb_act(act):
            act.wait_ge(mod_b.lo_set, 2 * KT)
            act.wait_ge(b_stored, 16 * KT)
            with act.Fori(0, PAIRS) as it:
                act.wait_ge(nb.shifted, it * nb.NA)
                for hd in range(2):
                    act.dma_start(nb_bias[:, hd, :], a["rel_bias"][ds(it * 2 + hd, 1)].rearrange("a p n -> (a p) n")
                                  ).then_inc(b_loaded, 16)
                act.wait_ge(nb.chunk, it * 6 + 1)
                act.wait_ge(w_used, it * 4 + (U_B + 1))
                for hd in range(2):
                    ins = nc.scalar.activation(nb.q2[hd][0:HD, :], bank(0, 2)[rows_of(hd)], ACT.Copy, scale=HD ** -0.5)
                ins.then_inc(b_hi, 1)
                act.wait_ge(nb.chunk, it * 6 + 3)
                act.wait_ge(w_used, it * 4 + (U_B + 2))
                for hd in range(2):
                    for half in range(2):
                        ins = nc.scalar.copy(nb_k2a[hd][rows_of(half), :], layer_a.flat(3)[rows_of(hd)])
                ins.then_inc(b_hi, 1)
                act.wait_ge(nb.chunk, it * 6 + 5)
                act.wait_ge(w_used, it * 4 + (U_B + 3))
                nc.scalar.copy(nb_vt, layer_a.flat(0)).then_inc(b_v, 1)
                act.wait_ge(nb.chunk, it * 6 + 6)
                act.wait_ge(w_used, it * 4 + (U_B + 4))
                nc.scalar.activation(nb.silu[:], bank(3, 2), ACT.Silu).then_inc(b_g, 1)
                act.wait_ge(b_vt, it + 1)
                vt = ps[:, 0:TC].rearrange("p (j t) -> p j t", t=P)
                act.wait_ge(b_set, 1)
                nc.scalar.copy(nb_v[0][:, :, 0:HD], vt[:, :, 0:HD])
                nc.scalar.copy(nb_v[1][:, :, HD:P], vt[:, :, HD:P]).then_inc(b_vc, 1)
                nb.act(act, it)
                nb.finish_act(act, it, it, T)

        def nb_dve(dve):
            dve.wait_ge(b_stored, 16 * KT)
            for hd in range(2):
                dve.memset(nb_v[hd][:], 1.0)
                dve.memset(nb_mid[:, hd, 0:C], 0.0)
            dve.drain().then_inc(b_set, 1)
            with dve.Fori(0, PAIRS) as it:
                dve.wait_ge(b_loaded, it * 32 + 32)
                for hd in range(2):
                    rows = nb_bias[:, hd, :].rearrange("p (r c) -> p r c", c=GRID_W)
                    dve.tensor_tensor(rows, rows, consts[:, K_COL:K_COL + GRID_W].unsqueeze(1)
                                      .broadcast_to([P, 14, GRID_W]), ALU.add)
                dve.drain()
                for hd in range(2):
                    rows = nb_bias[:, hd, :].rearrange("p (r c) -> p r c", c=GRID_W)[:, 2:11, :]
                    dve.tensor_tensor(nb_mid[:, hd, C:].rearrange("p (r c) -> p r c", c=GRID_W), rows,
                                      consts[:, K_ROW:K_ROW + 9].unsqueeze(2).broadcast_to([P, 9, GRID_W]), ALU.add)
                dve.wait_ge(b_hi, it * 2 + 1)
                for hd in range(2):
                    ins = dve.scalar_tensor_tensor(nb.q2[hd][HD:P, :], bank(0, 2)[rows_of(hd)], HD ** -0.5,
                                                   nb.q2[hd][0:HD, :].bitcast(F32), ALU.mult, ALU.subtract)
                ins.then_inc(b_lo, 1)
                dve.wait_ge(b_hi, it * 2 + 2)
                for hd in range(2):
                    for half in range(2):
                        ins = dve.tensor_tensor(nb_k2b[hd][rows_of(half), :], layer_a.flat(3)[rows_of(hd)],
                                                nb_k2a[hd][0:HD, :].bitcast(F32), ALU.subtract)
                ins.then_inc(b_lo, 1)
                dve.drain()
                dve.wait_ge(b_vt, it + 1)

                def masks(u):
                    blk, hd = nb.blocks[u // 2], u % 2
                    if 2 <= blk["b"] <= 5:
                        return [(0, blk["width"], nb_mid[:, hd, :])]
                    c0 = (blk["first_row"] + 6) * GRID_W
                    return [(0, C, nb_mid[:, hd, 0:C]), (C, CH, nb_bias[:, hd, c0:c0 + CH])]

                nb.dve(dve, it, lambda u, nm: dve.memset(nm, 3e38), masks)
                nb.finish_dve(dve, it)

        b_stored = sem("b_stored")
        out_stored = sem("out_stored")

        def store_a(act):
            for k in range(KT):
                act.wait_ge(layer_a.normed, k + 1)
                act.dma_start(h_dram[k, :, 0:T], layer_a.h[:, k, 0:T]).then_inc(b_stored, 16)

        def store_b(act):
            for k in range(KT):
                act.wait_ge(layer_b.normed, KT + k + 1)
                act.dma_start(a["out"][k], layer_b.h[:, k, :]).then_inc(out_stored, 16)
            act.wait_ge(out_stored, 16 * KT)

        block = ctx.enter_context(nc.Block())

        @block.sync
        def _(sp):
            stream_loads(sp)
            sp.dma_start(vecs[:], a["vecs"]).then_inc(loaded, 16)
            sp.dma_start(consts[:], a["consts"]).then_inc(loaded, 16)
            for k in range(KT):
                sp.dma_start(x_sb[:, k, :], a["x_t"][:, k, :]).then_inc(x_loaded, 16)
            stream_loads_rest(sp)

        @block.gpsimd
        def _(pool):
            stream_splits(pool)

        @block.scalar
        def _(act):
            norm1_act(act)
            hgrn_act(act)
            fz_act_part(act)
            fox_act(act)
            out1_act(act)
            ple_act(act)
            norm4_act(act)
            mod_a.act(act)
            wa_act(act)
            layer_a.act(act, wa)
            store_a(act)
            mod_b.act(act)
            nb_act(act)
            layer_b.act(act, nb)
            store_b(act)

        @block.tensor
        def _(pe):
            norm1_pe(pe)
            hgrn_pe(pe)
            fz_pe(pe)
            fox_pe(pe)
            out1_pe(pe)
            ple_pe(pe)
            gate_pe(pe)
            norm4_pe(pe)
            wa_pe(pe)
            layer_a.pe(pe, wa)
            nb_pe(pe)
            layer_b.pe(pe, nb)

        @block.vector
        def _(dve):
            norm1_dve(dve)
            hgrn_dve(dve)
            fz_dve(dve)
            fox_dve(dve)
            out1_dve(dve)
            ple_dve(dve)
            ada_dve(dve)
            norm4_dve(dve)
            dve.drain()
            dve.wait_ge(ctx_loaded, 16)
            mod_a.dve(dve)
            wa_dve(dve)
            layer_a.dve(dve)
            dve.drain()
            mod_b.dve(dve)
            nb_dve(dve)
            layer_b.dve(dve)


def _tiles(v):
    return v.reshape(-1, P).T


def _unit(w, c0, width=P):
    cols = w[:, c0:c0 + width]
    if cols.shape[1] < width:
        cols = np.concatenate([cols, np.zeros((w.shape[0], width - cols.shape[1]), w.dtype)], 1)
    return cols.reshape(-1, P, width).transpose(1, 0, 2).reshape(P, -1)


def lay_out(x, p, norm_w, w_in, fox_fb, hgrn_gn, hgrn_lb_logits, w_out, w_ple, w_ple_gate, final_norm_w,
            c_2, ctx_2, c_ctx_2, w_ada_2, b_ada_2, ln_g_2, ln_b_2, a_w_in_2, a_w_out_2, a_sink_2,
            b_w_in_2, b_w_out_2, b_rel_bias_2):
    w1, wo, wp, wg = w_in[0], w_out[0], w_ple[0], w_ple_gate[0]
    wa, wao, wb, wbo = a_w_in_2[0], a_w_out_2[0], b_w_in_2[0], b_w_out_2[0]
    units = []
    for h in range(HG):
        units += [_unit(w1, j * D + h * P) for j in (1, 0, 2, 3)]
    units += [_unit(w1, 8 * D)] * 2
    for h in range(PAIRS):
        units += [_unit(w1, (4 + j) * D + h * P) for j in range(4)]
    for m in range(KT):
        units += [_unit(wo[:D], m * P), _unit(wo[D:], m * P)]
    for half in range(2):
        units.append(np.concatenate([_unit(wp, (4 * half + m) * P) for m in range(4)], 1))
    units += [_unit(wg, m * P) for m in range(KT)]
    for j in range(2):
        units += [_unit(wa, D + j * P), _unit(wa, D + 256 + j * P)]
        for g in range(4):
            units += [_unit(wa, (4 * j + g) * P), _unit(wa, D + 512 + (4 * j + g) * P)]
    units += [_unit(wao, m * P) for m in range(KT)]
    for h in range(PAIRS):
        units += [_unit(wb, j * D + h * P) for j in range(4)]
    units += [_unit(wbo, m * P) for m in range(KT)]
    assert len(units) == UNITS

    s = np.arange(P)
    level = np.zeros((P, 8, P), np.float32)
    for lv in range(LEVELS):
        H = 1 << lv
        level[:, lv] = ((s[:, None] // (2 * H) == s[None] // (2 * H))
                        & (s[:, None] % (2 * H) < H) & (s[None] % (2 * H) >= H))
    level[:, 7] = np.eye(P)
    consts = np.zeros((P, K_END), np.float32)
    consts[:, K_ID:K_ID + P] = np.eye(P)
    masks = np.zeros((P, 2, T), np.float32)
    masks[:, 0] = level.reshape(P, -1)
    masks[:, 1] = (np.arange(T) % HGRN_CHUNK != 0)
    consts[:, K_TRI:K_TRI + P] = np.where(s[None] > s[:, None], BIG, 0.0)

    win = consts[:, K_WIN:K_WIN + 640]
    win[:, 0:P] = np.where(s[None] < s[:, None], BIG, 0.0)
    win[:, 2 * P:3 * P] = np.where(s[None] > s[:, None], BIG, 0.0)
    qc, kc, second = s % GRID_W, np.arange(GRID_W), s // GRID_W
    first = np.clip(qc - 8, 0, GRID_W - 16)
    consts[:, K_COL:K_COL + GRID_W] = np.where((kc[None] >= first[:, None]) & (kc[None] < first[:, None] + 16), 0.0, BIG)
    consts[:, K_ROW + 8] = np.where(second == 0, BIG, 0.0)
    consts[:, K_ROW] = np.where(second == 1, BIG, 0.0)
    rows = np.arange(-6, 8)[None, :, None] - second[:, None, None] + 7
    rel_bias = b_rel_bias_2[0][:, rows, np.clip(kc[None, None] - qc[:, None, None] + 15, 0, 30)].reshape(16, P, -1)

    t = np.arange(T)
    inv = (np.float32(10000.0) ** (-np.arange(16, dtype=np.float32) / np.float32(16))).astype(np.float32)
    angles = [(pos.astype(np.float32)[None] * inv[:, None]).astype(np.float32) for pos in (t // GRID_W, t % GRID_W)]
    rope = np.zeros((P, 2, T), np.float32)
    for part in range(4):
        ang = angles[part % 2]
        for b, sign in ((0, -1.0), (1, 1.0)):
            r = slice(32 * part + 16 * b, 32 * part + 16 * b + 16)
            rope[r, 0] = np.cos(ang)
            rope[r, 1] = sign * np.sin(ang)

    vecs = np.concatenate([_tiles(norm_w[0]), _tiles(hgrn_gn[0]), _tiles(final_norm_w),
                           _tiles(ln_g_2.reshape(-1)), _tiles(ln_b_2.reshape(-1)), _tiles(b_ada_2.reshape(-1)),
                           _tiles(hgrn_lb_logits[0])], 1)
    lay = lambda v: np.ascontiguousarray(v)
    return {
        "w_stream": lay(np.stack(units)),
        "vecs": lay(vecs),
        "consts": consts,
        "hgrn_masks": masks,
        "fox_fb": lay(fox_fb[0][:, None]),
        "cond": lay(np.concatenate([c_2, c_ctx_2[None]])),
        "w_ada": lay(w_ada_2.reshape(2, D, 24, P).transpose(0, 2, 3, 1).reshape(ADA_UNITS, P, D)),
        "p_t": lay(p[0, 0].T.reshape(2, P, T).transpose(1, 0, 2)),
        "ctx_t": lay(ctx_2[0].T.reshape(KT, P, C).transpose(1, 0, 2)),
        "rope": rope,
        "rel_bias": lay(rel_bias),
        "a_sink": lay(a_sink_2[0][None]),
        "x_t": lay(x[0].T.reshape(KT, P, T).transpose(1, 0, 2)),
    }


def kernel(**inputs):
    from concourse import bacc
    from concourse.bass_utils import run_bass_kernel_spmd

    arrays = {f"in_{k}": v for k, v in lay_out(**{k: np.asarray(v) for k, v in inputs.items()}).items()}
    nc = bacc.Bacc("TRN2", target_bir_lowering=False, num_devices=1)
    tensors = {k[3:]: nc.dram_tensor(k, v.shape, mybir.dt.from_np(v.dtype), kind="ExternalInput").ap()
               for k, v in arrays.items()}
    tensors["out"] = nc.dram_tensor("out_t", (KT, P, T), F32, kind="ExternalOutput").ap()
    build_program(nc, tensors)
    out = run_bass_kernel_spmd(nc, [arrays], core_ids=[0]).results[0]["out_t"]
    return np.ascontiguousarray(out.reshape(1, D, T).transpose(0, 2, 1))
```

```python
from contextlib import ExitStack

import numpy as np
import concourse.bass as bass
from concourse import mybir

F32 = mybir.dt.float32
F32R = mybir.dt.float32r
ALU = mybir.AluOpType
ACT = mybir.ActivationFunctionType
AX = mybir.AxisListType.X
ds = bass.ds

P = 128
T = 1024
D = 1024
C = 256
TC = T + C
KT = D // P
CH = 512
PLE = 256
HG = 8
PAIRS = 8
HD = 64
HGRN_CHUNK = 32
LEVELS = 7
GRID_W = 64
BIG = -1e30
EPS = 1e-6
LN_EPS = 1e-5
ALPHA = (2.0 * 2) ** 0.25
ADA_UNITS = 48

V_NORM, V_GN, V_FINAL, V_LNG, V_LNB, V_BADA, V_LB, V_END = 0, 8, 16, 24, 40, 56, 104, 112
K_ID, K_TRI, K_WIN, K_COL, K_ROW, K_END = 0, 128, 256, 256 + 640, 256 + 640 + 64, 256 + 640 + 64 + 9

U_HGRN = 0
U_FZ = U_HGRN + 4 * HG
U_FOX = U_FZ + 2
U_OUT = U_FOX + 4 * PAIRS
U_PLE = U_OUT + 2 * KT
U_GATE = U_PLE + 2
U_A = U_GATE + KT
U_A_OUT = U_A + 20
U_B = U_A_OUT + KT
U_B_OUT = U_B + 4 * PAIRS
UNITS = U_B_OUT + KT
assert UNITS % 2 == 0


def build_program(nc, a, stop=99):
    ctx = ExitStack()

    def sb(name, shape, dt=F32, at=None):
        return (at or ctx).enter_context(nc.sbuf_tensor(name, shape, dt))

    def sem(name):
        return ctx.enter_context(nc.semaphore(name))

    with ctx:
        ps = ctx.enter_context(nc.psum_tensor("ps", [P, 8 * CH], F32))

        def bank(b, n=1):
            return ps[:, b * CH:(b + n) * CH]

        h_dram = nc.dram_tensor("residual", [KT, P, TC], F32).ap()
        y_dram = nc.dram_tensor("y_parts", [2, 16, P, TC], F32).ap()

        consts = sb("consts", [P, K_END])
        vecs = sb("vecs", [P, V_END])
        ident = consts[:, K_ID:K_ID + P]
        ada = sb("ada", [P, ADA_UNITS, 2])
        adv = sb("adv", [P, ADA_UNITS, 2])
        ones_mean = sb("ones_mean", [P, P])
        small = sb("small", [P, 8])
        raw = sb("raw", [P, 2, KT * P])
        w_hi = sb("w_hi", [P, 2, KT * P], F32R)
        w_lo = sb("w_lo", [P, 2, KT * P], F32R)

        def whi(slot, k):
            return w_hi[:, slot, k * P:(k + 1) * P]

        def wlo(slot, k):
            return w_lo[:, slot, k * P:(k + 1) * P]

        loaded = sem("loaded")
        x_loaded = sem("x_loaded")
        raw_loaded = [sem("raw_loaded0"), sem("raw_loaded1")]
        w_ready = sem("w_ready")
        w_used = sem("w_used")
        consts_set = sem("consts_set")

        block1 = ctx.enter_context(ExitStack())
        u_hi = sb("u_hi", [P, KT, T], F32R, block1)
        u_lo = sb("u_lo", [P, KT, T], F32R, block1)
        u_ready = sem("u_ready")

        def project(pe, n, slot, hi, lo, chunks, done, tiles=range(KT), first=0, start=True, stop=True, last=True):
            pe.wait_ge(w_ready, n + 1)
            for c, (cols, out, waits) in enumerate(chunks):
                for s, v in waits:
                    pe.wait_ge(s, v)
                for i, k in enumerate(tiles):
                    for p, (w, u) in enumerate(((whi, hi), (whi, lo), (wlo, hi))):
                        mm = pe.matmul(out, w(slot, k), u[:, first + i, cols],
                                       start=start and i == 0 and p == 0,
                                       stop=stop and i == len(tiles) - 1 and p == 2)
                mm.then_inc(w_used if last and c == len(chunks) - 1 else done, 1)

        def stream_loads(sp):
            for s in range(2):
                sp.dma_start(raw[:, s, :], a["w_stream"][s]).then_inc(raw_loaded[s], 16)

        def stream_loads_rest(sp):
            with sp.Fori(1, UNITS // 2) as i:
                for s in range(2):
                    sp.wait_ge(w_ready, i * 2 + (s - 1))
                    sp.dma_start(raw[:, s, :], a["w_stream"][ds(i * 2 + s, 1)].rearrange("a p n -> (a p) n")
                                 ).then_inc(raw_loaded[s], 16)

        def split_unit(pool, s):
            zero = small[:, 0:1].broadcast_to([P, KT * P])
            pool.tensor_tensor(w_hi[:, s, :], raw[:, s, :], zero, ALU.add)
            pool.drain()
            pool.tensor_tensor(w_lo[:, s, :], raw[:, s, :], w_hi[:, s, :].bitcast(F32),
                               ALU.subtract).then_inc(w_ready, 1)

        def stream_splits(pool):
            pool.wait_ge(consts_set, 1)
            for s in range(2):
                pool.wait_ge(raw_loaded[s], 16)
                split_unit(pool, s)
            with pool.Fori(1, UNITS // 2) as i:
                for s in range(2):
                    pool.wait_ge(raw_loaded[s], i * 16 + 16)
                    pool.wait_ge(w_used, i * 2 + (s - 1))
                    split_unit(pool, s)

        ph1 = ctx.enter_context(ExitStack())
        x_sb = sb("x_sb", [P, KT, T], at=ph1)
        sq1 = sb("sq1", [P, 2, T], at=ph1)
        rstd1 = sb("rstd1", [P, T], at=ph1)
        ph1.close()
        n1_sq = sem("n1_sq")
        n1_sum = sem("n1_sum")
        n1_sd = sem("n1_sd")
        n1_scaled = sem("n1_scaled")
        n1_hi = sem("n1_hi")

        def norm1_act(act):
            act.wait_ge(x_loaded, 16 * KT)
            act.wait_ge(consts_set, 1)
            for k in range(KT):
                if k >= 2:
                    act.wait_ge(n1_sum, k - 1)
                nc.scalar.activation(sq1[:, k % 2, :], x_sb[:, k, :], ACT.Square).then_inc(n1_sq, 1)
            act.wait_ge(n1_sum, KT)
            nc.scalar.activation(rstd1[:], bank(0, 2), ACT.Sqrt, bias=small[:, 1:2]).then_inc(n1_sd, 1)
            for k in range(KT):
                act.wait_ge(n1_scaled, k + 1)
                nc.scalar.copy(u_hi[:, k, :], x_sb[:, k, :]).then_inc(n1_hi, 1)

        def norm1_pe(pe):
            pe.wait_ge(consts_set, 1)
            for k in range(KT):
                pe.wait_ge(n1_sq, k + 1)
                for c in range(2):
                    mm = pe.matmul(bank(c), ones_mean[:], sq1[:, k % 2, c * CH:(c + 1) * CH],
                                   start=k == 0, stop=k == KT - 1)
                mm.then_inc(n1_sum, 1)

        def norm1_dve(dve):
            dve.memset(small[:, 0:1], 0.0)
            dve.memset(small[:, 1:2], EPS)
            dve.memset(small[:, 2:3], LN_EPS)
            dve.memset(ones_mean[:], 1.0 / D)
            dve.drain().then_inc(consts_set, 1)
            dve.wait_ge(loaded, 32)
            dve.wait_ge(n1_sd, 1)
            dve.reciprocal(rstd1[:], rstd1[:])
            dve.drain()
            for k in range(KT):
                dve.scalar_tensor_tensor(x_sb[:, k, :], x_sb[:, k, :], vecs[:, V_NORM + k:V_NORM + k + 1],
                                         rstd1[:], ALU.mult, ALU.mult).then_inc(n1_scaled, 1)
            for k in range(KT):
                dve.wait_ge(n1_hi, k + 1)
                dve.tensor_tensor(u_lo[:, k, :], x_sb[:, k, :], u_hi[:, k, :].bitcast(F32),
                                  ALU.subtract).then_inc(u_ready, 1)

        ph2 = ctx.enter_context(ExitStack())
        hgrn_masks = sb("hgrn_masks", [P, 2, T], at=ph2)
        z_f = sb("z_f", [P, T], at=ph2)
        t_a = sb("t_a", [P, T], at=ph2)
        t_g = sb("t_g", [P, T], at=ph2)
        k_t = sb("k_t", [P, T], at=ph2)
        q_t = sb("q_t", [P, T], at=ph2)
        i_t = sb("i_t", [P, T], at=ph2)
        b32 = sb("b32", [P, T], at=ph2)
        b128 = sb("b128", [P, T], at=ph2)
        off = sb("off", [P, 8, 4], at=ph2)
        tile_decay = sb("tile_decay", [P, 8], at=ph2)
        lev = sb("lev", [P, LEVELS, T], at=ph2)
        q_in = sb("q_in", [P, T], at=ph2)
        k_out = sb("k_out", [P, T], at=ph2)
        k_tok = sb("k_tok", [P, 8, P], at=ph2)
        i_tok = sb("i_tok", [P, 8, P], at=ph2)
        masked = sb("masked", [P, 8, P], at=ph2)
        scores = sb("scores", [P, 2, P], at=ph2)
        state = sb("state", [P, 2, P], at=ph2)
        silu_h = sb("silu_h", [P, T], at=ph2)
        o_n = sb("o_n", [P, T], at=ph2)
        ssq = sb("ssq", [P, 8], at=ph2)
        rs8 = sb("rs8", [P, 8], at=ph2)
        head_vec = sb("head_vec", [P, 4], at=ph2)
        lnom = sb("lnom", [P, 8], at=ph2)
        yh_hi = sb("yh_hi", [P, T], F32R, ph2)
        yh_lo = sb("yh_lo", [P, T], F32R, ph2)
        ph2.close()

        h_chunk = sem("h_chunk")
        h_z = sem("h_z")
        h_t2 = sem("h_t2")
        h_k = sem("h_k")
        h_q = sem("h_q")
        h_it = sem("h_it")
        h_tr = sem("h_tr")
        h_tok = sem("h_tok")
        h_e = sem("h_e")
        h_x = sem("h_x")
        h_kout = sem("h_kout")
        h_ops = sem("h_ops")
        h_sg = sem("h_sg")
        h_lv = sem("h_lv")
        h_sc = sem("h_sc")
        h_ds = sem("h_ds")
        h_s = sem("h_s")
        h_o = sem("h_o")
        h_sd = sem("h_sd")
        h_on = sem("h_on")
        h_yt = sem("h_yt")
        h_y = sem("h_y")
        h_hi = sem("h_hi")
        h_lo = sem("h_lo")
        h_spill = sem("h_spill")
        lb_set = sem("lb_set")
        lb_exp = sem("lb_exp")

        def hgrn_pe(pe):
            pe.wait_ge(u_ready, KT)
            with pe.Fori(0, HG) as h:
                n = h * 4 + U_HGRN

                def unit(j, b, waits):
                    project(pe, n + j, j % 2, u_hi, u_lo,
                            [(slice(c * CH, c * CH + CH), bank(b + c), waits if c == 0 else []) for c in range(2)],
                            h_chunk)

                unit(0, 0, [(h_sc, h * 8)])
                unit(1, 2, [])
                unit(2, 4, [(h_on, h)])
                unit(3, 0, [(h_z, h + 1)])
                pe.wait_ge(h_it, h + 1)
                pe.wait_ge(h_yt, h)
                for j in range(8):
                    mm = pe.transpose(ps[:, 6 * CH + j * P:6 * CH + (j + 1) * P], i_t[:, j * P:(j + 1) * P], ident)
                mm.then_inc(h_tr, 1)
                pe.wait_ge(h_ops, h + 1)

                def level_products(j):
                    if j == 0:
                        pe.wait_ge(h_sg, h + 1)
                    if j >= 2:
                        pe.wait_ge(h_sc, h * 8 + (j - 1))
                    t = slice(j * P, (j + 1) * P)
                    for lv in range(LEVELS + 1):
                        o = ps[:, (j % 2) * 2 * CH + lv * P:(j % 2) * 2 * CH + (lv + 1) * P]
                        if lv < LEVELS:
                            mm = pe.matmul(o, lev[:, lv, t], lev[:, lv, t], start=True, stop=True)
                        else:
                            mm = pe.matmul(o, k_t[:, t], q_t[:, t], start=True, stop=True)
                    mm.then_inc(h_lv, 1)

                level_products(0)
                pe.wait_ge(h_kout, h + 1)
                pe.wait_ge(h_tok, h * 2 + 1)
                for j in range(8):
                    mm = pe.transpose(ps[:, 6 * CH + j * P:6 * CH + (j + 1) * P], k_out[:, j * P:(j + 1) * P], ident)
                mm.then_inc(h_tr, 1)
                for j in range(8):
                    if j < 7:
                        level_products(j + 1)
                        if j == 0:
                            pe.wait_ge(h_tok, h * 2 + 2)
                        else:
                            pe.wait_ge(h_s, h * 7 + j)
                        pe.matmul(ps[:, 6 * CH:6 * CH + P], k_tok[:, j, :], i_tok[:, j, :],
                                  start=True, stop=True).then_inc(h_ds, 1)
                    pe.wait_ge(h_sc, h * 8 + (j + 1))
                    o = ps[:, 4 * CH + j * P:4 * CH + (j + 1) * P]
                    mm = pe.matmul(o, scores[:, j % 2, :], i_tok[:, j, :], start=True, stop=j == 0)
                    if j:
                        pe.wait_ge(h_s, h * 7 + j)
                        mm = pe.matmul(o, q_in[:, j * P:(j + 1) * P], state[:, j % 2, :], start=False, stop=True)
                    mm.then_inc(h_o, 1)
                pe.wait_ge(h_on, h + 1)
                for j in range(8):
                    mm = pe.transpose(ps[:, 6 * CH + j * P:6 * CH + (j + 1) * P], o_n[:, j * P:(j + 1) * P], ident)
                mm.then_inc(h_y, 1)

        def hgrn_act(act):
            act.wait_ge(lb_set, 1)
            act.dma_start(hgrn_masks[:], a["hgrn_masks"]).then_inc(loaded, 16)
            nc.scalar.activation(lnom[:], lnom[:], ACT.Exp).then_inc(lb_exp, 1)
            act.wait_ge(lb_set, 2)
            nc.scalar.activation(lnom[:], lnom[:], ACT.Ln, bias=1.0, scale=-1.0).then_inc(lb_exp, 1)
            with act.Fori(0, HG) as h:
                act.wait_ge(h_chunk, h * 4 + 1)
                act.wait_ge(w_used, h * 4 + 1)
                nc.scalar.copy(z_f[:], bank(0, 2))
                nc.scalar.activation(t_a[:], bank(0, 2), ACT.Abs)
                act.drain()
                nc.scalar.activation(t_a[:], t_a[:], ACT.Exp, scale=-1.0)
                act.drain()
                nc.scalar.activation(t_a[:], t_a[:], ACT.Ln, bias=1.0).then_inc(h_z, 1)
                act.wait_ge(h_t2, h + 1)
                nc.scalar.activation(k_t[:], t_a[:], ACT.Exp).then_inc(h_k, 1)
                for lv in range(LEVELS):
                    act.wait_ge(h_e, h * 9 + (lv + 1))
                    nc.scalar.activation(lev[:, lv, :], lev[:, lv, :], ACT.Exp).then_inc(h_x, 1)
                act.wait_ge(h_e, h * 9 + 9)
                nc.scalar.activation(q_in[:], b128[:], ACT.Exp).then_inc(h_x, 1)
                nc.scalar.activation(k_out[:], k_out[:], ACT.Exp)
                nc.scalar.activation(tile_decay[:], b128[:].rearrange("p (j t) -> p j t", j=8)[:, :, P - 1],
                                     ACT.Exp).then_inc(h_x, 1)
                act.wait_ge(h_chunk, h * 4 + 2)
                act.wait_ge(w_used, h * 4 + 2)
                nc.scalar.activation(q_t[:], bank(2, 2), ACT.Copy, scale=float(P) ** -0.5).then_inc(h_q, 1)
                act.wait_ge(h_chunk, h * 4 + 3)
                act.wait_ge(w_used, h * 4 + 3)
                nc.scalar.copy(i_t[:], bank(4, 2)).then_inc(h_it, 1)
                act.wait_ge(h_chunk, h * 4 + 4)
                act.wait_ge(w_used, h * 4 + 4)
                nc.scalar.activation(silu_h[:], bank(0, 2), ACT.Silu).then_inc(h_sg, 1)
                act.wait_ge(h_tr, h * 2 + 1)
                nc.scalar.copy(i_tok[:].rearrange("p j t -> p (j t)"), bank(6, 2)).then_inc(h_tok, 1)
                act.wait_ge(h_tr, h * 2 + 2)
                nc.scalar.copy(k_tok[:].rearrange("p j t -> p (j t)"), bank(6, 2)).then_inc(h_tok, 1)
                for j in range(8):
                    if j % 4 == 0:
                        act.wait_ge(h_o, h * 8 + (j + 4))
                    nc.scalar.activation(q_in[:, j * P:(j + 1) * P], ps[:, 4 * CH + j * P:4 * CH + (j + 1) * P],
                                         ACT.Square, accum_out=ssq[:, j:j + 1])
                act.drain()
                nc.scalar.activation(ssq[:], ssq[:], ACT.Sqrt, bias=small[:, 1:2], scale=1.0 / P).then_inc(h_sd, 1)
                act.wait_ge(h_yt, h + 1)
                act.wait_ge(h_spill, h * 32)
                nc.scalar.copy(yh_hi[:], o_n[:]).then_inc(h_hi, 1)
                act.wait_ge(h_lo, h + 1)
                for part, src in ((0, yh_hi), (1, yh_lo)):
                    act.dma_start(y_dram[part, ds(h, 1), :, 0:T].rearrange("a p t -> (a p) t"), src[:].bitcast(F32)
                                  ).then_inc(h_spill, 16)

        def hgrn_dve(dve):
            lb_in = vecs[:, V_LB:V_LB + 8]
            dve.wait_ge(u_ready, KT)
            dve.tensor_tensor(lnom[:], lb_in, lb_in, ALU.subtract).then_inc(lb_set, 1)
            dve.wait_ge(lb_exp, 1)
            dve.reciprocal(ssq[:], lnom[:])
            dve.drain()
            dve.tensor_tensor(lnom[:], lnom[:], ssq[:], ALU.mult)
            dve.drain()
            dve.tensor_tensor(lnom[:], lnom[:], lnom[:], ALU.subtract)
            dve.drain().then_inc(lb_set, 1)
            dve.wait_ge(lb_exp, 2)
            dve.wait_ge(loaded, 48)
            with dve.Fori(0, HG) as h:
                dve.tensor_copy(head_vec[:, 0:1], vecs[:, ds(h + V_GN, 1)])
                dve.tensor_copy(head_vec[:, 1:2], lnom[:, ds(h, 1)])
                dve.drain()
                dve.wait_ge(h_z, h + 1)
                dve.scalar_tensor_tensor(t_g[:], z_f[:], 0.0, t_a[:], ALU.min, ALU.subtract)
                dve.drain()
                dve.tensor_tensor(t_a[:], t_g[:], z_f[:], ALU.subtract)
                dve.tensor_scalar(t_g[:], t_g[:], head_vec[:, 1:2], None, ALU.add)
                dve.drain()
                dve.tensor_scalar(t_a[:], t_a[:], head_vec[:, 1:2], None, ALU.add).then_inc(h_t2, 1)
                dve.tensor_tensor_scan(b32[:], hgrn_masks[:, 1, :], t_g[:], 0.0, ALU.mult, ALU.add)
                dve.drain()
                tot = b32[:].rearrange("p (j c t) -> p j c t", c=4, t=32)[:, :, :, 31]
                dve.memset(off[:, :, 0], 0.0)
                dve.tensor_copy(off[:, :, 1], tot[:, :, 0])
                dve.tensor_tensor(off[:, :, 2], tot[:, :, 0], tot[:, :, 1], ALU.add)
                dve.drain()
                dve.tensor_tensor(off[:, :, 3], off[:, :, 2], tot[:, :, 2], ALU.add)
                dve.drain()
                dve.tensor_tensor(b128[:].rearrange("p (c t) -> p c t", t=32),
                                  b32[:].rearrange("p (c t) -> p c t", t=32),
                                  off[:].rearrange("p j c -> p (j c)").unsqueeze(2).broadcast_to([P, 32, 32]), ALU.add)
                dve.drain()
                for lv in range(LEVELS):
                    H = 1 << lv
                    b = (b32 if 2 * H <= HGRN_CHUNK else b128)[:].rearrange("p (g r t) -> p g r t", r=2, t=H)
                    e = lev[:, lv, :].rearrange("p (g r t) -> p g r t", r=2, t=H)
                    mid = b[:, :, 0, H - 1:H].broadcast_to([P, T // (2 * H), H])
                    dve.tensor_tensor(e[:, :, 0, :], mid, b[:, :, 0, :], ALU.subtract)
                    dve.tensor_tensor(e[:, :, 1, :], b[:, :, 1, :], mid, ALU.subtract).then_inc(h_e, 1)
                bt = b128[:].rearrange("p (j t) -> p j t", t=P)
                dve.tensor_tensor(k_out[:].rearrange("p (j t) -> p j t", t=P),
                                  bt[:, :, P - 1:P].broadcast_to([P, 8, P]), bt, ALU.subtract).then_inc(h_e, 2)
                dve.wait_ge(h_k, h + 1)
                for lv in range(LEVELS):
                    H = 1 << lv
                    e = lev[:, lv, :].rearrange("p (g r t) -> p g r t", r=2, t=H)
                    k = k_t[:].rearrange("p (g r t) -> p g r t", r=2, t=H)
                    dve.wait_ge(h_x, h * 9 + (lv + 1))
                    dve.tensor_tensor(e[:, :, 0, :], e[:, :, 0, :], k[:, :, 0, :], ALU.mult)
                dve.wait_ge(h_x, h * 9 + 9)
                dve.tensor_tensor(k_out[:], k_out[:], k_t[:], ALU.mult).then_inc(h_kout, 1)
                dve.wait_ge(h_q, h + 1)
                dve.tensor_tensor(q_in[:], q_in[:], q_t[:], ALU.mult)
                for lv in range(LEVELS):
                    H = 1 << lv
                    e = lev[:, lv, :].rearrange("p (g r t) -> p g r t", r=2, t=H)
                    q = q_t[:].rearrange("p (g r t) -> p g r t", r=2, t=H)
                    dve.tensor_tensor(e[:, :, 1, :], e[:, :, 1, :], q[:, :, 1, :], ALU.mult)
                dve.drain().then_inc(h_ops, 1)

                def tile_scores(j):
                    dve.drain()
                    dve.wait_ge(h_lv, h * 8 + (j + 1))
                    if j >= 2:
                        dve.wait_ge(h_o, h * 8 + (j - 1))
                    dve.tensor_tensor(masked[:].rearrange("p l t -> p (l t)"), bank((j % 2) * 2, 2),
                                      hgrn_masks[:, 0, :], ALU.mult)
                    dve.drain()
                    dve.tensor_reduce(scores[:, j % 2, :], masked[:].rearrange("p l t -> p t l"), AX,
                                      ALU.add).then_inc(h_sc, 1)

                tile_scores(0)
                for j in range(7):
                    tile_scores(j + 1)
                    if j:
                        dve.drain()
                    dve.wait_ge(h_ds, h * 7 + (j + 1))
                    if j == 0:
                        dve.tensor_copy(state[:, 1, :], ps[:, 6 * CH:6 * CH + P]).then_inc(h_s, 1)
                    else:
                        dve.wait_ge(h_o, h * 8 + j)
                        dve.scalar_tensor_tensor(state[:, (j + 1) % 2, :], state[:, j % 2, :],
                                                 tile_decay[:, j:j + 1], ps[:, 6 * CH:6 * CH + P],
                                                 ALU.mult, ALU.add).then_inc(h_s, 1)
                dve.wait_ge(h_sd, h + 1)
                dve.reciprocal(rs8[:], ssq[:])
                dve.drain()
                dve.tensor_tensor(o_n[:].rearrange("p (j t) -> p j t", t=P),
                                  bank(4, 2).rearrange("p (j t) -> p j t", t=P),
                                  rs8[:].unsqueeze(2).broadcast_to([P, 8, P]), ALU.mult).then_inc(h_on, 1)
                dve.wait_ge(h_y, h + 1)
                dve.scalar_tensor_tensor(o_n[:], bank(6, 2), head_vec[:, 0:1], silu_h[:],
                                         ALU.mult, ALU.mult).then_inc(h_yt, 1)
                dve.wait_ge(h_hi, h + 1)
                dve.tensor_tensor(yh_lo[:], o_n[:], yh_hi[:].bitcast(F32), ALU.subtract).then_inc(h_lo, 1)

        class Attention:

            def __init__(self, name, blocks, halves, width, keys, q_cols, area, ahead=2):
                self.blocks, self.halves, self.name = blocks, halves, name
                self.NB, self.NA, self.NH = len(blocks), 2 * len(blocks), len(halves)
                self.q2 = [sb(f"{name}_q2_{i}", [P, q_cols], F32R, area) for i in range(2)]
                self.l = sb(f"{name}_l", [P, 3, width], at=area)
                self.pt = sb(f"{name}_pt", [P, 3, CH], at=area)
                self.nm = sb(f"{name}_nm", [P, self.NA, 2], at=area)
                self.rs = sb(f"{name}_rs", [P, self.NA], at=area)
                self.ri = sb(f"{name}_ri", [P, self.NA], at=area)
                self.o_tok = sb(f"{name}_o_tok", [P, self.NB, P], at=area)
                self.silu = sb(f"{name}_silu", [P, q_cols], at=area)
                self.y = sb(f"{name}_y", [P, q_cols], at=area)
                self.y_hi = sb(f"{name}_y_hi", [P, q_cols], F32R, area)
                self.y_lo = sb(f"{name}_y_lo", [P, q_cols], F32R, area)
                self.scored = sem(f"{name}_scored")
                self.shifted = sem(f"{name}_shifted")
                self.exped = sem(f"{name}_exped")
                self.turned = sem(f"{name}_turned")
                self.copied = {"act": sem(f"{name}_copied_act"), "dve": sem(f"{name}_copied_dve")}
                self.valued = sem(f"{name}_valued")
                self.left = sem(f"{name}_left")
                self.hi_done = sem(f"{name}_hi_done")
                self.lo_done = sem(f"{name}_lo_done")
                self.spilled = sem(f"{name}_spilled")
                self.chunk = sem(f"{name}_chunk")
                self.plan(ahead)

            def plan(self, ahead):
                self.groups, self.copier, self.place, self.v_place = [], [], [], []
                self.steps = [("S", u) for u in range(min(ahead, self.NA))]
                load, waiting, late = {"act": 0, "dve": 0}, [], []

                def add(group, eng, cost):
                    load[eng] += cost
                    self.place.append(self.copier.count(eng))
                    self.v_place.append(sum(g[0] == "P" for g in self.groups))
                    self.groups.append(group)
                    self.copier.append(eng)
                    self.steps.append(("T", len(self.groups) - 1))

                def value():
                    g = waiting.pop(0)
                    self.steps.append(("V", g))
                    _, u, _, c1 = self.groups[g]
                    if u % 2 and c1 == len(self.blocks[u // 2]["chunks"]):
                        self.steps.append(("O", u // 2))
                        for hf, bs in enumerate(self.halves):
                            if u // 2 == bs[-1]:
                                late.append(hf)

                for u in range(self.NA):
                    if u + ahead < self.NA:
                        self.steps.append(("S", u + ahead))
                    blk = self.blocks[u // 2]
                    n, w = len(blk["chunks"]), blk["width"]
                    load["act"] += 200 + 0.83 * w
                    load["dve"] += 250 + 1.04 * w + (100 if u % 2 else 0)
                    for hf in [late.pop(0)] if late else []:
                        add(("Y", hf), "dve", 60 + 1.04 * P * len(self.halves[hf]))
                    parts = (n + 3) // 4
                    if n > 2:
                        parts = max(parts, 2)
                    for i in range(parts):
                        c0, c1 = n * i // parts, n * (i + 1) // parts
                        cost = {"act": 190 + 0.83 * P * (c1 - c0), "dve": 70 + 1.04 * P * (c1 - c0)}
                        eng = min(cost, key=lambda e: load[e] + cost[e])
                        add(("P", u, c0, c1), eng, cost[eng])
                        waiting.append(len(self.groups) - 1)
                        if len(waiting) > 2:
                            value()
                while waiting:
                    value()
                for hf in late:
                    add(("Y", hf), "dve", 0)
                self.NG = len(self.groups)
                self.NV = sum(g[0] == "P" for g in self.groups)
                self.copies = {e: self.copier.count(e) for e in load}

            def last_group(self, u):
                return max(g for g, x in enumerate(self.groups) if x[0] == "P" and x[1] == u)

            def all_copied(self, it):
                return [(self.copied[e], it * self.copies[e]) for e in ("act", "dve")]

            def group_copied(self, it, g):
                e = self.copier[g]
                return self.copied[e], it * self.copies[e] + (self.place[g] + 1)

            def pe(self, pe, it, k2a, k2b, v, before):
                for step in self.steps:
                    if step[0] == "S":
                        u = step[1]
                        blk = self.blocks[u // 2]
                        pe.wait_ge(self.shifted, it * self.NA + max(u - 1, 0))
                        for s, w in before.get(step, []):
                            pe.wait_ge(s, w)
                        q = self.q2[u % 2][:, blk["b"] * P:(blk["b"] + 1) * P]
                        for pc, kc, n in blk["runs"]:
                            o = ps[:, (u % 2) * 2 * CH + pc:(u % 2) * 2 * CH + pc + n]
                            pe.matmul(o, q, k2a[u % 2][:, kc:kc + n], start=True, stop=False)
                            mm = pe.matmul(o, q, k2b[u % 2][:, kc:kc + n], start=False, stop=True)
                        mm.then_inc(self.scored, 1)
                    elif step[0] == "T":
                        g = step[1]
                        for s, w in [self.group_copied(it, g - 2)] if g >= 2 else self.all_copied(it):
                            pe.wait_ge(s, w)
                        out = ps[:, (4 + g % 2) * CH:(5 + g % 2) * CH]
                        if self.groups[g][0] == "P":
                            _, u, c0, c1 = self.groups[g]
                            pe.wait_ge(self.exped, it * self.NA + (u + 1))
                            for s, w in before.get(step, []):
                                pe.wait_ge(s, w)
                            for c in range(c0, c1):
                                pc, n, _ = self.blocks[u // 2]["chunks"][c]
                                mm = pe.transpose(out[0:n, (c - c0) * P:(c - c0 + 1) * P],
                                                  self.l[:, u % 3, pc:pc + n], ident)
                        else:
                            bs = self.halves[self.groups[g][1]]
                            pe.wait_ge(self.left, it * self.NB + (bs[-1] + 1))
                            for i, b in enumerate(bs):
                                mm = pe.transpose(out[:, i * P:(i + 1) * P], self.o_tok[:, b, :], ident)
                        mm.then_inc(self.turned, 1)
                    elif step[0] == "V":
                        g = step[1]
                        _, u, c0, c1 = self.groups[g]
                        b, hd = u // 2, u % 2
                        blk = self.blocks[b]
                        pe.wait_ge(*self.group_copied(it, g))
                        if c0 == 0 and hd == 0:
                            pe.wait_ge(self.left, it * self.NB + max(b - 1, 0))
                            for s, w in before.get(("V", b), []):
                                pe.wait_ge(s, w)
                        o0 = (6 + b % 2) * CH + hd * HD
                        vals, cols = v[hd]
                        for c in range(c0, c1):
                            _, n, vb = blk["chunks"][c]
                            mm = pe.matmul(ps[:, o0:o0 + HD],
                                           self.pt[0:n, self.v_place[g] % 3, (c - c0) * P:(c - c0 + 1) * P],
                                           vals[0:n, vb, cols], start=c == 0, stop=c == len(blk["chunks"]) - 1)
                        mm.then_inc(self.valued, 1)

            def act(self, act, it):
                for step in self.steps:
                    if step[0] == "S":
                        u = step[1]
                        w = self.blocks[u // 2]["width"]
                        act.wait_ge(self.shifted, it * self.NA + (u + 1))
                        nc.scalar.activation(self.l[:, u % 3, 0:w], self.l[:, u % 3, 0:w], ACT.Exp, scale=-1.0,
                                             bias=self.nm[:, u, 1:2], accum_out=self.rs[:, u:u + 1]
                                             ).then_inc(self.exped, 1)
                    elif step[0] == "T" and self.copier[step[1]] == "act":
                        self.copy_group(act, it, step[1], nc.scalar.copy)

            def copy_group(self, eng, it, g, copy):
                _, u, c0, c1 = self.groups[g]
                eng.wait_ge(self.turned, it * self.NG + (g + 1))
                i = self.v_place[g]
                eng.wait_ge(self.valued, it * self.NV + max(i - 2, 0))
                n = self.blocks[u // 2]["chunks"][c1 - 1][1]
                full = (c1 - c0 - (n < P)) * P
                src = ps[:, (4 + g % 2) * CH:(5 + g % 2) * CH]
                if n < P:
                    ins = copy(self.pt[0:n, i % 3, full:full + P], src[0:n, full:full + P])
                if full:
                    ins = copy(self.pt[:, i % 3, 0:full], src[:, 0:full])
                ins.then_inc(self.copied[self.copier[g]], 1)

            def dve(self, dve, it, start, masks):
                for step in self.steps:
                    if step[0] == "S":
                        u = step[1]
                        blk = self.blocks[u // 2]
                        dve.wait_ge(self.turned, it * self.NG + (self.last_group(u - 3) + 1 if u >= 3 else 0))
                        dve.wait_ge(self.scored, it * self.NA + (u + 1))
                        start(u, self.nm[:, u, 0:1])
                        segs = masks(u)
                        dve.drain()
                        p1 = (u % 2) * 2 * CH + blk["first"]
                        for i, (p0, n, mask) in enumerate(segs):
                            if i:
                                dve.drain()
                            end = i == len(segs) - 1
                            ins = dve.tensor_tensor_reduce(
                                self.l[:, u % 3, p0:p0 + n], ps[:, p1 + p0:p1 + p0 + n], mask, -1.0,
                                self.nm[:, u, 0:1], ALU.add, ALU.min,
                                self.nm[:, u, 1:2] if end else self.nm[:, u, 0:1])
                        ins.then_inc(self.shifted, 1)
                    elif step[0] == "T" and self.copier[step[1]] == "dve":
                        g = step[1]
                        if self.groups[g][0] == "P":
                            self.copy_group(dve, it, g, dve.tensor_copy)
                            continue
                        bs = self.halves[self.groups[g][1]]
                        t0, n = self.blocks[bs[0]]["b"] * P, len(bs) * P
                        dve.wait_ge(self.turned, it * self.NG + (g + 1))
                        dve.tensor_tensor(self.y[:, t0:t0 + n], ps[:, (4 + g % 2) * CH:(4 + g % 2) * CH + n],
                                          self.silu[:, t0:t0 + n], ALU.mult).then_inc(self.copied["dve"], 1)
                    elif step[0] == "O":
                        b = step[1]
                        dve.wait_ge(self.valued, it * self.NV + (self.v_place[self.last_group(2 * b + 1)] + 1))
                        dve.reciprocal(self.ri[:, 2 * b:2 * b + 2], self.rs[:, 2 * b:2 * b + 2])
                        dve.drain()
                        dve.tensor_tensor(self.o_tok[:, b, :].rearrange("p (h d) -> p h d", h=2),
                                          ps[:, (6 + b % 2) * CH:(6 + b % 2) * CH + P].rearrange("p (h d) -> p h d", h=2),
                                          self.ri[:, 2 * b:2 * b + 2].unsqueeze(2).broadcast_to([P, 2, HD]),
                                          ALU.mult).then_inc(self.left, 1)

            def finish_act(self, act, it, y_index, cols):
                act.wait_ge(self.copied["dve"], (it + 1) * self.copies["dve"])
                act.wait_ge(self.spilled, it * 32)
                nc.scalar.copy(self.y_hi[:], self.y[:]).then_inc(self.hi_done, 1)
                act.wait_ge(self.lo_done, it + 1)
                for part, src in ((0, self.y_hi), (1, self.y_lo)):
                    act.dma_start(y_dram[part, ds(y_index, 1), :, 0:cols].rearrange("a p t -> (a p) t"),
                                  src[:].bitcast(F32)).then_inc(self.spilled, 16)

            def finish_dve(self, dve, it):
                dve.wait_ge(self.hi_done, it + 1)
                dve.tensor_tensor(self.y_lo[:], self.y[:], self.y_hi[:].bitcast(F32),
                                  ALU.subtract).then_inc(self.lo_done, 1)

        def rows_of(hd):
            return slice(hd * HD, hd * HD + HD)

        ph3 = ctx.enter_context(ExitStack())

        def fox_block(b):
            w = (b + 1) * P
            first = max(min(w, CH) if w <= CH else w // 2 // P * P, 2 * P)
            runs = [(CH - first, 0, first)]
            if w > first:
                runs.append((CH, first, w - first))
            return {"b": b, "width": w, "first": CH - first, "runs": runs,
                    "chunks": [(c * P, P, c) for c in range(b + 1)]}

        fox = Attention("fox", [fox_block(b) for b in range(8)], [[0, 1, 2, 3], [4, 5, 6, 7]], T, T, T, ph3)
        fx_k2a = [sb(f"fx_k2a{i}", [P, T], F32R, ph3) for i in range(2)]
        fx_k2b = [sb(f"fx_k2b{i}", [P, T], F32R, ph3) for i in range(2)]
        fx_v = sb("fx_v", [P, 8, P], at=ph3)
        fx_vt = sb("fx_vt", [P, T], at=ph3)
        nf = sb("nf", [P, T], at=ph3)
        nf_t = sb("nf_t", [P, T], at=ph3)
        fb = sb("fb", [16, 1], at=ph3)
        nf_b = sb("nf_b", [P, 2, T], at=ph3)
        nf_tri = sb("nf_tri", [P, 2, P], at=ph3)
        cond = sb("cond", [P, 2, D], at=ph3)
        ada_w = sb("ada_w", [P, 3, D], at=ph3)
        ada_acc = sb("ada_acc", [P, 12], at=ph3)
        ph3.close()

        fb_loaded = sem("fb_loaded")
        fz_shift = sem("fz_shift")
        fz_act = sem("fz_act")
        fz_done = sem("fz_done")
        nf_stored = sem("nf_stored")
        nf_loaded = sem("nf_loaded")
        f_hi = sem("f_hi")
        f_lo = sem("f_lo")
        f_v = sem("f_v")
        f_g = sem("f_g")
        f_vt = sem("f_vt")
        f_vc = sem("f_vc")
        cond_set = sem("cond_set")
        ada_loaded = sem("ada_loaded")
        ada_done = sem("ada_done")
        area3 = sem("area3")
        nf_dram = nc.dram_tensor("nf_rows", [16, T], F32).ap()

        def fz_pe(pe):
            pe.wait_ge(h_yt, HG)
            pe.wait_ge(h_sc, 8 * HG)
            project(pe, U_FZ, 0, u_hi, u_lo, [(slice(c * CH, c * CH + CH), bank(c), []) for c in range(2)], h_chunk)
            pe.wait_ge(w_ready, U_FZ + 2)
            pe.drain().then_inc(w_used, 1)

        def fz_act_part(act):
            act.wait_ge(h_spill, 32 * HG)
            act.dma_start(fb[:], a["fox_fb"]).then_inc(fb_loaded, 16)
            for i in range(2):
                act.dma_start(cond[:, i, :], a["cond"][i:i + 1, :].broadcast_to([P, D])).then_inc(fb_loaded, 16)
            act.wait_ge(h_chunk, 4 * HG + 1)
            act.wait_ge(w_used, U_FZ + 1)
            act.wait_ge(fb_loaded, 48)
            r = slice(0, 16)
            nc.scalar.activation(nf_t[r], ps[r, 0:T], ACT.Identity, bias=fb[:, 0:1])
            nc.scalar.activation(nf[r], ps[r, 0:T], ACT.Abs, bias=fb[:, 0:1])
            act.drain()
            nc.scalar.activation(nf[r], nf[r], ACT.Exp, scale=-1.0)
            act.drain()
            nc.scalar.activation(nf[r], nf[r], ACT.Ln, bias=1.0).then_inc(fz_act, 1)
            nc.scalar.activation(cond[:].rearrange("p a b -> p (a b)"), cond[:].rearrange("p a b -> p (a b)"),
                                 ACT.Silu).then_inc(cond_set, 1)
            act.wait_ge(fz_done, 1)
            act.dma_start(nf_dram, nf[r]).then_inc(nf_stored, 16)
            act.wait_ge(nf_stored, 16)

        def fz_dve(dve):
            dve.wait_ge(h_spill, 32 * HG)
            dve.memset(nf_b[0:16, 0, :], 1.0)
            dve.drain().then_inc(area3, 1)
            dve.wait_ge(fz_act, 1)
            r = slice(0, 16)
            dve.scalar_tensor_tensor(nf_t[r], nf_t[r], 0.0, nf[r], ALU.min, ALU.subtract)
            dve.drain()
            dve.tensor_tensor_scan(nf[r], nf_b[r, 0, :], nf_t[r], 0.0, ALU.mult, ALU.subtract)
            dve.drain().then_inc(fz_done, 1)

        def fox_pe(pe):
            with pe.Fori(0, PAIRS) as it:
                n = it * 4 + U_FOX

                def unit(j, b, waits):
                    project(pe, n + j, j % 2, u_hi, u_lo,
                            [(slice(c * CH, c * CH + CH), bank(b + c), waits if c == 0 else []) for c in range(2)],
                            fox.chunk)

                unit(0, 0, [(fox.shifted, it * fox.NA), (fz_act, 1)])
                unit(1, 2, [])
                unit(2, 4, fox.all_copied(it))
                unit(3, 6, [(fox.left, it * fox.NB)])
                pe.wait_ge(f_v, it + 1)
                for j in range(8):
                    mm = pe.transpose(ps[:, 4 * CH + j * P:4 * CH + (j + 1) * P], fx_vt[:, j * P:(j + 1) * P], ident)
                mm.then_inc(f_vt, 1)
                fox.pe(pe, it, fx_k2a, fx_k2b, [(fx_v, rows_of(hd)) for hd in range(2)],
                       {("S", 0): [(f_lo, it * 2 + 2)],
                        ("T", 0): [(f_vc, it + 1)],
                        ("V", 0): [(f_g, it + 1)]})

        def fox_act(act):
            act.wait_ge(area3, 1)
            with act.Fori(0, PAIRS) as it:
                act.wait_ge(fox.shifted, it * fox.NA)
                for hd in range(2):
                    act.dma_start(nf_b[:, hd, :], nf_dram[ds(it * 2 + hd, 1), :].broadcast_to([P, T])
                                  ).then_inc(nf_loaded, 16)

                def load_ada(half):
                    act.wait_ge(ada_done, it * 2 + half)
                    for j in range(3):
                        act.dma_start(ada_w[:, j, :], a["w_ada"][ds(it * 6 + (3 * half + j), 1)
                                                                 ].rearrange("a p n -> (a p) n")
                                      ).then_inc(ada_loaded, 16)

                load_ada(0)
                act.wait_ge(fox.chunk, it * 4 + 1)
                act.wait_ge(w_used, it * 4 + (U_FOX + 1))
                for hd in range(2):
                    ins = nc.scalar.activation(fox.q2[hd][0:HD, :], bank(0, 2)[rows_of(hd)], ACT.Copy, scale=HD ** -0.5)
                ins.then_inc(f_hi, 1)
                act.wait_ge(fox.chunk, it * 4 + 2)
                act.wait_ge(w_used, it * 4 + (U_FOX + 2))
                for hd in range(2):
                    for half in range(2):
                        ins = nc.scalar.copy(fx_k2a[hd][rows_of(half), :], bank(2, 2)[rows_of(hd)])
                ins.then_inc(f_hi, 1)
                load_ada(1)
                act.wait_ge(fox.chunk, it * 4 + 3)
                act.wait_ge(w_used, it * 4 + (U_FOX + 3))
                nc.scalar.copy(fx_vt[:], bank(4, 2)).then_inc(f_v, 1)
                act.wait_ge(fox.chunk, it * 4 + 4)
                act.wait_ge(w_used, it * 4 + (U_FOX + 4))
                nc.scalar.activation(fox.silu[:], bank(6, 2), ACT.Silu).then_inc(f_g, 1)
                act.wait_ge(f_vt, it + 1)
                nc.scalar.copy(fx_v[:].rearrange("p j t -> p (j t)"), bank(4, 2)).then_inc(f_vc, 1)
                fox.act(act, it)
                fox.finish_act(act, it, it + 8, T)

        def fox_dve(dve):
            dve.wait_ge(cond_set, 1)
            with dve.Fori(0, PAIRS) as it:
                dve.wait_ge(fox.turned, it * fox.NG)

                def dot_ada(half):
                    for j in range(3):
                        for i in range(2):
                            k = 6 * half + 2 * j + i
                            dve.wait_ge(ada_loaded, it * 96 + 48 * (half + 1))
                            dve.memset(ada_acc[:, k:k + 1], 0.0)
                            dve.drain()
                            ins = dve.tensor_tensor_reduce(fox.l[:, i, :], ada_w[:, j, :], cond[:, i, :], 1.0,
                                                           ada_acc[:, k:k + 1], ALU.mult, ALU.add,
                                                           ada_acc[:, k:k + 1])
                    ins.then_inc(ada_done, 1)

                dot_ada(0)
                dve.wait_ge(f_hi, it * 2 + 1)
                for hd in range(2):
                    ins = dve.scalar_tensor_tensor(fox.q2[hd][HD:P, :], bank(0, 2)[rows_of(hd)], HD ** -0.5,
                                                   fox.q2[hd][0:HD, :].bitcast(F32), ALU.mult, ALU.subtract)
                ins.then_inc(f_lo, 1)
                dve.wait_ge(f_hi, it * 2 + 2)
                for hd in range(2):
                    for half in range(2):
                        ins = dve.tensor_tensor(fx_k2b[hd][rows_of(half), :], bank(2, 2)[rows_of(hd)],
                                                fx_k2a[hd][0:HD, :].bitcast(F32), ALU.subtract)
                ins.then_inc(f_lo, 1)
                dot_ada(1)
                dve.drain()
                dve.tensor_copy(ada[:].rearrange("p u i -> p (u i)")[:, ds(it * 12, 12)], ada_acc[:])
                dve.drain()
                dve.wait_ge(nf_loaded, it * 32 + 32)

                def masks(u):
                    b, hd = u // 2, u % 2
                    dve.tensor_tensor(nf_tri[:, hd, :], nf_b[:, hd, b * P:(b + 1) * P],
                                      consts[:, K_TRI:K_TRI + P], ALU.add)
                    return ([(0, b * P, nf_b[:, hd, 0:b * P])] if b else []) + [(b * P, P, nf_tri[:, hd, :])]

                fox.dve(dve, it, lambda u, nm: dve.memset(nm, 3e38), masks)
                fox.finish_dve(dve, it)

        block1.close()
        ph4 = ctx.enter_context(ExitStack())
        y_hi = sb("y_hi", [P, 16, T], F32R, ph4)
        y_lo = sb("y_lo", [P, 16, T], F32R, ph4)
        h_area = ctx.enter_context(ExitStack())
        h_sb = sb("h_sb", [P, KT, T], at=h_area)
        x_in = sb("x_in", [P, 2, T], at=h_area)
        ctx_in = sb("ctx_in", [P, KT, C], at=h_area)
        h_area.close()
        ph4.close()
        y4_loaded = sem("y4_loaded")
        x4_loaded = sem("x4_loaded")
        o_chunk = sem("o_chunk")
        o_added = sem("o_added")

        ph4b = ctx.enter_context(ExitStack())
        r_hi = sb("r_hi", [P, KT, T], F32R, ph4b)
        r_lo = sb("r_lo", [P, KT, T], F32R, ph4b)
        ple = sb("ple", [P, KT, T], at=ph4b)
        p_hi = sb("p_hi", [P, 2, T], F32R, ph4b)
        p_lo = sb("p_lo", [P, 2, T], F32R, ph4b)
        sig = sb("sig", [P, 2, T], at=ph4b)
        ph4b.close()
        p_loaded = sem("p_loaded")
        p_hi_set = sem("p_hi_set")
        p_lo_set = sem("p_lo_set")
        h_hi_set = sem("h_hi_set")
        h_lo_set = sem("h_lo_set")
        ple_chunk = sem("ple_chunk")
        ple_done = sem("ple_done")
        g_chunk = sem("g_chunk")
        g_sig = sem("g_sig")
        g_added = sem("g_added")

        def two_chunks(b, waits):
            return [(slice(c * CH, c * CH + CH), bank(b + c), waits if c == 0 else []) for c in range(2)]

        def out1_pe(pe):
            pe.wait_ge(y4_loaded, 16 * 32)
            with pe.Fori(0, KT // 2) as i:
                for m in range(2):
                    n = i * 4 + (U_OUT + 2 * m)
                    free = [(o_added, i * 2 + (m - 1))] if m else [(o_added, i * 2)]
                    project(pe, n, 0, y_hi, y_lo, two_chunks(2 * m, free), o_chunk, stop=False)
                    project(pe, n + 1, 1, y_hi, y_lo, two_chunks(2 * m, []), o_chunk, first=KT, start=False)

        def out1_act(act):
            act.wait_ge(fox.spilled, 32 * PAIRS)
            act.wait_ge(fox.valued, PAIRS * fox.NV)
            for k in range(2 * KT):
                for part, dst in ((0, y_hi), (1, y_lo)):
                    act.dma_start(dst[:, k, :].bitcast(F32), y_dram[part, k, :, 0:T]).then_inc(y4_loaded, 16)
            with act.Fori(0, KT // 2) as i:
                for m in range(2):
                    act.wait_ge(o_added, i * 2)
                    act.dma_start(x_in[:, m, :], a["x_t"][:, ds(i * 2 + m, 1), :].rearrange("p a t -> p (a t)")
                                  ).then_inc(x4_loaded, 16)

        def out1_dve(dve):
            with dve.Fori(0, KT // 2) as i:
                for m in range(2):
                    dve.wait_ge(x4_loaded, i * 32 + 32)
                    dve.wait_ge(o_chunk, i * 4 + (2 * m + 2))
                    dve.wait_ge(w_used, i * 4 + (U_OUT + 2 * m + 2))
                    dve.tensor_tensor(h_sb[:, ds(i * 2 + m, 1), :].rearrange("p a t -> p (a t)"),
                                      bank(2 * m, 2), x_in[:, m, :], ALU.add).then_inc(o_added, 1)

        def ple_pe(pe):
            pe.wait_ge(p_lo_set, 1)
            for half in range(2):
                for m in range(4):
                    j = 4 * half + m
                    free = [(ple_done, j - 1)] if j >= 2 else [(o_added, KT)]
                    project(pe, U_PLE + half, half, p_hi, p_lo, two_chunks(2 * (m % 2), free), ple_chunk,
                            tiles=(2 * m, 2 * m + 1), last=m == 3)

        def gate_pe(pe):
            pe.wait_ge(h_lo_set, KT)
            pe.wait_ge(ple_done, KT)
            with pe.Fori(0, KT // 2) as i:
                for m in range(2):
                    free = [(g_sig, i * 2 + (m - 1))] if m else [(g_sig, i * 2)]
                    project(pe, i * 2 + (U_GATE + m), m, r_hi, r_lo, two_chunks(2 * m, free), g_chunk)

        def ple_act(act):
            act.wait_ge(o_added, KT)
            act.dma_start(x_in[:], a["p_t"]).then_inc(p_loaded, 16)
            act.wait_ge(p_loaded, 16)
            nc.scalar.copy(p_hi[:], x_in[:]).then_inc(p_hi_set, 1)
            for k in range(KT):
                nc.scalar.copy(r_hi[:, k, :], h_sb[:, k, :]).then_inc(h_hi_set, 1)
            for m in range(KT):
                act.wait_ge(ple_chunk, 2 * (m + 1) - (m + 1) // 4)
                act.wait_ge(w_used, U_PLE + (m + 1) // 4)
                nc.scalar.copy(ple[:, m, :], bank(2 * (m % 2), 2)).then_inc(ple_done, 1)
            with act.Fori(0, KT // 2) as i:
                for m in range(2):
                    act.wait_ge(g_added, i * 2)
                    act.wait_ge(g_chunk, i * 2 + (m + 1))
                    act.wait_ge(w_used, i * 2 + (U_GATE + m + 1))
                    nc.scalar.activation(sig[:, m, :], bank(2 * m, 2), ACT.Sigmoid).then_inc(g_sig, 1)

        def ple_dve(dve):
            dve.wait_ge(p_hi_set, 1)
            dve.tensor_tensor(p_lo[:], x_in[:], p_hi[:].bitcast(F32), ALU.subtract).then_inc(p_lo_set, 1)
            for k in range(KT):
                dve.wait_ge(h_hi_set, k + 1)
                dve.tensor_tensor(r_lo[:, k, :], h_sb[:, k, :], r_hi[:, k, :].bitcast(F32),
                                  ALU.subtract).then_inc(h_lo_set, 1)
            dve.wait_ge(ple_done, KT)
            with dve.Fori(0, KT // 2) as i:
                for m in range(2):
                    dve.wait_ge(g_sig, i * 2 + (m + 1))
                    row = lambda t: t[:, ds(i * 2 + m, 1), :].rearrange("p a t -> p (a t)")
                    dve.tensor_tensor(sig[:, m, :], sig[:, m, :], row(ple), ALU.mult)
                    dve.drain()
                    dve.tensor_tensor(row(h_sb), row(h_sb), sig[:, m, :], ALU.add).then_inc(g_added, 1)

        ph4c = ctx.enter_context(ExitStack())
        sq4 = sb("sq4", [P, 2, T], at=ph4c)
        rstd4 = sb("rstd4", [P, T], at=ph4c)
        ph4c.close()
        n4_sq = sem("n4_sq")
        n4_sum = sem("n4_sum")
        n4_sd = sem("n4_sd")
        n4_h = sem("n4_h")
        h_stored = sem("h_stored")
        ctx_loaded = sem("ctx_loaded")

        def norm4_act(act):
            act.wait_ge(g_added, KT)
            act.dma_start(ctx_in[:], a["ctx_t"]).then_inc(ctx_loaded, 16)
            for k in range(KT):
                if k >= 2:
                    act.wait_ge(n4_sum, k - 1)
                nc.scalar.activation(sq4[:, k % 2, :], h_sb[:, k, :], ACT.Square).then_inc(n4_sq, 1)
            act.wait_ge(n4_sum, KT)
            nc.scalar.activation(rstd4[:], bank(0, 2), ACT.Sqrt, bias=small[:, 1:2]).then_inc(n4_sd, 1)
            for k in range(KT):
                act.wait_ge(n4_h, k + 1)
                act.dma_start(h_dram[k, :, 0:T], h_sb[:, k, :]).then_inc(h_stored, 16)
            act.wait_ge(ctx_loaded, 16)
            act.dma_start(h_dram[:, :, T:TC].rearrange("k p t -> p k t"), ctx_in[:]).then_inc(h_stored, 16)

        def norm4_pe(pe):
            for k in range(KT):
                pe.wait_ge(n4_sq, k + 1)
                for c in range(2):
                    mm = pe.matmul(bank(c), ones_mean[:], sq4[:, k % 2, c * CH:(c + 1) * CH],
                                   start=k == 0, stop=k == KT - 1)
                mm.then_inc(n4_sum, 1)

        def norm4_dve(dve):
            dve.wait_ge(n4_sd, 1)
            dve.reciprocal(rstd4[:], rstd4[:])
            dve.drain()
            for k in range(KT):
                dve.scalar_tensor_tensor(h_sb[:, k, :], h_sb[:, k, :], vecs[:, V_FINAL + k:V_FINAL + k + 1],
                                         rstd4[:], ALU.mult, ALU.mult).then_inc(n4_h, 1)

        ada_set = sem("ada_set")

        def ada_dve(dve):
            dve.tensor_tensor(adv[:], ada[:], vecs[:, V_BADA:V_BADA + ADA_UNITS].unsqueeze(2)
                              .broadcast_to([P, ADA_UNITS, 2]), ALU.add)
            dve.drain()
            for l in range(2):
                sc = adv[:, 24 * l + 8:24 * l + 16, :]
                dve.tensor_scalar(sc, sc, 1.0, None, ALU.add)
            dve.drain().then_inc(ada_set, 1)

        class Layer:

            def __init__(self, l, name, n_out, cols, first=None):
                self.l, self.name, self.n_out, self.cols = l, name, n_out, cols
                self.chunks = [(0, CH), (CH, CH), (T, C)][:3 if cols == TC else 2]
                area = ctx.enter_context(ExitStack())
                self.yh = sb(f"{name}_out_yh", [P, KT, cols], F32R, area)
                self.yl = sb(f"{name}_out_yl", [P, KT, cols], F32R, area)
                self.h = sb(f"{name}_h", [P, KT, cols], at=area)
                self.res = sb(f"{name}_res", [P, 2, cols], at=area)
                self.gate = sb(f"{name}_gate", [P, 2, 2], at=area)
                self.tmp = sb(f"{name}_tmp", [P, 2, cols], at=area)
                area.close()
                area = ctx.enter_context(ExitStack())
                self.sq = sb(f"{name}_sq", [P, 2, cols], at=area)
                self.mean = sb(f"{name}_mean", [P, cols], at=area)
                self.rstd = sb(f"{name}_rstd", [P, cols], at=area)
                assert 4 * 4 * cols <= 2 * 4 * KT * cols
                area.close()
                self.base = l * KT
                if first is None:
                    self.y_loaded = sem("layer_y_loaded")
                    self.res_loaded = sem("layer_res_loaded")
                    self.chunk = sem("layer_chunk")
                    self.gated = sem("layer_gated")
                    self.added = sem("layer_added")
                    self.mean_sum = sem("layer_mean_sum")
                    self.centred = sem("layer_centred")
                    self.sq_set = sem("layer_sq_set")
                    self.sq_sum = sem("layer_sq_sum")
                    self.sd = sem("layer_sd")
                    self.normed = sem("layer_normed")
                else:
                    self.y_loaded = first.y_loaded
                    self.res_loaded = first.res_loaded
                    self.chunk = first.chunk
                    self.gated = first.gated
                    self.added = first.added
                    self.mean_sum = first.mean_sum
                    self.centred = first.centred
                    self.sq_set = first.sq_set
                    self.sq_sum = first.sq_sum
                    self.sd = first.sd
                    self.normed = first.normed

            def span(self, b, waits=()):
                return [(slice(t, t + n), ps[:, b * CH + t:b * CH + t + n], waits if t == 0 else [])
                        for t, n in self.chunks]

            def flat(self, b):
                return ps[:, b * CH:b * CH + self.cols]

            def pe(self, pe, mixer):
                pe.wait_ge(self.y_loaded, 16 * 2 * (self.base + KT))
                n = len(self.chunks)
                with pe.Fori(0, KT // 2) as i:
                    for m in range(2):
                        project(pe, i * 2 + (self.n_out + m), m, self.yh, self.yl,
                                self.span(3 * m, [(self.gated, i * 2 + (self.base + max(m - 1, 0)))]), self.chunk)
                for k in range(KT):
                    if k == 0:
                        pe.wait_ge(self.added, self.base + KT)
                    for t, w in self.chunks:
                        mm = pe.matmul(ps[:, t:t + w], ones_mean[:], self.h[:, k, t:t + w],
                                       start=k == 0, stop=k == KT - 1)
                mm.then_inc(self.mean_sum, 1)
                for k in range(KT):
                    pe.wait_ge(self.sq_set, self.base + k + 1)
                    for t, w in self.chunks:
                        mm = pe.matmul(ps[:, 3 * CH + t:3 * CH + t + w], ones_mean[:], self.sq[:, k % 2, t:t + w],
                                       start=k == 0, stop=k == KT - 1)
                    mm.then_inc(self.sq_sum, 1)

            def act(self, act, mixer):
                act.wait_ge(mixer.spilled, 32 * PAIRS)
                act.wait_ge(mixer.valued, PAIRS * mixer.NV)
                for k in range(KT):
                    for part, dst in ((0, self.yh), (1, self.yl)):
                        act.dma_start(dst[:, k, :].bitcast(F32), y_dram[part, k, :, 0:self.cols]
                                      ).then_inc(self.y_loaded, 16)
                with act.Fori(0, KT // 2) as i:
                    for m in range(2):
                        act.wait_ge(self.added, i * 2 + self.base)
                        act.dma_start(self.res[:, m, :], h_dram[ds(i * 2 + m, 1), :, 0:self.cols]
                                      .rearrange("a p t -> (a p) t")).then_inc(self.res_loaded, 16)
                for k in range(KT):
                    act.wait_ge(self.centred, self.base + k + 1)
                    if k >= 2:
                        act.wait_ge(self.sq_sum, self.base + k - 1)
                    nc.scalar.activation(self.sq[:, k % 2, :], self.h[:, k, :], ACT.Square).then_inc(self.sq_set, 1)
                act.wait_ge(self.sq_sum, self.base + KT)
                nc.scalar.activation(self.rstd[:], self.flat(3), ACT.Sqrt, bias=small[:, 2:3]).then_inc(self.sd, 1)

            def dve(self, dve):
                l = self.l
                with dve.Fori(0, KT // 2) as i:
                    for m in range(2):
                        dve.tensor_copy(self.gate[:, m, :],
                                        adv[:, ds(i * 2 + (24 * l + 16 + m), 1), :].rearrange("p a i -> p (a i)"))
                        dve.drain()
                        dve.wait_ge(self.chunk, (i * 2 + (m + 1)) * (len(self.chunks) - 1) + 2 * self.base)
                        dve.wait_ge(w_used, i * 2 + (self.n_out + m + 1))
                        ins = dve.tensor_scalar(self.tmp[:, m, 0:T], ps[:, 3 * m * CH:3 * m * CH + T],
                                                self.gate[:, m, 0:1], None, ALU.mult)
                        if self.cols > T:
                            ins = dve.tensor_scalar(self.tmp[:, m, T:], ps[:, 3 * m * CH + T:3 * m * CH + TC],
                                                    self.gate[:, m, 1:2], None, ALU.mult)
                        ins.then_inc(self.gated, 1)
                        dve.drain()
                        dve.wait_ge(self.res_loaded, i * 32 + (16 * self.base + 32))
                        dve.scalar_tensor_tensor(self.h[:, ds(i * 2 + m, 1), :].rearrange("p a t -> p (a t)"),
                                                 self.res[:, m, :], ALPHA, self.tmp[:, m, :], ALU.mult, ALU.add
                                                 ).then_inc(self.added, 1)
                dve.wait_ge(self.mean_sum, l + 1)
                dve.tensor_copy(self.mean[:], self.flat(0))
                dve.drain()
                for k in range(KT):
                    dve.tensor_tensor(self.h[:, k, :], self.h[:, k, :], self.mean[:], ALU.subtract
                                      ).then_inc(self.centred, 1)
                dve.wait_ge(self.sd, l + 1)
                dve.reciprocal(self.rstd[:], self.rstd[:])
                dve.drain()
                for k in range(KT):
                    g = vecs[:, V_LNG + 8 * l + k:V_LNG + 8 * l + k + 1]
                    b = vecs[:, V_LNB + 8 * l + k:V_LNB + 8 * l + k + 1]
                    dve.scalar_tensor_tensor(self.h[:, k, :], self.h[:, k, :], g, self.rstd[:], ALU.mult, ALU.mult)
                    dve.drain()
                    dve.tensor_scalar(self.h[:, k, :], self.h[:, k, :], b, None, ALU.add).then_inc(self.normed, 1)

        class Modulated:

            def __init__(self, l, name, h_of, first=None):
                self.l, self.h_of = l, h_of
                self.area = ctx.enter_context(ExitStack())
                self.hi = sb(f"{name}_u_hi", [P, KT, TC], F32R, self.area)
                self.lo = sb(f"{name}_u_lo", [P, KT, TC], F32R, self.area)
                self.base = l * KT
                if first is None:
                    self.made = sem("u_made")
                    self.hi_set = sem("u_hi_set")
                    self.lo_set = sem("u_lo_set")
                else:
                    self.made, self.hi_set, self.lo_set = first.made, first.hi_set, first.lo_set

            def act(self, act):
                for k in range(KT):
                    act.wait_ge(self.made, self.base + k + 1)
                    nc.scalar.copy(self.hi[:, k, :], self.u[:, k % 2, :]).then_inc(self.hi_set, 1)

            def dve(self, dve):
                def low(k):
                    dve.wait_ge(self.hi_set, self.base + k + 1)
                    dve.tensor_tensor(self.lo[:, k, :], self.u[:, k % 2, :], self.hi[:, k, :].bitcast(F32),
                                      ALU.subtract).then_inc(self.lo_set, 1)
                for k in range(KT):
                    if k >= 2:
                        dve.drain()
                    for i, (t, n) in enumerate(((0, T), (T, C))):
                        ins = dve.tensor_scalar(self.u[:, k % 2, t:t + n], self.h_of(k, i),
                                                adv[:, 24 * self.l + 8 + k, i:i + 1], adv[:, 24 * self.l + k, i:i + 1],
                                                ALU.mult, ALU.add)
                    ins.then_inc(self.made, 1)
                    if k:
                        low(k - 1)
                low(KT - 1)

        mod_a = Modulated(0, "wa", lambda k, i: ctx_in[:, k, :] if i else h_sb[:, k, :])
        with ExitStack() as above:
            mod_a.u = sb("wa_u", [P, 2, TC], at=above)

        def window_block(b):
            if b >= 8:
                lo, hi = 0, 0
            else:
                lo, hi = max(b - 1, 0), min(b + 2, 8)
            n = (hi - lo) * P
            runs = [(CH - n, lo * P, n)] if n else []
            runs.append((CH, T, C))
            chunks = [(c * P, P, lo + c) for c in range(hi - lo)] + [(n + c * P, P, 8 + c) for c in range(2)]
            return {"b": b, "width": n + C + 1, "first": CH - n, "runs": runs, "chunks": chunks, "lat": n}

        ph6 = ctx.enter_context(ExitStack())
        wa = Attention("wa", [window_block(b) for b in range(10)], [[0, 1, 2, 3], [4, 5, 6, 7], [8, 9]],
                       3 * P + C + 1, TC, TC, ph6)
        wa_k2a = [sb(f"wa_k2a{i}", [P, TC], F32R, ph6) for i in range(2)]
        wa_k2b = [sb(f"wa_k2b{i}", [P, TC], F32R, ph6) for i in range(2)]
        wa_v = sb("wa_v", [P, 10, P], at=ph6)
        rope = sb("rope", [P, 2, T], at=ph6)
        nsink = sb("nsink", [P, 16], at=ph6)
        head_sink = sb("head_sink", [P, 2], at=ph6)
        ph6.close()
        wa_shuf = wa.l[:].rearrange("p s w -> p (s w)")[:, 0:T]
        a_loaded = sem("a_loaded")
        a_set = sem("a_set")
        a_copied = sem("a_copied")
        a_turned = sem("a_turned")
        a_hi = sem("a_hi")
        a_lo = sem("a_lo")
        a_vt = sem("a_vt")
        a_vc = sem("a_vc")
        a_g = sem("a_g")

        def wa_pe(pe):
            pe.wait_ge(mod_a.lo_set, KT)
            with pe.Fori(0, 2) as j:
                def unit(i, b, waits):
                    project(pe, j * 10 + (U_A + i), i % 2, mod_a.hi, mod_a.lo,
                            layer_a.span(b, waits), wa.chunk)

                unit(0, 0, [(wa.shifted, j * (4 * wa.NA))])
                unit(1, 3, wa.all_copied(j * 4))
                pe.wait_ge(a_copied, j * 6 + 2)
                for t in range(10):
                    mm = pe.transpose(ps[:, t * P:(t + 1) * P], wa.y[:, t * P:(t + 1) * P], ident)
                mm.then_inc(a_vt, 1)
                for g in range(4):
                    it = j * 4 + g
                    unit(2 + 2 * g, 0, [(wa.shifted, it * wa.NA), (a_vc, j + 1)])
                    unit(3 + 2 * g, 3, wa.all_copied(it))
                    wa.pe(pe, it, [wa_k2a[g // 2]] * 2, [wa_k2b[g // 2]] * 2, [(wa_v, rows_of(g // 2))] * 2,
                          {("S", 0): [(a_lo, j * 5 + (g + 2))],
                           ("S", 1): [(a_g, it + 1)]})

        def wa_act(act):
            act.wait_ge(mod_a.lo_set, KT)
            act.wait_ge(h_stored, 16 * (KT + 1))
            act.dma_start(rope[:], a["rope"]).then_inc(a_loaded, 16)
            act.dma_start(nsink[:], a["a_sink"].broadcast_to([P, 16])).then_inc(a_loaded, 16)
            with act.Fori(0, 2) as j:
                def copied(i, b, scale=1.0):
                    act.wait_ge(wa.chunk, j * 20 + 2 * (i + 1))
                    act.wait_ge(w_used, j * 10 + (U_A + i + 1))
                    return nc.scalar.activation(wa.y[:], layer_a.flat(b), ACT.Copy, scale=scale
                                                ).then_inc(a_copied, 1)

                copied(0, 0)
                act.wait_ge(a_turned, j * 5 + 1)
                for kk in range(2):
                    for half in range(2):
                        ins = nc.scalar.copy(wa_k2a[kk][rows_of(half), :], wa.y[rows_of(kk), :])
                ins.then_inc(a_hi, 1)
                act.wait_ge(a_lo, j * 5 + 1)
                copied(1, 3)
                act.wait_ge(a_vt, j + 1)
                vt = ps[:, 0:TC].rearrange("p (j t) -> p j t", t=P)
                nc.scalar.copy(wa_v[:], vt).then_inc(a_vc, 1)
                for g in range(4):
                    it = j * 4 + g
                    copied(2 + 2 * g, 0, HD ** -0.5)
                    act.wait_ge(a_turned, j * 5 + (g + 2))
                    for hd in range(2):
                        ins = nc.scalar.copy(wa.q2[hd][rows_of(hd), :], wa.y[rows_of(hd), :])
                    ins.then_inc(a_hi, 1)
                    act.wait_ge(wa.chunk, j * 20 + 2 * (4 + 2 * g))
                    act.wait_ge(w_used, j * 10 + (U_A + 4 + 2 * g))
                    nc.scalar.activation(wa.silu[:], layer_a.flat(3), ACT.Silu).then_inc(a_g, 1)
                    wa.act(act, it)
                    wa.finish_act(act, it, it, TC)

        def wa_dve(dve):
            dve.wait_ge(h_stored, 16 * (KT + 1))
            dve.wait_ge(a_loaded, 32)
            dve.tensor_scalar(nsink[:], nsink[:], -1.0, None, ALU.mult)
            dve.drain().then_inc(a_set, 1)
            with dve.Fori(0, 2) as j:
                def rotate(i, n, it):
                    dve.drain()
                    dve.wait_ge(wa.turned, it * wa.NG)
                    dve.wait_ge(a_copied, j * 6 + i)
                    dve.tensor_copy(head_sink[:], nsink[:, ds(n, 2)])
                    dve.stream_shuffle(wa_shuf, wa.y[:, 0:T], [(x + 16) % 32 for x in range(32)])
                    dve.drain()
                    dve.tensor_tensor(wa.y[:, 0:T], wa.y[:, 0:T], rope[:, 0, :], ALU.mult)
                    dve.tensor_tensor(wa_shuf, wa_shuf, rope[:, 1, :], ALU.mult)
                    dve.drain()
                    dve.tensor_tensor(wa.y[:, 0:T], wa.y[:, 0:T], wa_shuf, ALU.add).then_inc(a_turned, 1)

                rotate(1, j * 8, j * 4)
                dve.wait_ge(a_hi, j * 5 + 1)
                for kk in range(2):
                    r = rows_of(kk)
                    for half in range(2):
                        ins = dve.tensor_tensor(wa_k2b[kk][rows_of(half), :], wa.y[r, :],
                                                wa_k2a[kk][r, :].bitcast(F32), ALU.subtract)
                ins.then_inc(a_lo, 1)
                for g in range(4):
                    it = j * 4 + g
                    rotate(3 + g, it * 2, it)
                    dve.wait_ge(a_hi, j * 5 + (g + 2))
                    for hd in range(2):
                        r = rows_of(hd)
                        ins = dve.tensor_tensor(wa.q2[hd][rows_of(1 - hd), :], wa.y[r, :],
                                                wa.q2[hd][r, :].bitcast(F32), ALU.subtract)
                    ins.then_inc(a_lo, 1)
                    dve.drain()

                    def masks(u):
                        blk = wa.blocks[u // 2]
                        b, n, w = blk["b"], blk["lat"], blk["width"]
                        dve.tensor_copy(wa.l[:, u % 3, w - 1:w], head_sink[:, u % 2:u % 2 + 1])
                        win = consts[:, K_WIN:K_WIN + 3 * P + C]
                        if b == 7:
                            return [(0, n, win[:, 0:n]), (n, C, win[:, 3 * P:])]
                        return [(0, n + C, win[:, 3 * P - n:])]

                    wa.dve(dve, it, lambda u, nm: dve.tensor_copy(nm, head_sink[:, u % 2:u % 2 + 1]), masks)
                    wa.finish_dve(dve, it)

        mod_a.area.close()
        layer_a = Layer(0, "la", U_A_OUT, TC)
        mod_b = Modulated(1, "nb", lambda k, i: layer_a.h[:, k, T:TC] if i else layer_a.h[:, k, 0:T], mod_a)
        with ExitStack() as above:
            sb("layer_a_h_place", [P, KT, TC], at=above)
            mod_b.u = sb("nb_u", [P, 2, TC], at=above)

        def near_block(b):
            rs = min(max(2 * b - 4, 0), 8)
            n = (9 if 2 <= b <= 5 else 8) * GRID_W
            chunks = [(c * P, P, 8 + c) for c in range(2)]
            chunks += [(C + c * P, min(P, n - c * P), rs // 2 + c) for c in range((n + P - 1) // P)]
            return {"b": b, "width": C + n, "first": 0, "chunks": chunks, "first_row": rs - 2 * b,
                    "runs": [(0, T, C), (C, rs * GRID_W, CH - C), (CH, rs * GRID_W + CH - C, n + C - CH)]}

        ph7 = ctx.enter_context(ExitStack())
        nb = Attention("nb", [near_block(b) for b in range(8)], [[0, 1, 2, 3], [4, 5, 6, 7]],
                       C + 9 * GRID_W, T, T, ph7)
        nb_k2a = [sb(f"nb_k2a{i}", [P, TC], F32R, ph7) for i in range(2)]
        nb_k2b = [sb(f"nb_k2b{i}", [P, TC], F32R, ph7) for i in range(2)]
        nb_v = sb("nb_v", [P, 10, P], at=ph7)
        nb_bias = sb("nb_bias", [P, 2, 14 * GRID_W], at=ph7)
        nb_mid = sb("nb_mid", [P, 2, C + 9 * GRID_W], at=ph7)
        ph7.close()
        mod_b.area.close()
        nb_vt = nb.l[:].rearrange("p s w -> p (s w)")[:, 0:TC]
        b_loaded = sem("b_loaded")
        b_hi = sem("b_hi")
        b_lo = sem("b_lo")
        b_v = sem("b_v")
        b_vt = sem("b_vt")
        b_vc = sem("b_vc")
        b_g = sem("b_g")
        layer_b = Layer(1, "lb", U_B_OUT, T, layer_a)

        def nb_pe(pe):
            pe.wait_ge(mod_b.lo_set, 2 * KT)
            with pe.Fori(0, PAIRS) as it:
                n = it * 4 + U_B
                project(pe, n, 0, mod_b.hi, mod_b.lo, two_chunks(6, [(nb.left, it * nb.NB)]), nb.chunk)
                project(pe, n + 1, 1, mod_b.hi, mod_b.lo, layer_a.span(3, nb.all_copied(it)), nb.chunk)
                project(pe, n + 2, 0, mod_b.hi, mod_b.lo, layer_a.span(0, [(nb.shifted, it * nb.NA)]), nb.chunk)
                project(pe, n + 3, 1, mod_b.hi, mod_b.lo, two_chunks(6, [(b_lo, it * 2 + 1)]), nb.chunk)
                pe.wait_ge(b_lo, it * 2 + 2)
                pe.wait_ge(b_v, it + 1)
                for t in range(10):
                    mm = pe.transpose(ps[:, 3 * CH + t * P:3 * CH + (t + 1) * P], nb_vt[:, t * P:(t + 1) * P], ident)
                mm.then_inc(b_vt, 1)
                nb.pe(pe, it, nb_k2a, nb_k2b, [(nb_v, rows_of(hd)) for hd in range(2)],
                      {("S", 1): [(b_vc, it + 1)],
                       ("V", 0): [(b_g, it + 1)]})

        def nb_act(act):
            act.wait_ge(mod_b.lo_set, 2 * KT)
            act.wait_ge(b_stored, 16 * KT)
            with act.Fori(0, PAIRS) as it:
                act.wait_ge(nb.shifted, it * nb.NA)
                for hd in range(2):
                    act.dma_start(nb_bias[:, hd, :], a["rel_bias"][ds(it * 2 + hd, 1)].rearrange("a p n -> (a p) n")
                                  ).then_inc(b_loaded, 16)
                act.wait_ge(nb.chunk, it * 6 + 1)
                act.wait_ge(w_used, it * 4 + (U_B + 1))
                for hd in range(2):
                    ins = nc.scalar.activation(nb.q2[hd][0:HD, :], bank(6, 2)[rows_of(hd)], ACT.Copy, scale=HD ** -0.5)
                ins.then_inc(b_hi, 1)
                act.wait_ge(nb.chunk, it * 6 + 3)
                act.wait_ge(w_used, it * 4 + (U_B + 2))
                for hd in range(2):
                    for half in range(2):
                        ins = nc.scalar.copy(nb_k2a[hd][rows_of(half), :], layer_a.flat(3)[rows_of(hd)])
                ins.then_inc(b_hi, 1)
                act.wait_ge(nb.chunk, it * 6 + 5)
                act.wait_ge(w_used, it * 4 + (U_B + 3))
                nc.scalar.copy(nb_vt, layer_a.flat(0)).then_inc(b_v, 1)
                act.wait_ge(nb.chunk, it * 6 + 6)
                act.wait_ge(w_used, it * 4 + (U_B + 4))
                nc.scalar.activation(nb.silu[:], bank(6, 2), ACT.Silu).then_inc(b_g, 1)
                act.wait_ge(b_vt, it + 1)
                nc.scalar.copy(nb_v[:].rearrange("p j t -> p (j t)"), layer_a.flat(3)).then_inc(b_vc, 1)
                nb.act(act, it)
                nb.finish_act(act, it, it, T)

        def nb_dve(dve):
            dve.wait_ge(b_stored, 16 * KT)
            for hd in range(2):
                dve.memset(nb_mid[:, hd, 0:C], 0.0)
            dve.drain()
            with dve.Fori(0, PAIRS) as it:
                dve.wait_ge(b_loaded, it * 32 + 32)
                for hd in range(2):
                    rows = nb_bias[:, hd, :].rearrange("p (r c) -> p r c", c=GRID_W)
                    dve.tensor_tensor(rows, rows, consts[:, K_COL:K_COL + GRID_W].unsqueeze(1)
                                      .broadcast_to([P, 14, GRID_W]), ALU.add)
                dve.drain()
                for hd in range(2):
                    rows = nb_bias[:, hd, :].rearrange("p (r c) -> p r c", c=GRID_W)[:, 2:11, :]
                    dve.tensor_tensor(nb_mid[:, hd, C:].rearrange("p (r c) -> p r c", c=GRID_W), rows,
                                      consts[:, K_ROW:K_ROW + 9].unsqueeze(2).broadcast_to([P, 9, GRID_W]), ALU.add)
                dve.wait_ge(b_hi, it * 2 + 1)
                for hd in range(2):
                    ins = dve.scalar_tensor_tensor(nb.q2[hd][HD:P, :], bank(6, 2)[rows_of(hd)], HD ** -0.5,
                                                   nb.q2[hd][0:HD, :].bitcast(F32), ALU.mult, ALU.subtract)
                ins.then_inc(b_lo, 1)
                dve.wait_ge(b_hi, it * 2 + 2)
                for hd in range(2):
                    for half in range(2):
                        ins = dve.tensor_tensor(nb_k2b[hd][rows_of(half), :], layer_a.flat(3)[rows_of(hd)],
                                                nb_k2a[hd][0:HD, :].bitcast(F32), ALU.subtract)
                ins.then_inc(b_lo, 1)
                dve.drain()
                dve.wait_ge(b_vt, it + 1)

                def masks(u):
                    blk, hd = nb.blocks[u // 2], u % 2
                    if 2 <= blk["b"] <= 5:
                        return [(0, blk["width"], nb_mid[:, hd, :])]
                    c0 = (blk["first_row"] + 6) * GRID_W
                    return [(0, C, nb_mid[:, hd, 0:C]), (C, CH, nb_bias[:, hd, c0:c0 + CH])]

                nb.dve(dve, it, lambda u, nm: dve.memset(nm, 3e38), masks)
                nb.finish_dve(dve, it)

        b_stored = sem("b_stored")
        out_stored = sem("out_stored")

        def store_a(act):
            for k in range(KT):
                act.wait_ge(layer_a.normed, k + 1)
                act.dma_start(h_dram[k, :, 0:T], layer_a.h[:, k, 0:T]).then_inc(b_stored, 16)

        def store_b(act):
            for k in range(KT):
                act.wait_ge(layer_b.normed, KT + k + 1)
                act.dma_start(a["out"][k], layer_b.h[:, k, :]).then_inc(out_stored, 16)
            act.wait_ge(out_stored, 16 * KT)

        block = ctx.enter_context(nc.Block())

        @block.sync
        def _(sp):
            stream_loads(sp)
            sp.dma_start(vecs[:], a["vecs"]).then_inc(loaded, 16)
            sp.dma_start(consts[:], a["consts"]).then_inc(loaded, 16)
            for k in range(KT):
                sp.dma_start(x_sb[:, k, :], a["x_t"][:, k, :]).then_inc(x_loaded, 16)
            stream_loads_rest(sp)

        @block.gpsimd
        def _(pool):
            stream_splits(pool)

        @block.scalar
        def _(act):
            norm1_act(act)
            hgrn_act(act)
            fz_act_part(act)
            fox_act(act)
            out1_act(act)
            ple_act(act)
            norm4_act(act)
            mod_a.act(act)
            wa_act(act)
            layer_a.act(act, wa)
            store_a(act)
            mod_b.act(act)
            nb_act(act)
            layer_b.act(act, nb)
            store_b(act)

        @block.tensor
        def _(pe):
            norm1_pe(pe)
            hgrn_pe(pe)
            fz_pe(pe)
            fox_pe(pe)
            out1_pe(pe)
            ple_pe(pe)
            gate_pe(pe)
            norm4_pe(pe)
            wa_pe(pe)
            layer_a.pe(pe, wa)
            nb_pe(pe)
            layer_b.pe(pe, nb)

        @block.vector
        def _(dve):
            norm1_dve(dve)
            hgrn_dve(dve)
            fz_dve(dve)
            fox_dve(dve)
            out1_dve(dve)
            ple_dve(dve)
            ada_dve(dve)
            norm4_dve(dve)
            dve.drain()
            dve.wait_ge(ctx_loaded, 16)
            mod_a.dve(dve)
            wa_dve(dve)
            layer_a.dve(dve)
            dve.drain()
            mod_b.dve(dve)
            nb_dve(dve)
            layer_b.dve(dve)


def _tiles(v):
    return v.reshape(-1, P).T


def _unit(w, c0, width=P):
    cols = w[:, c0:c0 + width]
    if cols.shape[1] < width:
        cols = np.concatenate([cols, np.zeros((w.shape[0], width - cols.shape[1]), w.dtype)], 1)
    return cols.reshape(-1, P, width).transpose(1, 0, 2).reshape(P, -1)


def lay_out(x, p, norm_w, w_in, fox_fb, hgrn_gn, hgrn_lb_logits, w_out, w_ple, w_ple_gate, final_norm_w,
            c_2, ctx_2, c_ctx_2, w_ada_2, b_ada_2, ln_g_2, ln_b_2, a_w_in_2, a_w_out_2, a_sink_2,
            b_w_in_2, b_w_out_2, b_rel_bias_2):
    w1, wo, wp, wg = w_in[0], w_out[0], w_ple[0], w_ple_gate[0]
    wa, wao, wb, wbo = a_w_in_2[0], a_w_out_2[0], b_w_in_2[0], b_w_out_2[0]
    units = []
    for h in range(HG):
        units += [_unit(w1, j * D + h * P) for j in (1, 0, 2, 3)]
    units += [_unit(w1, 8 * D)] * 2
    for h in range(PAIRS):
        units += [_unit(w1, (4 + j) * D + h * P) for j in range(4)]
    for m in range(KT):
        units += [_unit(wo[:D], m * P), _unit(wo[D:], m * P)]
    for half in range(2):
        units.append(np.concatenate([_unit(wp, (4 * half + m) * P) for m in range(4)], 1))
    units += [_unit(wg, m * P) for m in range(KT)]
    for j in range(2):
        units += [_unit(wa, D + j * P), _unit(wa, D + 256 + j * P)]
        for g in range(4):
            units += [_unit(wa, (4 * j + g) * P), _unit(wa, D + 512 + (4 * j + g) * P)]
    units += [_unit(wao, m * P) for m in range(KT)]
    for h in range(PAIRS):
        units += [_unit(wb, j * D + h * P) for j in range(4)]
    units += [_unit(wbo, m * P) for m in range(KT)]
    assert len(units) == UNITS

    s = np.arange(P)
    level = np.zeros((P, 8, P), np.float32)
    for lv in range(LEVELS):
        H = 1 << lv
        level[:, lv] = ((s[:, None] // (2 * H) == s[None] // (2 * H))
                        & (s[:, None] % (2 * H) < H) & (s[None] % (2 * H) >= H))
    level[:, 7] = np.eye(P)
    consts = np.zeros((P, K_END), np.float32)
    consts[:, K_ID:K_ID + P] = np.eye(P)
    masks = np.zeros((P, 2, T), np.float32)
    masks[:, 0] = level.reshape(P, -1)
    masks[:, 1] = (np.arange(T) % HGRN_CHUNK != 0)
    consts[:, K_TRI:K_TRI + P] = np.where(s[None] > s[:, None], BIG, 0.0)

    win = consts[:, K_WIN:K_WIN + 640]
    win[:, 0:P] = np.where(s[None] < s[:, None], BIG, 0.0)
    win[:, 2 * P:3 * P] = np.where(s[None] > s[:, None], BIG, 0.0)
    qc, kc, second = s % GRID_W, np.arange(GRID_W), s // GRID_W
    first = np.clip(qc - 8, 0, GRID_W - 16)
    consts[:, K_COL:K_COL + GRID_W] = np.where((kc[None] >= first[:, None]) & (kc[None] < first[:, None] + 16), 0.0, BIG)
    consts[:, K_ROW + 8] = np.where(second == 0, BIG, 0.0)
    consts[:, K_ROW] = np.where(second == 1, BIG, 0.0)
    rows = np.arange(-6, 8)[None, :, None] - second[:, None, None] + 7
    rel_bias = b_rel_bias_2[0][:, rows, np.clip(kc[None, None] - qc[:, None, None] + 15, 0, 30)].reshape(16, P, -1)

    t = np.arange(T)
    inv = (np.float32(10000.0) ** (-np.arange(16, dtype=np.float32) / np.float32(16))).astype(np.float32)
    angles = [(pos.astype(np.float32)[None] * inv[:, None]).astype(np.float32) for pos in (t // GRID_W, t % GRID_W)]
    rope = np.zeros((P, 2, T), np.float32)
    for part in range(4):
        ang = angles[part % 2]
        for b, sign in ((0, -1.0), (1, 1.0)):
            r = slice(32 * part + 16 * b, 32 * part + 16 * b + 16)
            rope[r, 0] = np.cos(ang)
            rope[r, 1] = sign * np.sin(ang)

    vecs = np.concatenate([_tiles(norm_w[0]), _tiles(hgrn_gn[0]), _tiles(final_norm_w),
                           _tiles(ln_g_2.reshape(-1)), _tiles(ln_b_2.reshape(-1)), _tiles(b_ada_2.reshape(-1)),
                           _tiles(hgrn_lb_logits[0])], 1)
    lay = lambda v: np.ascontiguousarray(v)
    return {
        "w_stream": lay(np.stack(units)),
        "vecs": lay(vecs),
        "consts": consts,
        "hgrn_masks": masks,
        "fox_fb": lay(fox_fb[0][:, None]),
        "cond": lay(np.concatenate([c_2, c_ctx_2[None]])),
        "w_ada": lay(w_ada_2.reshape(2, D, 24, P).transpose(0, 2, 3, 1).reshape(ADA_UNITS, P, D)),
        "p_t": lay(p[0, 0].T.reshape(2, P, T).transpose(1, 0, 2)),
        "ctx_t": lay(ctx_2[0].T.reshape(KT, P, C).transpose(1, 0, 2)),
        "rope": rope,
        "rel_bias": lay(rel_bias),
        "a_sink": lay(a_sink_2[0][None]),
        "x_t": lay(x[0].T.reshape(KT, P, T).transpose(1, 0, 2)),
    }


def kernel(**inputs):
    from concourse import bacc
    from concourse.bass_utils import run_bass_kernel_spmd

    arrays = {f"in_{k}": v for k, v in lay_out(**{k: np.asarray(v) for k, v in inputs.items()}).items()}
    nc = bacc.Bacc("TRN2", target_bir_lowering=False, num_devices=1)
    tensors = {k[3:]: nc.dram_tensor(k, v.shape, mybir.dt.from_np(v.dtype), kind="ExternalInput").ap()
               for k, v in arrays.items()}
    tensors["out"] = nc.dram_tensor("out_t", (KT, P, T), F32, kind="ExternalOutput").ap()
    build_program(nc, tensors)
    out = run_bass_kernel_spmd(nc, [arrays], core_ids=[0]).results[0]["out_t"]
    return np.ascontiguousarray(out.reshape(1, D, T).transpose(0, 2, 1))
```

```python
from contextlib import ExitStack

import numpy as np
import concourse.bass as bass
from concourse import mybir

F32 = mybir.dt.float32
F32R = mybir.dt.float32r
ALU = mybir.AluOpType
ACT = mybir.ActivationFunctionType
AX = mybir.AxisListType.X
ds = bass.ds

P = 128
T = 1024
D = 1024
C = 256
TC = T + C
KT = D // P
CH = 512
PLE = 256
HG = 8
PAIRS = 8
HD = 64
HGRN_CHUNK = 32
LEVELS = 7
GRID_W = 64
BIG = -1e30
EPS = 1e-6
LN_EPS = 1e-5
ALPHA = (2.0 * 2) ** 0.25
ADA_UNITS = 48

V_NORM, V_GN, V_FINAL, V_LNG, V_LNB, V_BADA, V_LB, V_END = 0, 8, 16, 24, 40, 56, 104, 112
K_ID, K_TRI, K_WIN, K_COL, K_ROW, K_END = 0, 128, 256, 256 + 640, 256 + 640 + 64, 256 + 640 + 64 + 9

U_HGRN = 0
U_FZ = U_HGRN + 4 * HG
U_FOX = U_FZ + 2
U_OUT = U_FOX + 4 * PAIRS
U_PLE = U_OUT + 2 * KT
U_GATE = U_PLE + 2
U_A = U_GATE + KT
U_A_OUT = U_A + 20
U_B = U_A_OUT + KT
U_B_OUT = U_B + 4 * PAIRS
UNITS = U_B_OUT + KT
assert UNITS % 2 == 0


def build_program(nc, a):
    ctx = ExitStack()

    def sb(name, shape, dt=F32, at=None):
        return (at or ctx).enter_context(nc.sbuf_tensor(name, shape, dt))

    def sem(name):
        return ctx.enter_context(nc.semaphore(name))

    with ctx:
        ps = ctx.enter_context(nc.psum_tensor("ps", [P, 8 * CH], F32))

        def bank(b, n=1):
            return ps[:, b * CH:(b + n) * CH]

        h_dram = nc.dram_tensor("residual", [KT, P, TC], F32).ap()
        y_dram = nc.dram_tensor("y_parts", [2, 17, P, TC], F32).ap()

        consts = sb("consts", [P, K_END])
        vecs = sb("vecs", [P, V_END])
        ident = consts[:, K_ID:K_ID + P]
        ada = sb("ada", [P, ADA_UNITS, 2])
        adv = sb("adv", [P, ADA_UNITS, 2])
        mod_g = sb("mod_g", [P, 2, KT, 2])
        mod_shift = sb("mod_shift", [P, 2, KT, 2])
        gates = sb("gates", [P, 2, KT, 3])
        ones_mean = sb("ones_mean", [P, P])
        small = sb("small", [P, 8])
        raw = sb("raw", [P, 2, KT * P])
        w_hi = sb("w_hi", [P, 2, KT * P], F32R)
        w_lo = sb("w_lo", [P, 2, KT * P], F32R)

        def whi(slot, k):
            return w_hi[:, slot, k * P:(k + 1) * P]

        def wlo(slot, k):
            return w_lo[:, slot, k * P:(k + 1) * P]

        loaded = sem("loaded")
        x_loaded = [sem(f"x_loaded{i}") for i in range(4)]
        raw_loaded = [sem("raw_loaded0"), sem("raw_loaded1")]
        w_ready = sem("w_ready")
        w_used = sem("w_used")
        consts_set = sem("consts_set")
        std = sb("std", [P, TC // P])
        stat_sd = sem("stat_sd")
        stat_diag = sem("stat_diag")
        stat_row = sem("stat_row")

        block1 = ctx.enter_context(ExitStack())
        u_hi = sb("u_hi", [P, KT, T], F32R, block1)
        u_lo = sb("u_lo", [P, KT, T], F32R, block1)
        u_ready = sem("u_ready")

        def token_means(pe, src, cols, b, k, n=KT):
            for j in range(cols // P):
                mm = pe.matmul(ps[:, b * CH + j:b * CH + j + 1], src[:, j * P:(j + 1) * P], ones_mean[:, 0:1],
                               start=k == 0 and j == 0, stop=k == n - 1 and (j + 1) * P == cols)
            return mm

        def standard_deviations(act, cols, b, eps):
            n = cols // P
            nc.scalar.activation(std[:, 0:n], ps[:, b * CH:b * CH + n], ACT.Sqrt, bias=eps).then_inc(stat_sd, 1)

        def inverse_diagonals(dve, cols, diag, norm):
            n = cols // P
            dve.wait_ge(stat_sd, norm)
            dve.reciprocal(std[:, 0:n], std[:, 0:n])
            dve.drain()
            dve.scalar_tensor_tensor(diag[:, 0:cols].rearrange("p (j t) -> p j t", t=P),
                                     ident.unsqueeze(1).broadcast_to([P, n, P]), float(D),
                                     std[:, 0:n].unsqueeze(2).broadcast_to([P, n, P]), ALU.mult, ALU.mult
                                     ).then_inc(stat_diag, 1)

        def spread_rows(pe, cols, diag, b, norm):
            pe.wait_ge(stat_diag, norm)
            for c in range(0, cols, CH):
                w = min(CH, cols - c)
                mm = pe.matmul(ps[:, b * CH + c:b * CH + c + w], ones_mean[:], diag[:, c:c + w], start=True, stop=True)
            mm.then_inc(stat_row, 1)

        def project(pe, n, slot, hi, lo, chunks, done, tiles=range(KT), first=0, start=True, stop=True, last=True,
                    ready=None, tiles_outer=False):
            pe.wait_ge(w_ready, n + 1)
            steps = [(c, i) for c in range(len(chunks)) for i in range(len(tiles))]
            if tiles_outer:
                steps.sort(key=lambda s: s[1])
            for c, i in steps:
                cols, out, waits = chunks[c]
                if i == 0:
                    for s, v in waits:
                        pe.wait_ge(s, v)
                if ready and (c == 0):
                    pe.wait_ge(*ready(i))
                for p, (w, u) in enumerate(((whi, hi), (whi, lo), (wlo, hi))):
                    mm = pe.matmul(out, w(slot, tiles[i]), u[:, first + i, cols],
                                   start=start and i == 0 and p == 0,
                                   stop=stop and i == len(tiles) - 1 and p == 2)
                if i == len(tiles) - 1:
                    mm.then_inc(w_used if last and c == len(chunks) - 1 else done, 1)

        def stream_loads(sp):
            for s in range(2):
                sp.dma_start(raw[:, s, :], a["w_stream"][s]).then_inc(raw_loaded[s], 16)

        def stream_loads_to(sp, n0, n1):
            with sp.Fori(n0 // 2, n1 // 2) as i:
                for s in range(2):
                    sp.wait_ge(w_ready, i * 2 + (s - 1))
                    sp.dma_start(raw[:, s, :], a["w_stream"][ds(i * 2 + s, 1)].rearrange("a p n -> (a p) n")
                                 ).then_inc(raw_loaded[s], 16)

        def split_unit(pool, s):
            zero = small[:, 0:1].broadcast_to([P, KT * P])
            pool.tensor_tensor(w_hi[:, s, :], raw[:, s, :], zero, ALU.add)
            pool.drain()
            pool.tensor_tensor(w_lo[:, s, :], raw[:, s, :], w_hi[:, s, :].bitcast(F32),
                               ALU.subtract).then_inc(w_ready, 1)

        def stream_splits(pool):
            pool.wait_ge(consts_set, 1)
            for s in range(2):
                pool.wait_ge(raw_loaded[s], 16)
                split_unit(pool, s)
            with pool.Fori(1, UNITS // 2) as i:
                for s in range(2):
                    pool.wait_ge(raw_loaded[s], i * 16 + 16)
                    pool.wait_ge(w_used, i * 2 + (s - 1))
                    split_unit(pool, s)

        ph1 = ctx.enter_context(ExitStack())
        x_sb = sb("x_sb", [P, KT, T], at=ph1)
        sq1 = sb("sq1", [P, 2, T], at=ph1)
        diag1 = sb("diag1", [P, T], at=ph1)
        ph1.close()
        n1_sq = sem("n1_sq")
        n1_sum = sem("n1_sum")
        n1_scaled = sem("n1_scaled")
        n1_hi = sem("n1_hi")

        def norm1_act(act):
            for k in range(KT):
                act.wait_ge(x_loaded[k // 2], 16)
                if k >= 2:
                    act.wait_ge(n1_sum, k - 1)
                nc.scalar.activation(sq1[:, k % 2, :], x_sb[:, k, :], ACT.Square).then_inc(n1_sq, 1)
            act.wait_ge(consts_set, 1)
            act.wait_ge(n1_sum, KT)
            standard_deviations(act, T, 2, small[:, 1:2])
            for k in range(KT):
                act.wait_ge(n1_scaled, k + 1)
                nc.scalar.copy(u_hi[:, k, :], x_sb[:, k, :]).then_inc(n1_hi, 1)

        def norm1_pe(pe):
            pe.wait_ge(consts_set, 1)
            for k in range(KT):
                pe.wait_ge(n1_sq, k + 1)
                token_means(pe, sq1[:, k % 2, :], T, 2, k).then_inc(n1_sum, 1)
            spread_rows(pe, T, diag1, 6, 1)

        def norm1_dve(dve):
            dve.memset(small[:, 0:1], 0.0)
            dve.memset(small[:, 1:2], EPS)
            dve.memset(small[:, 2:3], LN_EPS)
            dve.memset(ones_mean[:], 1.0 / D)
            dve.drain().then_inc(consts_set, 1)
            dve.wait_ge(loaded, 32)
            inverse_diagonals(dve, T, diag1, 1)
            dve.wait_ge(stat_row, 1)

            def low(k):
                dve.wait_ge(n1_hi, k + 1)
                dve.tensor_tensor(u_lo[:, k, :], x_sb[:, k, :], u_hi[:, k, :].bitcast(F32),
                                  ALU.subtract).then_inc(u_ready, 1)
            for k in range(KT):
                dve.scalar_tensor_tensor(x_sb[:, k, :], x_sb[:, k, :], vecs[:, V_NORM + k:V_NORM + k + 1],
                                         bank(6, 2), ALU.mult, ALU.mult).then_inc(n1_scaled, 1)
                if k:
                    low(k - 1)
            low(KT - 1)

        ph2 = ctx.enter_context(ExitStack())
        hgrn_masks = sb("hgrn_masks", [P, 2, T], at=ph2)
        z_f = sb("z_f", [P, T], at=ph2)
        t_a = sb("t_a", [P, T], at=ph2)
        t_g = sb("t_g", [P, T], at=ph2)
        k_t = sb("k_t", [P, T], at=ph2)
        q_t = sb("q_t", [P, T], at=ph2)
        i_t = sb("i_t", [P, T], at=ph2)
        b32 = sb("b32", [P, T], at=ph2)
        b128 = sb("b128", [P, T], at=ph2)
        off = sb("off", [P, 8, 4], at=ph2)
        tile_decay = sb("tile_decay", [P, 8], at=ph2)
        lev = sb("lev", [P, LEVELS, T], at=ph2)
        q_in = sb("q_in", [P, T], at=ph2)
        k_out = sb("k_out", [P, T], at=ph2)
        k_tok = sb("k_tok", [P, 8, P], at=ph2)
        i_tok = sb("i_tok", [P, 8, P], at=ph2)
        scores = sb("scores", [P, 8, P], at=ph2)
        pairs = z_f[:].rearrange("p (s t) -> p s t", s=2)
        states = b32[:].rearrange("p (j t) -> p j t", t=P)
        silu_h = sb("silu_h", [P, T], at=ph2)
        o_n = sb("o_n", [P, T], at=ph2)
        ssq = sb("ssq", [P, 8], at=ph2)
        rs8 = sb("rs8", [P, 8], at=ph2)
        head_vec = sb("head_vec", [P, 4], at=ph2)
        lnom = sb("lnom", [P, 8], at=ph2)
        yh_hi = sb("yh_hi", [P, T], F32R, ph2)
        yh_lo = sb("yh_lo", [P, T], F32R, ph2)
        ph2.close()

        h_chunk = sem("h_chunk")
        h_z = sem("h_z")
        h_t2 = sem("h_t2")
        h_k = sem("h_k")
        h_q = sem("h_q")
        h_it = sem("h_it")
        h_tr = sem("h_tr")
        h_tok = sem("h_tok")
        h_e = sem("h_e")
        h_x = sem("h_x")
        h_kout = sem("h_kout")
        h_ops = sem("h_ops")
        h_sg = sem("h_sg")
        h_lv = sem("h_lv")
        h_sc = sem("h_sc")
        h_acc = sem("h_acc")
        h_ds = sem("h_ds")
        h_s = sem("h_s")
        h_o = sem("h_o")
        h_sd = sem("h_sd")
        h_on = sem("h_on")
        h_yt = sem("h_yt")
        h_y = sem("h_y")
        h_start = sem("h_start")
        h_hi = sem("h_hi")
        h_lo = sem("h_lo")
        h_spill = sem("h_spill")
        lb_set = sem("lb_set")
        lb_exp = sem("lb_exp")

        def hgrn_pe(pe):
            def turn_outputs(h):
                pe.wait_ge(h_start, 1)
                pe.wait_ge(h_on, h)
                for j in range(8):
                    mm = pe.transpose(ps[:, 6 * CH + j * P:6 * CH + (j + 1) * P], o_n[:, j * P:(j + 1) * P], ident)
                mm.then_inc(h_y, 1)

            with pe.Fori(0, HG) as h:
                n = h * 4 + U_HGRN

                def unit(j, b, waits):
                    project(pe, n + j, j % 2, u_hi, u_lo,
                            [(slice(c * CH, c * CH + CH), bank(b + c), waits if c == 0 else []) for c in range(2)],
                            h_chunk, ready=(lambda k: (u_ready, k + 1)) if j == 0 else None)

                unit(0, 0, [(h_sc, h * 8)])
                turn_outputs(h)
                unit(1, 2, [])
                unit(2, 4, [(h_on, h)])
                unit(3, 0, [(h_z, h + 1)])
                pe.wait_ge(h_it, h + 1)
                pe.wait_ge(h_yt, h + 1)
                for j in range(8):
                    mm = pe.transpose(ps[:, 6 * CH + j * P:6 * CH + (j + 1) * P], i_t[:, j * P:(j + 1) * P], ident)
                mm.then_inc(h_tr, 1)
                for what in (h_k, h_q, h_sg):
                    pe.wait_ge(what, h + 1)
                for j in range(8):
                    mm = pe.matmul(ps[:, j * P:(j + 1) * P], k_t[:, j * P:(j + 1) * P], q_t[:, j * P:(j + 1) * P],
                                   start=True, stop=True)
                mm.then_inc(h_lv, 1)
                pe.wait_ge(h_kout, h + 1)
                pe.wait_ge(h_tok, h * 2 + 1)
                for j in range(8):
                    mm = pe.transpose(ps[:, 6 * CH + j * P:6 * CH + (j + 1) * P], k_out[:, j * P:(j + 1) * P], ident)
                mm.then_inc(h_tr, 1)
                pe.wait_ge(h_ops, h + 1)
                for lv in range(LEVELS):
                    pe.wait_ge(h_sc, h * 8 + max(lv - 2, 0 if lv < 2 else 1))
                    H = 1 << lv
                    for j in range(8):
                        q = lev[:, lv, j * P:(j + 1) * P].rearrange("p (g r t) -> p g r t", r=2, t=H)[:, :, 1, :]
                        mm = pe.matmul(ps[:, (lv + 2) % 4 * CH + j * HD:(lv + 2) % 4 * CH + (j + 1) * HD],
                                       lev[:, lv, j * P:(j + 1) * P], q, start=True, stop=True)
                    mm.then_inc(h_lv, 1)
                    if lv == 1:
                        pe.wait_ge(h_tok, h * 2 + 2)
                        for j in range(7):
                            mm = pe.matmul(ps[:, 6 * CH + j * P:6 * CH + (j + 1) * P], k_tok[:, j, :], i_tok[:, j, :],
                                           start=True, stop=True)
                        mm.then_inc(h_ds, 1)
                pe.wait_ge(h_acc, h + 1)
                for j in range(8):
                    o = ps[:, 4 * CH + j * P:4 * CH + (j + 1) * P]
                    mm = pe.matmul(o, scores[:, j, :], i_tok[:, j, :], start=True, stop=j == 0)
                    if j:
                        pe.wait_ge(h_s, h * 7 + j)
                        mm = pe.matmul(o, q_in[:, j * P:(j + 1) * P], states[:, j - 1, :], start=False, stop=True)
                    mm.then_inc(h_o, 1)
            turn_outputs(HG)

        def hgrn_act(act):
            act.wait_ge(lb_set, 1)
            act.dma_start(hgrn_masks[:], a["hgrn_masks"]).then_inc(loaded, 16)
            nc.scalar.activation(lnom[:], lnom[:], ACT.Exp).then_inc(lb_exp, 1)
            act.wait_ge(lb_set, 2)
            nc.scalar.activation(lnom[:], lnom[:], ACT.Ln, bias=1.0, scale=-1.0).then_inc(lb_exp, 1)

            def high_part(h):
                act.wait_ge(h_yt, h + 1)
                act.wait_ge(h_spill, h * 32)
                nc.scalar.copy(yh_hi[:], o_n[:]).then_inc(h_hi, 1)

            def spill(h):
                act.wait_ge(h_lo, h + 1)
                for part, src in ((0, yh_hi), (1, yh_lo)):
                    row = y_dram[part, h, :, 0:T] if isinstance(h, int) else (
                        y_dram[part, ds(h, 1), :, 0:T].rearrange("a p t -> (a p) t"))
                    act.dma_start(row, src[:].bitcast(F32)).then_inc(h_spill, 16)

            with act.Fori(0, HG) as h:
                act.wait_ge(h_chunk, h * 4 + 1)
                act.wait_ge(w_used, h * 4 + 1)
                nc.scalar.copy(z_f[:], bank(0, 2))
                nc.scalar.activation(t_a[:], bank(0, 2), ACT.Abs)
                act.drain()
                nc.scalar.activation(t_a[:], t_a[:], ACT.Exp, scale=-1.0)
                act.drain()
                nc.scalar.activation(t_a[:], t_a[:], ACT.Ln, bias=1.0).then_inc(h_z, 1)
                high_part(h)
                act.wait_ge(h_t2, h + 1)
                nc.scalar.activation(k_t[:], t_a[:], ACT.Exp).then_inc(h_k, 1)
                for lv in range(LEVELS):
                    act.wait_ge(h_e, h * 9 + (lv + 1))
                    nc.scalar.activation(lev[:, lv, :], lev[:, lv, :], ACT.Exp).then_inc(h_x, 1)
                act.wait_ge(h_e, h * 9 + 9)
                nc.scalar.activation(q_in[:], b128[:], ACT.Exp).then_inc(h_x, 1)
                nc.scalar.activation(k_out[:], k_out[:], ACT.Exp)
                nc.scalar.activation(tile_decay[:], b128[:].rearrange("p (j t) -> p j t", j=8)[:, :, P - 1],
                                     ACT.Exp).then_inc(h_x, 1)
                act.wait_ge(h_chunk, h * 4 + 2)
                act.wait_ge(w_used, h * 4 + 2)
                nc.scalar.activation(q_t[:], bank(2, 2), ACT.Copy, scale=float(P) ** -0.5).then_inc(h_q, 1)
                spill(h)
                act.wait_ge(h_chunk, h * 4 + 3)
                act.wait_ge(w_used, h * 4 + 3)
                nc.scalar.copy(i_t[:], bank(4, 2)).then_inc(h_it, 1)
                act.wait_ge(h_chunk, h * 4 + 4)
                act.wait_ge(w_used, h * 4 + 4)
                nc.scalar.activation(silu_h[:], bank(0, 2), ACT.Silu).then_inc(h_sg, 1)
                act.wait_ge(h_tr, h * 2 + 1)
                nc.scalar.copy(i_tok[:].rearrange("p j t -> p (j t)"), bank(6, 2)).then_inc(h_tok, 1)
                act.wait_ge(h_tr, h * 2 + 2)
                nc.scalar.copy(k_tok[:].rearrange("p j t -> p (j t)"), bank(6, 2)).then_inc(h_tok, 1)
                for j in range(8):
                    if j % 4 == 0:
                        act.wait_ge(h_o, h * 8 + (j + 4))
                    nc.scalar.activation(q_in[:, j * P:(j + 1) * P], ps[:, 4 * CH + j * P:4 * CH + (j + 1) * P],
                                         ACT.Square, accum_out=ssq[:, j:j + 1])
                act.drain()
                nc.scalar.activation(ssq[:], ssq[:], ACT.Sqrt, bias=small[:, 1:2], scale=1.0 / P).then_inc(h_sd, 1)
            high_part(HG)
            spill(HG)

        def hgrn_dve(dve):
            lb_in = vecs[:, V_LB:V_LB + 8]
            dve.wait_ge(u_ready, KT)
            for what in (o_n, silu_h, head_vec):
                dve.memset(what[:], 0.0)
            dve.drain().then_inc(h_start, 1)
            dve.tensor_tensor(lnom[:], lb_in, lb_in, ALU.subtract).then_inc(lb_set, 1)
            dve.wait_ge(lb_exp, 1)
            dve.reciprocal(ssq[:], lnom[:])
            dve.drain()
            dve.tensor_tensor(lnom[:], lnom[:], ssq[:], ALU.mult)
            dve.drain()
            dve.tensor_tensor(lnom[:], lnom[:], lnom[:], ALU.subtract)
            dve.drain().then_inc(lb_set, 1)
            dve.wait_ge(lb_exp, 2)
            dve.wait_ge(loaded, 48)
            def gate_outputs(h):
                dve.wait_ge(h_y, h + 1)
                dve.scalar_tensor_tensor(o_n[:], bank(6, 2), head_vec[:, 0:1], silu_h[:],
                                         ALU.mult, ALU.mult).then_inc(h_yt, 1)

            def low_part(h):
                dve.wait_ge(h_hi, h + 1)
                dve.tensor_tensor(yh_lo[:], o_n[:], yh_hi[:].bitcast(F32), ALU.subtract).then_inc(h_lo, 1)

            with dve.Fori(0, HG) as h:
                gate_outputs(h)
                dve.drain()
                dve.tensor_copy(head_vec[:, 0:1], vecs[:, ds(h + V_GN, 1)])
                dve.tensor_copy(head_vec[:, 1:2], lnom[:, ds(h, 1)])
                dve.drain()
                dve.wait_ge(h_z, h + 1)
                dve.scalar_tensor_tensor(t_g[:], z_f[:], 0.0, t_a[:], ALU.min, ALU.subtract)
                dve.drain()
                dve.tensor_tensor(t_a[:], t_g[:], z_f[:], ALU.subtract)
                dve.tensor_scalar(t_g[:], t_g[:], head_vec[:, 1:2], None, ALU.add)
                dve.drain()
                dve.tensor_scalar(t_a[:], t_a[:], head_vec[:, 1:2], None, ALU.add).then_inc(h_t2, 1)
                dve.tensor_tensor_scan(b32[:], hgrn_masks[:, 1, :], t_g[:], 0.0, ALU.mult, ALU.add)
                dve.drain()
                tot = b32[:].rearrange("p (j c t) -> p j c t", c=4, t=32)[:, :, :, 31]
                dve.memset(off[:, :, 0], 0.0)
                dve.tensor_copy(off[:, :, 1], tot[:, :, 0])
                dve.tensor_tensor(off[:, :, 2], tot[:, :, 0], tot[:, :, 1], ALU.add)
                dve.drain()
                dve.tensor_tensor(off[:, :, 3], off[:, :, 2], tot[:, :, 2], ALU.add)
                dve.drain()
                dve.tensor_tensor(b128[:].rearrange("p (c t) -> p c t", t=32),
                                  b32[:].rearrange("p (c t) -> p c t", t=32),
                                  off[:].rearrange("p j c -> p (j c)").unsqueeze(2).broadcast_to([P, 32, 32]), ALU.add)
                dve.drain()
                for lv in range(LEVELS):
                    H = 1 << lv
                    b = (b32 if 2 * H <= HGRN_CHUNK else b128)[:].rearrange("p (g r t) -> p g r t", r=2, t=H)
                    e = lev[:, lv, :].rearrange("p (g r t) -> p g r t", r=2, t=H)
                    mid = b[:, :, 0, H - 1:H].broadcast_to([P, T // (2 * H), H])
                    dve.tensor_tensor(e[:, :, 0, :], mid, b[:, :, 0, :], ALU.subtract)
                    dve.tensor_tensor(e[:, :, 1, :], b[:, :, 1, :], mid, ALU.subtract).then_inc(h_e, 1)
                bt = b128[:].rearrange("p (j t) -> p j t", t=P)
                dve.tensor_tensor(k_out[:].rearrange("p (j t) -> p j t", t=P),
                                  bt[:, :, P - 1:P].broadcast_to([P, 8, P]), bt, ALU.subtract).then_inc(h_e, 2)
                low_part(h)
                dve.wait_ge(h_k, h + 1)
                for lv in range(LEVELS):
                    H = 1 << lv
                    e = lev[:, lv, :].rearrange("p (g r t) -> p g r t", r=2, t=H)
                    k = k_t[:].rearrange("p (g r t) -> p g r t", r=2, t=H)
                    dve.wait_ge(h_x, h * 9 + (lv + 1))
                    dve.tensor_tensor(e[:, :, 0, :], e[:, :, 0, :], k[:, :, 0, :], ALU.mult)
                dve.wait_ge(h_x, h * 9 + 9)
                dve.tensor_tensor(k_out[:], k_out[:], k_t[:], ALU.mult).then_inc(h_kout, 1)
                dve.wait_ge(h_q, h + 1)
                dve.tensor_tensor(q_in[:], q_in[:], q_t[:], ALU.mult)
                for lv in range(LEVELS):
                    H = 1 << lv
                    e = lev[:, lv, :].rearrange("p (g r t) -> p g r t", r=2, t=H)
                    q = q_t[:].rearrange("p (g r t) -> p g r t", r=2, t=H)
                    dve.tensor_tensor(e[:, :, 1, :], e[:, :, 1, :], q[:, :, 1, :], ALU.mult)
                dve.drain().then_inc(h_ops, 1)

                own = hgrn_masks[:, 0, LEVELS * HD:LEVELS * HD + P]
                dve.wait_ge(h_lv, h * 8 + 1)
                dve.tensor_tensor(scores[:], bank(0, 2).rearrange("p (j t) -> p j t", t=P),
                                  own.unsqueeze(1).broadcast_to([P, 8, P]), ALU.mult).then_inc(h_sc, 1)

                def mask_level(lv):
                    dve.wait_ge(h_lv, h * 8 + (lv + 2))
                    dve.tensor_tensor(pairs[:, lv % 2, :].rearrange("p (j t) -> p j t", t=HD),
                                      bank((lv + 2) % 4).rearrange("p (j t) -> p j t", t=HD),
                                      hgrn_masks[:, 0, lv * HD:(lv + 1) * HD].unsqueeze(1).broadcast_to([P, 8, HD]),
                                      ALU.mult).then_inc(h_sc, 1)

                mask_level(0)
                for lv in range(LEVELS):
                    dve.drain()
                    if lv + 1 < LEVELS:
                        mask_level(lv + 1)
                    H = 1 << lv
                    at = scores[:].rearrange("p j t -> p (j t)").rearrange("p (g r t) -> p g r t", r=2, t=H)[:, :, 1, :]
                    ins = dve.tensor_tensor(at, at, pairs[:, lv % 2, :].rearrange("p (g t) -> p g t", t=H), ALU.add)
                    if lv + 1 == LEVELS:
                        ins.then_inc(h_acc, 1)
                    add = ps[:, 6 * CH + lv * P:6 * CH + (lv + 1) * P]
                    if lv == 0:
                        dve.wait_ge(h_ds, h + 1)
                        dve.tensor_copy(states[:, 0, :], add).then_inc(h_s, 1)
                    else:
                        dve.scalar_tensor_tensor(states[:, lv, :], states[:, lv - 1, :], tile_decay[:, lv:lv + 1],
                                                 add, ALU.mult, ALU.add).then_inc(h_s, 1)
                dve.wait_ge(h_sd, h + 1)
                dve.reciprocal(rs8[:], ssq[:])
                dve.drain()
                dve.tensor_tensor(o_n[:].rearrange("p (j t) -> p j t", t=P),
                                  bank(4, 2).rearrange("p (j t) -> p j t", t=P),
                                  rs8[:].unsqueeze(2).broadcast_to([P, 8, P]), ALU.mult).then_inc(h_on, 1)
            gate_outputs(HG)
            low_part(HG)

        class Attention:

            def __init__(self, name, blocks, halves, width, keys, q_cols, area, ahead=2):
                self.blocks, self.halves, self.name = blocks, halves, name
                self.NB, self.NA, self.NH = len(blocks), 2 * len(blocks), len(halves)
                self.silu = sb(f"{name}_silu", [P, q_cols], at=area)
                self.y = sb(f"{name}_y", [P, q_cols], at=area)
                self.q2 = [sb(f"{name}_q2_{i}", [P, q_cols], F32R, area) for i in range(2)]
                self.l = sb(f"{name}_l", [P, 3, width], at=area)
                self.pt = sb(f"{name}_pt", [P, 3, CH], at=area)
                self.nm = sb(f"{name}_nm", [P, self.NA, 2], at=area)
                self.rs = sb(f"{name}_rs", [P, self.NA], at=area)
                self.ri = sb(f"{name}_ri", [P, self.NA], at=area)
                self.mark = sb(f"{name}_mark", [P, self.NA], at=area)
                self.o_tok = sb(f"{name}_o_tok", [P, self.NB, P], at=area)
                self.y_hi = sb(f"{name}_y_hi", [P, q_cols], F32R, area)
                self.y_lo = sb(f"{name}_y_lo", [P, q_cols], F32R, area)
                self.scored = sem(f"{name}_scored")
                self.shifted = sem(f"{name}_shifted")
                self.exped = sem(f"{name}_exped")
                self.turned = sem(f"{name}_turned")
                self.copied = {"act": sem(f"{name}_copied_act"), "dve": sem(f"{name}_copied_dve")}
                self.valued = sem(f"{name}_valued")
                self.left = sem(f"{name}_left")
                self.hi_done = sem(f"{name}_hi_done")
                self.lo_done = sem(f"{name}_lo_done")
                self.spilled = sem(f"{name}_spilled")
                self.chunk = sem(f"{name}_chunk")
                self.plan(ahead)

            def plan(self, ahead):
                self.groups, self.copier, self.place, self.v_place = [], [], [], []
                self.steps = [("S", u) for u in range(min(ahead, self.NA))]
                load, waiting, late = {"act": 0, "dve": 0}, [], []

                def add(group, eng, cost):
                    load[eng] += cost
                    self.place.append(self.copier.count(eng))
                    self.v_place.append(sum(g[0] == "P" for g in self.groups))
                    self.groups.append(group)
                    self.copier.append(eng)
                    self.steps.append(("T", len(self.groups) - 1))

                def value():
                    g = waiting.pop(0)
                    self.steps.append(("V", g))
                    _, u, _, c1 = self.groups[g]
                    if u % 2 and c1 == len(self.blocks[u // 2]["chunks"]):
                        self.steps.append(("O", u // 2))
                        for hf, bs in enumerate(self.halves):
                            if u // 2 == bs[-1]:
                                late.append(hf)

                for u in range(self.NA):
                    if u + ahead < self.NA:
                        self.steps.append(("S", u + ahead))
                    blk = self.blocks[u // 2]
                    n, w = len(blk["chunks"]), blk["width"]
                    load["act"] += 200 + 0.83 * w
                    load["dve"] += 250 + 1.04 * w + (100 if u % 2 else 0)
                    for hf in [late.pop(0)] if late else []:
                        add(("Y", hf), "dve", 60 + 1.04 * P * len(self.halves[hf]))
                    parts = (n + 3) // 4
                    if n > 4:
                        parts = max(parts, 2)
                    for i in range(parts):
                        c0, c1 = n * i // parts, n * (i + 1) // parts
                        cost = {"act": 300 + 0.83 * P * (c1 - c0), "dve": 70 + 1.04 * P * (c1 - c0)}
                        eng = min(cost, key=lambda e: load[e] + cost[e])
                        add(("P", u, c0, c1), eng, cost[eng])
                        waiting.append(len(self.groups) - 1)
                        if len(waiting) > 2:
                            value()
                while waiting:
                    value()
                for hf in late:
                    add(("Y", hf), "dve", 0)
                self.NG = len(self.groups)
                self.NV = sum(g[0] == "P" for g in self.groups)
                self.copies = {e: self.copier.count(e) for e in load}

            def first_block(self, bs):
                return min(self.blocks[b]["b"] for b in bs)

            def last_group(self, u):
                return max(g for g, x in enumerate(self.groups) if x[0] == "P" and x[1] == u)

            def all_copied(self, it):
                return [(self.copied[e], it * self.copies[e]) for e in ("act", "dve")]

            def group_copied(self, it, g):
                e = self.copier[g]
                return self.copied[e], it * self.copies[e] + (self.place[g] + 1)

            def pe(self, pe, it, k2a, k2b, v, before):
                for step in self.steps:
                    if step[0] == "S":
                        u = step[1]
                        blk = self.blocks[u // 2]
                        pe.wait_ge(self.shifted, it * self.NA + max(u - 1, 0))
                        for s, w in before.get(step, []):
                            pe.wait_ge(s, w)
                        q = self.q2[u % 2][:, blk["b"] * P:(blk["b"] + 1) * P]
                        for pc, kc, n in blk["runs"]:
                            o = ps[:, (u % 2) * 2 * CH + pc:(u % 2) * 2 * CH + pc + n]
                            pe.matmul(o, q, k2a[u % 2][:, kc:kc + n], start=True, stop=False)
                            mm = pe.matmul(o, q, k2b[u % 2][:, kc:kc + n], start=False, stop=True)
                        mm.then_inc(self.scored, 1)
                    elif step[0] == "T":
                        g = step[1]
                        for s, w in [self.group_copied(it, g - 2)] if g >= 2 else self.all_copied(it):
                            pe.wait_ge(s, w)
                        out = ps[:, (4 + g % 2) * CH:(5 + g % 2) * CH]
                        if self.groups[g][0] == "P":
                            _, u, c0, c1 = self.groups[g]
                            pe.wait_ge(self.exped, it * self.NA + (u + 1))
                            for s, w in before.get(step, []):
                                pe.wait_ge(s, w)
                            for c in range(c0, c1):
                                pc, n, _ = self.blocks[u // 2]["chunks"][c]
                                mm = pe.transpose(out[0:n, (c - c0) * P:(c - c0 + 1) * P],
                                                  self.l[:, u % 3, pc:pc + n], ident)
                        else:
                            bs = self.halves[self.groups[g][1]]
                            pe.wait_ge(self.left, it * self.NB + (bs[-1] + 1))
                            for b in bs:
                                i = self.blocks[b]["b"] - self.first_block(bs)
                                mm = pe.transpose(out[:, i * P:(i + 1) * P], self.o_tok[:, b, :], ident)
                        mm.then_inc(self.turned, 1)
                    elif step[0] == "V":
                        g = step[1]
                        _, u, c0, c1 = self.groups[g]
                        b, hd = u // 2, u % 2
                        blk = self.blocks[b]
                        pe.wait_ge(*self.group_copied(it, g))
                        if c0 == 0 and hd == 0:
                            pe.wait_ge(self.left, it * self.NB + max(b - 1, 0))
                            for s, w in before.get(("V", b), []):
                                pe.wait_ge(s, w)
                        o0 = (6 + b % 2) * CH + hd * HD
                        vals, cols = v[hd]
                        for c in range(c0, c1):
                            _, n, vb = blk["chunks"][c]
                            mm = pe.matmul(ps[:, o0:o0 + HD],
                                           self.pt[0:n, self.v_place[g] % 3, (c - c0) * P:(c - c0 + 1) * P],
                                           vals[0:n, vb, cols], start=c == 0, stop=c == len(blk["chunks"]) - 1)
                        mm.then_inc(self.valued, 1)

            def act(self, act, it):
                for step in self.steps:
                    if step[0] == "S":
                        u = step[1]
                        w = self.blocks[u // 2]["width"]
                        act.wait_ge(self.shifted, it * self.NA + (u + 1))
                        nc.scalar.activation(self.l[:, u % 3, 0:w], self.l[:, u % 3, 0:w], ACT.Exp, scale=-1.0,
                                             bias=self.nm[:, u, 1:2], accum_out=self.rs[:, u:u + 1]
                                             ).then_inc(self.exped, 1)
                    elif step[0] == "T" and self.copier[step[1]] == "act":
                        self.copy_group(act, it, step[1], nc.scalar.copy)

            def copy_group(self, eng, it, g, copy):
                _, u, c0, c1 = self.groups[g]
                eng.wait_ge(self.turned, it * self.NG + (g + 1))
                i = self.v_place[g]
                eng.wait_ge(self.valued, it * self.NV + max(i - 2, 0))
                n = self.blocks[u // 2]["chunks"][c1 - 1][1]
                full = (c1 - c0 - (n < P)) * P
                src = ps[:, (4 + g % 2) * CH:(5 + g % 2) * CH]
                if n < P:
                    ins = copy(self.pt[0:n, i % 3, full:full + P], src[0:n, full:full + P])
                if full:
                    ins = copy(self.pt[:, i % 3, 0:full], src[:, 0:full])
                ins.then_inc(self.copied[self.copier[g]], 1)

            def dve(self, dve, it, start, masks):
                start(self.nm[:, :, 0].rearrange("p (b h) -> p b h", h=2))
                dve.drain()
                for step in self.steps:
                    if step[0] == "S":
                        u = step[1]
                        blk = self.blocks[u // 2]
                        dve.wait_ge(self.turned, it * self.NG + (self.last_group(u - 3) + 1 if u >= 3 else 0))
                        dve.wait_ge(self.scored, it * self.NA + (u + 1))
                        segs = masks(u)
                        p1 = (u % 2) * 2 * CH + blk["first"]
                        for i, (p0, n, mask) in enumerate(segs):
                            if i:
                                dve.drain()
                            end = i == len(segs) - 1
                            ins = dve.tensor_tensor_reduce(
                                self.l[:, u % 3, p0:p0 + n], ps[:, p1 + p0:p1 + p0 + n], mask, -1.0,
                                self.nm[:, u, 0:1], ALU.add, ALU.min,
                                self.nm[:, u, 1:2] if end else self.nm[:, u, 0:1])
                        ins.then_inc(self.shifted, 1)
                    elif step[0] == "T" and self.copier[step[1]] == "dve":
                        g = step[1]
                        if self.groups[g][0] == "P":
                            self.copy_group(dve, it, g, dve.tensor_copy)
                            continue
                        bs = self.halves[self.groups[g][1]]
                        t0, n = self.first_block(bs) * P, len(bs) * P
                        dve.wait_ge(self.turned, it * self.NG + (g + 1))
                        dve.tensor_tensor(self.y[:, t0:t0 + n], ps[:, (4 + g % 2) * CH:(4 + g % 2) * CH + n],
                                          self.silu[:, t0:t0 + n], ALU.mult).then_inc(self.copied["dve"], 1)
                    elif step[0] == "O":
                        b = step[1]
                        dve.wait_ge(self.valued, it * self.NV + (self.v_place[self.last_group(2 * b + 1)] + 1))
                        dve.reciprocal(self.ri[:, 2 * b:2 * b + 2], self.rs[:, 2 * b:2 * b + 2])
                        dve.drain()
                        dve.tensor_tensor(self.o_tok[:, b, :].rearrange("p (h d) -> p h d", h=2),
                                          ps[:, (6 + b % 2) * CH:(6 + b % 2) * CH + P].rearrange("p (h d) -> p h d", h=2),
                                          self.ri[:, 2 * b:2 * b + 2].unsqueeze(2).broadcast_to([P, 2, HD]),
                                          ALU.mult).then_inc(self.left, 1)

            def finish_act(self, act, it, y_index, cols):
                act.wait_ge(self.copied["dve"], (it + 1) * self.copies["dve"])
                act.wait_ge(self.spilled, it * 32)
                nc.scalar.copy(self.y_hi[:], self.y[:]).then_inc(self.hi_done, 1)
                act.wait_ge(self.lo_done, it + 1)
                for part, src in ((0, self.y_hi), (1, self.y_lo)):
                    act.dma_start(y_dram[part, ds(y_index, 1), :, 0:cols].rearrange("a p t -> (a p) t"),
                                  src[:].bitcast(F32)).then_inc(self.spilled, 16)

            def finish_dve(self, dve, it):
                dve.wait_ge(self.hi_done, it + 1)
                dve.tensor_tensor(self.y_lo[:], self.y[:], self.y_hi[:].bitcast(F32),
                                  ALU.subtract).then_inc(self.lo_done, 1)

        def rows_of(hd):
            return slice(hd * HD, hd * HD + HD)

        ph3 = ctx.enter_context(ExitStack())

        def fox_block(b):
            w = (b + 1) * P
            first = max(min(w, CH) if w <= CH else w // 2 // P * P, 2 * P)
            runs = [(CH - first, 0, first)]
            if w > first:
                runs.append((CH, first, w - first))
            return {"b": b, "width": w, "first": CH - first, "runs": runs,
                    "chunks": [(c * P, P, c) for c in range(b + 1)]}

        FOX_ORDER = [4, 7, 5, 6, 3, 0, 2, 1]
        fox = Attention("fox", [fox_block(b) for b in FOX_ORDER], [[0, 1, 2, 3], [4, 5, 6, 7]], T, T, T, ph3)
        fx_k2a = [sb(f"fx_k2a{i}", [P, T], F32R, ph3) for i in range(2)]
        fx_k2b = [sb(f"fx_k2b{i}", [P, T], F32R, ph3) for i in range(2)]
        fx_v = sb("fx_v", [P, 8, P], at=ph3)
        fx_vt = sb("fx_vt", [P, T], at=ph3)
        fb = sb("fb", [16, 1], at=ph3)
        nf_b = sb("nf_b", [P, 2, T], at=ph3)
        nf_tri = sb("nf_tri", [P, 2, T], at=ph3)
        nf = nf_tri[:, 0, :]
        nf_t = nf_tri[:, 1, :]
        cond = sb("cond", [P, 2, D], at=ph3)
        ada_w = sb("ada_w", [P, 3, D], at=ph3)
        ada_acc = sb("ada_acc", [P, 12], at=ph3)
        ph3.close()

        fb_loaded = sem("fb_loaded")
        fz_shift = sem("fz_shift")
        fz_act = sem("fz_act")
        fz_done = sem("fz_done")
        nf_stored = sem("nf_stored")
        nf_loaded = sem("nf_loaded")
        f_hi = sem("f_hi")
        f_lo = sem("f_lo")
        f_v = sem("f_v")
        f_g = sem("f_g")
        f_vt = sem("f_vt")
        f_vc = sem("f_vc")
        cond_set = sem("cond_set")
        ada_loaded = sem("ada_loaded")
        ada_done = sem("ada_done")
        area3 = sem("area3")
        nf_dram = nc.dram_tensor("nf_rows", [16, T], F32).ap()

        def fz_pe(pe):
            pe.wait_ge(h_sc, 8 * HG)
            project(pe, U_FZ, 0, u_hi, u_lo, [(slice(c * CH, c * CH + CH), bank(2 + c), []) for c in range(2)], h_chunk)
            pe.wait_ge(w_ready, U_FZ + 2)
            pe.drain().then_inc(w_used, 1)

        def fz_act_part(act):
            act.wait_ge(h_spill, 32 * (HG + 1))
            act.dma_start(fb[:], a["fox_fb"]).then_inc(fb_loaded, 16)
            for i in range(2):
                act.dma_start(cond[:, i, :], a["cond"][i:i + 1, :].broadcast_to([P, D])).then_inc(fb_loaded, 16)
            act.wait_ge(h_chunk, 4 * HG + 1)
            act.wait_ge(w_used, U_FZ + 1)
            act.wait_ge(fb_loaded, 48)
            r = slice(0, 16)
            nc.scalar.activation(nf_t[r], ps[r, 2 * CH:2 * CH + T], ACT.Identity, bias=fb[:, 0:1])
            nc.scalar.activation(nf[r], ps[r, 2 * CH:2 * CH + T], ACT.Abs, bias=fb[:, 0:1])
            act.drain()
            nc.scalar.activation(nf[r], nf[r], ACT.Exp, scale=-1.0)
            act.drain()
            nc.scalar.activation(nf[r], nf[r], ACT.Ln, bias=1.0).then_inc(fz_act, 1)
            nc.scalar.activation(cond[:].rearrange("p a b -> p (a b)"), cond[:].rearrange("p a b -> p (a b)"),
                                 ACT.Silu).then_inc(cond_set, 1)
            act.wait_ge(fz_done, 1)
            act.dma_start(nf_dram, nf[r]).then_inc(nf_stored, 16)
            act.wait_ge(nf_stored, 16)

        def fz_dve(dve):
            dve.wait_ge(h_spill, 32 * (HG + 1))
            dve.memset(nf_b[0:16, 0, :], 1.0)
            dve.drain().then_inc(area3, 1)
            dve.wait_ge(fz_act, 1)
            r = slice(0, 16)
            dve.scalar_tensor_tensor(nf_t[r], nf_t[r], 0.0, nf[r], ALU.min, ALU.subtract)
            dve.drain()
            dve.tensor_tensor_scan(nf[r], nf_b[r, 0, :], nf_t[r], 0.0, ALU.mult, ALU.subtract)
            dve.drain().then_inc(fz_done, 1)

        def fox_pe(pe):
            with pe.Fori(0, PAIRS) as it:
                n = it * 4 + U_FOX

                def unit(j, b, waits):
                    project(pe, n + j, j % 2, u_hi, u_lo,
                            [(slice(c * CH, c * CH + CH), bank(b + c), waits if c == 0 else []) for c in range(2)],
                            fox.chunk)

                unit(0, 0, [(fox.shifted, it * fox.NA)])
                unit(1, 2, [(fz_act, 1)])
                unit(2, 4, fox.all_copied(it) + [(h_on, HG)])
                unit(3, 6, [(fox.left, it * fox.NB), (h_yt, HG + 1)])
                pe.wait_ge(f_v, it + 1)
                for j in range(8):
                    mm = pe.transpose(ps[:, 4 * CH + j * P:4 * CH + (j + 1) * P], fx_vt[:, j * P:(j + 1) * P], ident)
                mm.then_inc(f_vt, 1)
                fox.pe(pe, it, fx_k2a, fx_k2b, [(fx_v, rows_of(hd)) for hd in range(2)],
                       {("S", 0): [(f_lo, it * 2 + 2)],
                        ("T", 0): [(f_vc, it + 1)],
                        ("V", 0): [(f_g, it + 1)]})

        def fox_act(act):
            act.wait_ge(area3, 1)
            with act.Fori(0, PAIRS) as it:
                act.wait_ge(fox.shifted, it * fox.NA)
                for hd in range(2):
                    act.dma_start(nf_b[:, hd, :], nf_dram[ds(it * 2 + hd, 1), :].broadcast_to([P, T])
                                  ).then_inc(nf_loaded, 16)

                def load_ada(half):
                    act.wait_ge(ada_done, it * 2 + half)
                    for j in range(3):
                        act.dma_start(ada_w[:, j, :], a["w_ada"][ds(it * 6 + (3 * half + j), 1)
                                                                 ].rearrange("a p n -> (a p) n")
                                      ).then_inc(ada_loaded, 16)

                load_ada(0)
                act.wait_ge(fox.chunk, it * 4 + 1)
                act.wait_ge(w_used, it * 4 + (U_FOX + 1))
                for hd in range(2):
                    ins = nc.scalar.activation(fox.q2[hd][0:HD, :], bank(0, 2)[rows_of(hd)], ACT.Copy, scale=HD ** -0.5)
                ins.then_inc(f_hi, 1)
                act.wait_ge(fox.chunk, it * 4 + 2)
                act.wait_ge(w_used, it * 4 + (U_FOX + 2))
                for hd in range(2):
                    for half in range(2):
                        ins = nc.scalar.copy(fx_k2a[hd][rows_of(half), :], bank(2, 2)[rows_of(hd)])
                ins.then_inc(f_hi, 1)
                load_ada(1)
                act.wait_ge(fox.chunk, it * 4 + 3)
                act.wait_ge(w_used, it * 4 + (U_FOX + 3))
                nc.scalar.copy(fx_vt[:], bank(4, 2)).then_inc(f_v, 1)
                act.wait_ge(fox.chunk, it * 4 + 4)
                act.wait_ge(w_used, it * 4 + (U_FOX + 4))
                nc.scalar.activation(fox.silu[:], bank(6, 2), ACT.Silu).then_inc(f_g, 1)
                act.wait_ge(f_vt, it + 1)
                nc.scalar.copy(fx_v[:].rearrange("p j t -> p (j t)"), bank(4, 2)).then_inc(f_vc, 1)
                fox.act(act, it)
                fox.finish_act(act, it, it + (1 + HG), T)

        def fox_dve(dve):
            dve.wait_ge(cond_set, 1)
            with dve.Fori(0, PAIRS) as it:
                dve.wait_ge(fox.turned, it * fox.NG)

                def dot_ada(half):
                    for j in range(3):
                        for i in range(2):
                            k = 6 * half + 2 * j + i
                            dve.wait_ge(ada_loaded, it * 96 + 48 * (half + 1))
                            dve.memset(ada_acc[:, k:k + 1], 0.0)
                            dve.drain()
                            ins = dve.tensor_tensor_reduce(fox.l[:, i, :], ada_w[:, j, :], cond[:, i, :], 1.0,
                                                           ada_acc[:, k:k + 1], ALU.mult, ALU.add,
                                                           ada_acc[:, k:k + 1])
                    ins.then_inc(ada_done, 1)

                dot_ada(0)
                dve.wait_ge(f_hi, it * 2 + 1)
                for hd in range(2):
                    ins = dve.scalar_tensor_tensor(fox.q2[hd][HD:P, :], bank(0, 2)[rows_of(hd)], HD ** -0.5,
                                                   fox.q2[hd][0:HD, :].bitcast(F32), ALU.mult, ALU.subtract)
                ins.then_inc(f_lo, 1)
                dve.wait_ge(f_hi, it * 2 + 2)
                for hd in range(2):
                    for half in range(2):
                        ins = dve.tensor_tensor(fx_k2b[hd][rows_of(half), :], bank(2, 2)[rows_of(hd)],
                                                fx_k2a[hd][0:HD, :].bitcast(F32), ALU.subtract)
                ins.then_inc(f_lo, 1)
                dot_ada(1)
                dve.drain()
                dve.tensor_copy(ada[:].rearrange("p u i -> p (u i)")[:, ds(it * 12, 12)], ada_acc[:])
                dve.drain()
                dve.wait_ge(nf_loaded, it * 32 + 32)

                for hd in range(2):
                    dve.tensor_tensor(nf_tri[:, hd, :].rearrange("p (b t) -> p b t", t=P),
                                      nf_b[:, hd, :].rearrange("p (b t) -> p b t", t=P),
                                      consts[:, K_TRI:K_TRI + P].unsqueeze(1).broadcast_to([P, 8, P]), ALU.add)

                def masks(u):
                    b, hd = FOX_ORDER[u // 2], u % 2
                    dve.memset(fox.mark[:, u:u + 1], 0.0)
                    return (([(0, b * P, nf_b[:, hd, 0:b * P])] if b else [])
                            + [(b * P, P, nf_tri[:, hd, b * P:(b + 1) * P])])

                fox.dve(dve, it, lambda nm: dve.memset(nm, 3e38), masks)
                fox.finish_dve(dve, it)

        block1.close()
        ph4 = ctx.enter_context(ExitStack())
        y_parts = [(sb(f"y_hi{i}", [P, KT, T], F32R, ph4), sb(f"y_lo{i}", [P, KT, T], F32R, ph4)) for i in range(2)]
        h_area = ctx.enter_context(ExitStack())
        h_sb = sb("h_sb", [P, KT, T], at=h_area)
        x_in = sb("x_in", [P, 2, T], at=h_area)
        ctx_in = sb("ctx_in", [P, KT, C], at=h_area)
        assert 2 * T == KT * C
        p_in = ctx_in[:].rearrange("p k t -> p (k t)")
        h_area.close()
        ph4.close()
        y4_loaded = [sem("y4_loaded_hgrn"), sem("y4_loaded_fox")]
        x4_loaded = sem("x4_loaded")
        o_chunk = sem("o_chunk")
        o_added = sem("o_added")

        ph4b = ctx.enter_context(ExitStack())
        r_hi = sb("r_hi", [P, KT, T], F32R, ph4b)
        r_lo = sb("r_lo", [P, KT, T], F32R, ph4b)
        ple = sb("ple", [P, KT, T], at=ph4b)
        p_hi = sb("p_hi", [P, 2, T], F32R, ph4b)
        p_lo = sb("p_lo", [P, 2, T], F32R, ph4b)
        sig = sb("sig", [P, 1, T], at=ph4b)
        sq4 = sb("sq4", [P, T], at=ph4b)
        acc4 = sb("acc4", [P, T], at=ph4b)
        ph4b.close()
        p_loaded = sem("p_loaded")
        p_hi_set = sem("p_hi_set")
        p_lo_set = sem("p_lo_set")
        h_hi_set = sem("h_hi_set")
        h_lo_set = sem("h_lo_set")
        ple_chunk = sem("ple_chunk")
        ple_done = sem("ple_done")
        g_chunk = sem("g_chunk")
        g_sig = sem("g_sig")
        g_added = sem("g_added")

        def two_chunks(b, waits):
            return [(slice(c * CH, c * CH + CH), bank(b + c), waits if c == 0 else []) for c in range(2)]

        def load_hgrn_parts(sp):
            sp.wait_ge(w_used, U_OUT)
            sp.wait_ge(h_spill, 32 * (HG + 1))
            for k in range(KT):
                for part in range(2):
                    sp.dma_start(y_parts[0][part][:, k, :].bitcast(F32), y_dram[part, 1 + k, :, 0:T]
                                 ).then_inc(y4_loaded[0], 16)

        def out1_pe(pe):
            with pe.Fori(0, 2) as i:
                for r in range(2):
                    pe.wait_ge(y4_loaded[r], 16 * 16)
                    for m in range(4):
                        free = [(o_added, i * (m + 1)), (fox.left, PAIRS * fox.NB)] + fox.all_copied(PAIRS)
                        project(pe, i * 8 + (U_OUT + 4 * r + m), m % 2, *y_parts[r],
                                two_chunks(2 * m, [] if r else free), o_chunk, start=r == 0, stop=r == 1)

        def out1_act(act):
            act.wait_ge(fox.spilled, 32 * PAIRS)
            act.wait_ge(fox.valued, PAIRS * fox.NV)
            for k in range(KT):
                for part in range(2):
                    act.dma_start(y_parts[1][part][:, k, :].bitcast(F32), y_dram[part, 1 + HG + k, :, 0:T]
                                  ).then_inc(y4_loaded[1], 16)
            act.dma_start(p_in, a["p_t"].rearrange("p s t -> p (s t)")).then_inc(p_loaded, 16)
            with act.Fori(0, KT // 2) as i:
                for m in range(2):
                    act.wait_ge(o_added, i * 2)
                    act.dma_start(x_in[:, m, :], a["x_t"][:, ds(i * 2 + m, 1), :].rearrange("p a t -> p (a t)")
                                  ).then_inc(x4_loaded, 16)

        def out1_dve(dve):
            with dve.Fori(0, 2) as i:
                for m in range(4):
                    dve.wait_ge(x4_loaded, i * 64 + (32 * (m // 2) + 32))
                    dve.wait_ge(o_chunk, i * 8 + (4 + m + 1))
                    dve.wait_ge(w_used, i * 8 + (U_OUT + 4 + m + 1))
                    dve.tensor_tensor(h_sb[:, ds(i * 4 + m, 1), :].rearrange("p a t -> p (a t)"),
                                      bank(2 * m, 2), x_in[:, m % 2, :], ALU.add).then_inc(o_added, 1)

        def ple_pe(pe):
            pe.wait_ge(p_lo_set, 1)
            for half in range(2):
                for m in range(4):
                    j = 4 * half + m
                    free = [(ple_done, j - 1)] if j >= 2 else [(o_added, KT)]
                    project(pe, U_PLE + half, half, p_hi, p_lo, two_chunks(2 * (m % 2), free), ple_chunk,
                            tiles=(2 * m, 2 * m + 1), last=m == 3)

        def gate_pe(pe):
            pe.wait_ge(h_lo_set, KT)
            pe.wait_ge(ple_done, KT)
            with pe.Fori(0, KT // 2) as i:
                for m in range(2):
                    free = [(g_sig, i * 2 + (m - 1))] if m else [(g_sig, i * 2)]
                    project(pe, i * 2 + (U_GATE + m), m, r_hi, r_lo, two_chunks(2 * m, free), g_chunk)

        def ple_act(act):
            act.wait_ge(w_used, U_OUT + 12)
            for k in range(KT):
                if k == KT - 1:
                    act.wait_ge(o_added, KT)
                    act.wait_ge(p_loaded, 16)
                    nc.scalar.copy(p_hi[:].rearrange("p s t -> p (s t)"), p_in).then_inc(p_hi_set, 1)
                act.wait_ge(o_added, k + 1)
                nc.scalar.copy(r_hi[:, k, :], h_sb[:, k, :]).then_inc(h_hi_set, 1)
            act.wait_ge(p_lo_set, 1)
            act.dma_start(ctx_in[:], a["ctx_t"]).then_inc(ctx_loaded, 16)
            for m in range(KT):
                act.wait_ge(ple_chunk, 2 * (m + 1) - (m + 1) // 4)
                act.wait_ge(w_used, U_PLE + (m + 1) // 4)
                nc.scalar.copy(ple[:, m, :], bank(2 * (m % 2), 2)).then_inc(ple_done, 1)
            with act.Fori(0, KT // 2) as i:
                for m in range(2):
                    act.wait_ge(g_chunk, i * 2 + (m + 1))
                    act.wait_ge(w_used, i * 2 + (U_GATE + m + 1))
                    nc.scalar.activation(sig[:, 0, :], bank(2 * m, 2), ACT.Sigmoid).then_inc(g_sig, 1)
                    act.wait_ge(g_added, i * 2 + (m + 1))
                    act.wait_ge(n4_acc, i * 2 + m)
                    nc.scalar.activation(sq4[:], h_sb[:, ds(i * 2 + m, 1), :].rearrange("p a t -> p (a t)"),
                                         ACT.Square).then_inc(n4_sq, 1)

        def ple_dve(dve):
            dve.wait_ge(p_hi_set, 1)
            dve.tensor_tensor(p_lo[:].rearrange("p s t -> p (s t)"), p_in,
                              p_hi[:].bitcast(F32).rearrange("p s t -> p (s t)"), ALU.subtract).then_inc(p_lo_set, 1)
            for k in range(KT):
                dve.wait_ge(h_hi_set, k + 1)
                dve.tensor_tensor(r_lo[:, k, :], h_sb[:, k, :], r_hi[:, k, :].bitcast(F32),
                                  ALU.subtract).then_inc(h_lo_set, 1)
            dve.wait_ge(ple_done, KT)
            dve.memset(acc4[:], 0.0)
            with dve.Fori(0, KT // 2) as i:
                for m in range(2):
                    dve.wait_ge(g_sig, i * 2 + (m + 1))
                    row = lambda t: t[:, ds(i * 2 + m, 1), :].rearrange("p a t -> p (a t)")
                    dve.tensor_tensor(sig[:, 0, :], sig[:, 0, :], row(ple), ALU.mult)
                    dve.drain()
                    dve.tensor_tensor(row(h_sb), row(h_sb), sig[:, 0, :], ALU.add).then_inc(g_added, 1)
                    dve.wait_ge(n4_sq, i * 2 + (m + 1))
                    dve.tensor_tensor(acc4[:], acc4[:], sq4[:], ALU.add).then_inc(n4_acc, 1)

        ph4c = ctx.enter_context(ExitStack())
        diag4 = sb("diag4", [P, T], at=ph4c)
        ph4c.close()
        n4_sq = sem("n4_sq")
        n4_acc = sem("n4_acc")
        n4_mean = sem("n4_mean")
        n4_h = sem("n4_h")
        h_stored = sem("h_stored")
        ctx_loaded = sem("ctx_loaded")

        def norm4_act(act):
            act.wait_ge(n4_mean, 1)
            standard_deviations(act, T, 4, small[:, 1:2])

        def store_h3(act):
            for k in range(KT):
                act.wait_ge(n4_h, k + 1)
                act.dma_start(h_dram[k, :, 0:T], h_sb[:, k, :]).then_inc(h_stored, 16)
            act.wait_ge(ctx_loaded, 16)
            act.dma_start(h_dram[:, :, T:TC].rearrange("k p t -> p k t"), ctx_in[:]).then_inc(h_stored, 16)

        def norm4_pe(pe):
            pe.wait_ge(n4_acc, KT)
            token_means(pe, acc4, T, 4, 0, 1).then_inc(n4_mean, 1)
            spread_rows(pe, T, diag4, 6, 2)

        def norm4_dve(dve):
            inverse_diagonals(dve, T, diag4, 2)
            dve.wait_ge(stat_row, 2)

        def scale_h3(dve):
            for k in range(KT):
                dve.scalar_tensor_tensor(h_sb[:, k, :], h_sb[:, k, :], vecs[:, V_FINAL + k:V_FINAL + k + 1],
                                         bank(6, 2), ALU.mult, ALU.mult).then_inc(n4_h, 1)


        def ada_dve(dve):
            dve.tensor_tensor(adv[:], ada[:], vecs[:, V_BADA:V_BADA + ADA_UNITS].unsqueeze(2)
                              .broadcast_to([P, ADA_UNITS, 2]), ALU.add)
            dve.memset(gates[:, 0, :, 2], 0.0)
            dve.tensor_scalar(gates[:, 1, :, 2], vecs[:, V_LNB:V_LNB + KT], ALPHA, None, ALU.mult)
            dve.drain()
            for l in range(2):
                dve.tensor_scalar(mod_g[:, l], adv[:, 24 * l + 8:24 * l + 16, :], 1.0, None, ALU.add)
                dve.tensor_copy(gates[:, l, :, 0:2], adv[:, 24 * l + 16:24 * l + 24, :])
            dve.drain()
            dve.tensor_copy(mod_shift[:, 0], adv[:, 0:8, :])
            dve.tensor_tensor(mod_shift[:, 1], mod_g[:, 1], vecs[:, V_LNB:V_LNB + KT].unsqueeze(2)
                              .broadcast_to([P, KT, 2]), ALU.mult)
            dve.drain()
            dve.tensor_tensor(mod_shift[:, 1], mod_shift[:, 1], adv[:, 24:32, :], ALU.add)
            dve.tensor_tensor(mod_g[:, 0, :, 0], mod_g[:, 0, :, 0], vecs[:, V_FINAL:V_FINAL + KT], ALU.mult)
            dve.tensor_tensor(mod_g[:, 1], mod_g[:, 1], vecs[:, V_LNG:V_LNG + KT].unsqueeze(2)
                              .broadcast_to([P, KT, 2]), ALU.mult)
            dve.drain()

        class Layer:

            def __init__(self, l, name, n_out, cols, first=None):
                self.l, self.name, self.n_out, self.cols, self.base = l, name, n_out, cols, l * KT
                self.chunks = [(0, CH), (CH, CH), (T, C)][:3 if cols == TC else 2]
                area = ctx.enter_context(ExitStack())
                self.yh = sb(f"{name}_out_yh", [P, KT, cols], F32R, area)
                self.yl = sb(f"{name}_out_yl", [P, KT, cols], F32R, area)
                self.acc = sb(f"{name}_acc", [P, cols], at=area)
                self.res = sb(f"{name}_res", [P, 2, cols], at=area)
                self.gate = sb(f"{name}_gate", [P, 2, 3], at=area)
                self.tmp = sb(f"{name}_tmp", [P, 1, cols], at=area)
                sb(f"{name}_gap", [P, 26 * 256], at=area)
                self.u = sb(f"{name}_u", [P, 2, T], at=area)
                self.h = sb(f"{name}_h", [P, KT, cols], at=area)
                area.close()
                area = ctx.enter_context(ExitStack())
                self.sq = sb(f"{name}_sq", [P, 2, cols], at=area)
                self.diag = sb(f"{name}_diag", [P, cols], at=area)
                area.close()
                for what in () if first else ("y_first", "y_last", "res_loaded", "chunk", "gated", "added", "summed",
                                              "mean_sum", "centred", "sq_set", "sq_sum", "normed"):
                    self.sems[what] = sem(f"layer_{what}")
                s = self.sems
                self.y_first, self.y_last, self.res_loaded = s["y_first"], s["y_last"], s["res_loaded"]
                self.chunk, self.gated, self.added, self.summed = s["chunk"], s["gated"], s["added"], s["summed"]
                self.mean_sum, self.centred, self.sq_set = s["mean_sum"], s["centred"], s["sq_set"]
                self.sq_sum, self.normed = s["sq_sum"], s["normed"]

            sems = {}

            def span(self, b, waits=(), ctx_waits=()):
                return [(slice(t, t + n), ps[:, b * CH + t:b * CH + t + n],
                         {0: list(waits), T: list(ctx_waits)}.get(t, [])) for t, n in self.chunks]

            def flat(self, b):
                return ps[:, b * CH:b * CH + self.cols]

            def load_parts(self, sp, mixer):
                sp.wait_ge(w_used, self.n_out)
                for k in range(KT):
                    sp.wait_ge(mixer.spilled, 32 * (k + 1 if k == KT - 1 else KT - 1))
                    for part, dst in ((0, self.yh), (1, self.yl)):
                        sp.dma_start(dst[:, k, :].bitcast(F32), y_dram[part, k, :, 0:self.cols]
                                     ).then_inc(self.y_last if k == KT - 1 else self.y_first, 16)

            def pe(self, pe, mixer):
                def ready(k):
                    return ((self.y_last, 32 * (self.l + 1)) if k == KT - 1 else
                            (self.y_first, 32 * (KT - 1) * (self.l + 1)))

                for s, v in mixer.all_copied(PAIRS) + [(mixer.left, PAIRS * mixer.NB)]:
                    pe.wait_ge(s, v)
                with pe.Fori(0, KT // 2) as i:
                    for m in range(2):
                        project(pe, i * 2 + (self.n_out + m), m, self.yh, self.yl,
                                self.span(3 * m, [(self.gated, i * 2 + (self.base + max(m - 1, 0)))]), self.chunk,
                                ready=ready, tiles_outer=m == 0)
                pe.wait_ge(self.summed, self.base + KT)
                for t, w in self.chunks:
                    mm = pe.matmul(ps[:, 3 * CH + t:3 * CH + t + w], ones_mean[:], self.acc[:, t:t + w],
                                   start=True, stop=True)
                mm.then_inc(self.mean_sum, 1)
                for k in range(KT):
                    pe.wait_ge(self.sq_set, self.base + k + 1)
                    token_means(pe, self.sq[:, k % 2, :], self.cols, 6, k).then_inc(self.sq_sum, 1)
                spread_rows(pe, self.cols, self.diag, 0, 3 + self.l)

            def act(self, act, mixer):
                act.wait_ge(mixer.spilled, 32 * PAIRS)
                act.wait_ge(mixer.valued, PAIRS * mixer.NV)
                with act.Fori(0, KT // 2) as i:
                    for m in range(2):
                        act.wait_ge(self.added, i * 2 + self.base)
                        act.dma_start(self.res[:, m, :], h_dram[ds(i * 2 + m, 1), :, 0:self.cols]
                                      .rearrange("a p t -> (a p) t")).then_inc(self.res_loaded, 16)
                for k in range(KT):
                    act.wait_ge(self.centred, self.base + k + 1)
                    if k >= 2:
                        act.wait_ge(self.sq_sum, self.base + k - 1)
                    nc.scalar.activation(self.sq[:, k % 2, :], self.h[:, k, :], ACT.Square).then_inc(self.sq_set, 1)
                act.wait_ge(self.sq_sum, self.base + KT)
                standard_deviations(act, self.cols, 6, small[:, 2:3])

            def dve(self, dve):
                l = self.l
                dve.memset(self.acc[:], 0.0)
                with dve.Fori(0, KT // 2) as i:
                    for m in range(2):
                        dve.tensor_copy(self.gate[:, m, :],
                                        gates[:, l, ds(i * 2 + m, 1), :].rearrange("p a i -> p (a i)"))
                        dve.drain()
                        dve.wait_ge(self.chunk, (i * 2 + (m + 1)) * (len(self.chunks) - 1) + 2 * self.base)
                        dve.wait_ge(w_used, i * 2 + (self.n_out + m + 1))
                        ins = dve.tensor_scalar(self.tmp[:, 0, 0:T], ps[:, 3 * m * CH:3 * m * CH + T],
                                                self.gate[:, m, 0:1], self.gate[:, m, 2:3], ALU.mult, ALU.add)
                        if self.cols > T:
                            ins = dve.tensor_scalar(self.tmp[:, 0, T:], ps[:, 3 * m * CH + T:3 * m * CH + TC],
                                                    self.gate[:, m, 1:2], None, ALU.mult)
                        ins.then_inc(self.gated, 1)
                        dve.drain()
                        dve.wait_ge(self.res_loaded, i * 32 + (16 * self.base + 32))
                        tile_h = self.h[:, ds(i * 2 + m, 1), :].rearrange("p a t -> p (a t)")
                        dve.scalar_tensor_tensor(tile_h, self.res[:, m, :], ALPHA, self.tmp[:, 0, :],
                                                 ALU.mult, ALU.add).then_inc(self.added, 1)
                        dve.drain()
                        dve.tensor_tensor(self.acc[:], self.acc[:], tile_h, ALU.add).then_inc(self.summed, 1)
                dve.wait_ge(self.mean_sum, l + 1)
                for k in range(KT):
                    dve.tensor_tensor(self.h[:, k, :], self.h[:, k, :], self.flat(3), ALU.subtract
                                      ).then_inc(self.centred, 1)
                inverse_diagonals(dve, self.cols, self.diag, 3 + l)
                dve.wait_ge(stat_row, 3 + l)

            def scale(self, dve):
                for k in range(KT):
                    dve.scalar_tensor_tensor(self.h[:, k, 0:T], self.h[:, k, 0:T],
                                             vecs[:, V_LNG + 8 * self.l + k:V_LNG + 8 * self.l + k + 1],
                                             ps[:, 0:T], ALU.mult, ALU.mult).then_inc(self.normed, 1)

        class Modulated:

            def __init__(self, l, name, u, source, rows, first=None):
                self.l, self.u, self.source, self.rows = l, u, source, rows
                self.area = ctx.enter_context(ExitStack())
                self.hi = sb(f"{name}_u_hi", [P, KT, TC], F32R, self.area)
                self.lo = sb(f"{name}_u_lo", [P, KT, TC], F32R, self.area)
                self.base = l * 2 * KT
                if first is None:
                    self.made = sem("u_made")
                    self.hi_set = sem("u_hi_set")
                    self.lo_set = sem("u_lo_set")
                else:
                    self.made, self.hi_set, self.lo_set = first.made, first.hi_set, first.lo_set

            def ready(self, k):
                return self.lo_set, self.base + k + 1

            def ctx_ready(self):
                return self.lo_set, self.base + 2 * KT

            def part(self, i):
                return (slice(0, T), slice(T, TC))[i]

            def act(self, act, i):
                for k in range(KT):
                    s = i * KT + k
                    act.wait_ge(self.made, self.base + s + 1)
                    n = (T, C)[i]
                    nc.scalar.activation(self.hi[:, k, self.part(i)], self.u[:, s % 2, 0:n], ACT.Identity,
                                         bias=mod_shift[:, self.l, k, i:i + 1]).then_inc(self.hi_set, 1)

            def dve(self, dve, i):
                n = (T, C)[i]

                def low(k):
                    s = i * KT + k
                    dve.wait_ge(self.hi_set, self.base + s + 1)
                    dve.scalar_tensor_tensor(self.lo[:, k, self.part(i)], self.u[:, s % 2, 0:n],
                                             mod_shift[:, self.l, k, i:i + 1], self.hi[:, k, self.part(i)].bitcast(F32),
                                             ALU.add, ALU.subtract).then_inc(self.lo_set, 1)
                for k in range(KT):
                    g = mod_g[:, self.l, k, i:i + 1]
                    dve.drain()
                    u, rows = self.u[:, k % 2, 0:n], self.rows(i)
                    if rows is None:
                        ins = dve.tensor_scalar(u, self.source(k, i), g, None, ALU.mult)
                    else:
                        ins = dve.scalar_tensor_tensor(u, self.source(k, i), g, rows, ALU.mult, ALU.mult)
                    ins.then_inc(self.made, 1)
                    if k:
                        low(k - 1)
                low(KT - 1)

        mod_a = Modulated(0, "wa", x_in, lambda k, i: ctx_in[:, k, :] if i else h_sb[:, k, :],
                          lambda i: None if i else bank(6, 2))

        def window_block(b):
            if b >= 8:
                lo, hi = 0, 0
            else:
                lo, hi = max(b - 1, 0), min(b + 2, 8)
            n = (hi - lo) * P
            runs = [(CH - n, lo * P, n)] if n else []
            runs.append((CH, T, C))
            chunks = [(c * P, P, lo + c) for c in range(hi - lo)] + [(n + c * P, P, 8 + c) for c in range(2)]
            return {"b": b, "width": n + C + 1, "first": CH - n, "runs": runs, "chunks": chunks, "lat": n}

        ph6 = ctx.enter_context(ExitStack())
        rope = sb("rope", [P, 2, T], at=ph6)
        wa_k2a = [sb(f"wa_k2a{i}", [P, TC], F32R, ph6) for i in range(2)]
        wa_k2b = [sb(f"wa_k2b{i}", [P, TC], F32R, ph6) for i in range(2)]
        wa_v = sb("wa_v", [P, 10, P], at=ph6)
        nsink = sb("nsink", [P, 16], at=ph6)
        head_sink = sb("head_sink", [P, 2], at=ph6)
        wa = Attention("wa", [window_block(b) for b in range(10)], [[0, 1, 2, 3], [4, 5, 6, 7], [8, 9]],
                       3 * P + C + 1, TC, TC, ph6)
        ph6.close()
        wa_vt = wa.y_lo[:].bitcast(F32)
        wa_shuf = wa.silu[:, 0:T]
        a_loaded = sem("a_loaded")
        a_set = sem("a_set")
        a_copied = sem("a_copied")
        a_turned = sem("a_turned")
        a_hi = sem("a_hi")
        a_lo = sem("a_lo")
        a_vt = sem("a_vt")
        a_vc = sem("a_vc")
        a_g = sem("a_g")

        def wa_pe(pe):
            with pe.Fori(0, 2) as j:
                def unit(i, b, waits):
                    project(pe, j * 10 + (U_A + i), i % 2, mod_a.hi, mod_a.lo,
                            layer_a.span(b, waits, [mod_a.ctx_ready()]), wa.chunk, ready=mod_a.ready)

                unit(0, 0, [(wa.shifted, j * (4 * wa.NA))])
                unit(1, 3, wa.all_copied(j * 4))
                pe.wait_ge(n4_h, KT)
                pe.wait_ge(a_copied, j * 6 + 2)
                for t in range(10):
                    mm = pe.transpose(ps[:, t * P:(t + 1) * P], wa_vt[:, t * P:(t + 1) * P], ident)
                mm.then_inc(a_vt, 1)
                for g in range(4):
                    it = j * 4 + g
                    unit(2 + 2 * g, 0, [(wa.shifted, it * wa.NA), (a_vc, j + 1)])
                    unit(3 + 2 * g, 3, wa.all_copied(it))
                    wa.pe(pe, it, [wa_k2a[g // 2]] * 2, [wa_k2b[g // 2]] * 2, [(wa_v, rows_of(g // 2))] * 2,
                          {("S", 0): [(a_lo, j * 5 + (g + 2))],
                           ("S", 1): [(a_g, it + 1)]})

        def load_tables(act):
            act.dma_start(rope[:], a["rope"]).then_inc(a_loaded, 16)
            act.dma_start(nsink[:], a["a_sink"].broadcast_to([P, 16])).then_inc(a_loaded, 16)

        def wa_act(act):
            with act.Fori(0, 2) as j:
                def copied(i, b, scale=1.0, to=wa.y[:]):
                    act.wait_ge(wa.chunk, j * 20 + 2 * (i + 1))
                    act.wait_ge(w_used, j * 10 + (U_A + i + 1))
                    return nc.scalar.activation(to, layer_a.flat(b), ACT.Copy, scale=scale
                                                ).then_inc(a_copied, 1)

                copied(0, 0)
                act.wait_ge(h_stored, 16 * (KT + 1))
                act.wait_ge(wa.spilled, j * (32 * 4))
                copied(1, 3, to=wa_vt)
                act.wait_ge(a_vt, j + 1)
                nc.scalar.copy(wa_v[:], ps[:, 0:TC].rearrange("p (j t) -> p j t", t=P)).then_inc(a_vc, 1)
                act.wait_ge(a_turned, j * 5 + 1)
                for kk in range(2):
                    for half in range(2):
                        ins = nc.scalar.copy(wa_k2a[kk][rows_of(half), :], wa.y[rows_of(kk), :])
                ins.then_inc(a_hi, 1)
                act.wait_ge(a_lo, j * 5 + 1)
                for g in range(4):
                    it = j * 4 + g
                    copied(2 + 2 * g, 0, HD ** -0.5)
                    act.wait_ge(a_turned, j * 5 + (g + 2))
                    for hd in range(2):
                        ins = nc.scalar.copy(wa.q2[hd][rows_of(hd), :], wa.y[rows_of(hd), :])
                    ins.then_inc(a_hi, 1)
                    act.wait_ge(wa.chunk, j * 20 + 2 * (4 + 2 * g))
                    act.wait_ge(w_used, j * 10 + (U_A + 4 + 2 * g))
                    nc.scalar.activation(wa.silu[:], layer_a.flat(3), ACT.Silu).then_inc(a_g, 1)
                    wa.act(act, it)
                    wa.finish_act(act, it, it, TC)

        def wa_dve(dve):
            dve.wait_ge(a_loaded, 32)
            dve.tensor_scalar(nsink[:], nsink[:], -1.0, None, ALU.mult)
            dve.drain().then_inc(a_set, 1)
            with dve.Fori(0, 2) as j:
                def rotate(i, n, it):
                    dve.drain()
                    dve.wait_ge(wa.turned, it * wa.NG)
                    dve.wait_ge(a_copied, j * 6 + i)
                    dve.tensor_copy(head_sink[:], nsink[:, ds(n, 2)])
                    dve.stream_shuffle(wa_shuf, wa.y[:, 0:T], [(x + 16) % 32 for x in range(32)])
                    dve.drain()
                    dve.tensor_tensor(wa.y[:, 0:T], wa.y[:, 0:T], rope[:, 0, :], ALU.mult)
                    dve.tensor_tensor(wa_shuf, wa_shuf, rope[:, 1, :], ALU.mult)
                    dve.drain()
                    dve.tensor_tensor(wa.y[:, 0:T], wa.y[:, 0:T], wa_shuf, ALU.add).then_inc(a_turned, 1)

                rotate(1, j * 8, j * 4)
                dve.wait_ge(a_hi, j * 5 + 1)
                for kk in range(2):
                    r = rows_of(kk)
                    for half in range(2):
                        ins = dve.tensor_tensor(wa_k2b[kk][rows_of(half), :], wa.y[r, :],
                                                wa_k2a[kk][r, :].bitcast(F32), ALU.subtract)
                ins.then_inc(a_lo, 1)
                for g in range(4):
                    it = j * 4 + g
                    rotate(3 + g, it * 2, it)
                    dve.wait_ge(a_hi, j * 5 + (g + 2))
                    for hd in range(2):
                        r = rows_of(hd)
                        ins = dve.tensor_tensor(wa.q2[hd][rows_of(1 - hd), :], wa.y[r, :],
                                                wa.q2[hd][r, :].bitcast(F32), ALU.subtract)
                    ins.then_inc(a_lo, 1)
                    dve.drain()

                    def masks(u):
                        blk = wa.blocks[u // 2]
                        b, n, w = blk["b"], blk["lat"], blk["width"]
                        dve.tensor_copy(wa.l[:, u % 3, w - 1:w], head_sink[:, u % 2:u % 2 + 1])
                        win = consts[:, K_WIN:K_WIN + 3 * P + C]
                        if b == 7:
                            return [(0, n, win[:, 0:n]), (n, C, win[:, 3 * P:])]
                        return [(0, n + C, win[:, 3 * P - n:])]

                    dve.wait_ge(h_stored, 16 * (KT + 1))
                    wa.dve(dve, it, lambda nm: dve.tensor_copy(nm, head_sink[:].unsqueeze(1).broadcast_to([P, 10, 2])),
                           masks)
                    wa.finish_dve(dve, it)

        mod_a.area.close()
        layer_a = Layer(0, "la", U_A_OUT, TC)
        mod_b = Modulated(1, "nb", layer_a.u, lambda k, i: layer_a.h[:, k, T:TC] if i else layer_a.h[:, k, 0:T],
                          lambda i: ps[:, T:TC] if i else ps[:, 0:T], mod_a)

        def near_block(b):
            rs = min(max(2 * b - 4, 0), 8)
            n = (9 if 2 <= b <= 5 else 8) * GRID_W
            chunks = [(c * P, P, 8 + c) for c in range(2)]
            chunks += [(C + c * P, min(P, n - c * P), rs // 2 + c) for c in range((n + P - 1) // P)]
            return {"b": b, "width": C + n, "first": 0, "chunks": chunks, "first_row": rs - 2 * b,
                    "runs": [(0, T, C), (C, rs * GRID_W, CH - C), (CH, rs * GRID_W + CH - C, n + C - CH)]}

        ph7 = ctx.enter_context(ExitStack())
        nb_k2a = [sb(f"nb_k2a{i}", [P, TC], F32R, ph7) for i in range(2)]
        nb_k2b = [sb(f"nb_k2b{i}", [P, TC], F32R, ph7) for i in range(2)]
        nb_v = sb("nb_v", [P, 10, P], at=ph7)
        nb = Attention("nb", [near_block(b) for b in range(8)], [[0, 1, 2, 3], [4, 5, 6, 7]],
                       C + 9 * GRID_W, T, T, ph7)
        nb_bias = sb("nb_bias", [P, 2, 14 * GRID_W], at=ph7)
        nb_mid = sb("nb_mid", [P, 2, C + 9 * GRID_W], at=ph7)
        ph7.close()
        mod_b.area.close()
        nb_vt = nb.l[:].rearrange("p s w -> p (s w)")[:, 0:TC]
        b_loaded = sem("b_loaded")
        b_hi = sem("b_hi")
        b_lo = sem("b_lo")
        b_v = sem("b_v")
        b_vt = sem("b_vt")
        b_vc = sem("b_vc")
        b_g = sem("b_g")
        layer_b = Layer(1, "lb", U_B_OUT, T, layer_a)

        def nb_pe(pe):
            with pe.Fori(0, PAIRS) as it:
                n = it * 4 + U_B
                project(pe, n, 0, mod_b.hi, mod_b.lo, two_chunks(6, [(nb.left, it * nb.NB)]), nb.chunk,
                        ready=mod_b.ready)
                project(pe, n + 1, 1, mod_b.hi, mod_b.lo, layer_a.span(3, nb.all_copied(it), [mod_b.ctx_ready()]),
                        nb.chunk)
                project(pe, n + 2, 0, mod_b.hi, mod_b.lo, layer_a.span(0, [(nb.shifted, it * nb.NA),
                                         (layer_a.normed, KT)]), nb.chunk)
                project(pe, n + 3, 1, mod_b.hi, mod_b.lo, two_chunks(6, [(b_lo, it * 2 + 1)]), nb.chunk)
                pe.wait_ge(b_lo, it * 2 + 2)
                pe.wait_ge(b_v, it + 1)
                for t in range(10):
                    mm = pe.transpose(ps[:, 3 * CH + t * P:3 * CH + (t + 1) * P], nb_vt[:, t * P:(t + 1) * P], ident)
                mm.then_inc(b_vt, 1)
                nb.pe(pe, it, nb_k2a, nb_k2b, [(nb_v, rows_of(hd)) for hd in range(2)],
                      {("S", 1): [(b_vc, it + 1)],
                       ("V", 0): [(b_g, it + 1)]})

        def nb_act(act):
            with act.Fori(0, PAIRS) as it:
                act.wait_ge(nb.shifted, it * nb.NA)
                act.wait_ge(nb.chunk, it * 6 + 1)
                act.wait_ge(w_used, it * 4 + (U_B + 1))
                for hd in range(2):
                    ins = nc.scalar.activation(nb.q2[hd][0:HD, :], bank(6, 2)[rows_of(hd)], ACT.Copy, scale=HD ** -0.5)
                ins.then_inc(b_hi, 1)
                act.wait_ge(nb.chunk, it * 6 + 3)
                act.wait_ge(w_used, it * 4 + (U_B + 2))
                for hd in range(2):
                    for half in range(2):
                        ins = nc.scalar.copy(nb_k2a[hd][rows_of(half), :], layer_a.flat(3)[rows_of(hd)])
                ins.then_inc(b_hi, 1)
                act.wait_ge(b_stored, 16 * KT)
                for hd in range(2):
                    act.dma_start(nb_bias[:, hd, :], a["rel_bias"][ds(it * 2 + hd, 1)].rearrange("a p n -> (a p) n")
                                  ).then_inc(b_loaded, 16)
                act.wait_ge(nb.chunk, it * 6 + 5)
                act.wait_ge(w_used, it * 4 + (U_B + 3))
                nc.scalar.copy(nb_vt, layer_a.flat(0)).then_inc(b_v, 1)
                act.wait_ge(nb.chunk, it * 6 + 6)
                act.wait_ge(w_used, it * 4 + (U_B + 4))
                nc.scalar.activation(nb.silu[:], bank(6, 2), ACT.Silu).then_inc(b_g, 1)
                act.wait_ge(b_vt, it + 1)
                nc.scalar.copy(nb_v[:].rearrange("p j t -> p (j t)"), layer_a.flat(3)).then_inc(b_vc, 1)
                nb.act(act, it)
                nb.finish_act(act, it, it, T)

        def nb_dve(dve):
            with dve.Fori(0, PAIRS) as it:
                dve.wait_ge(b_hi, it * 2 + 1)
                for hd in range(2):
                    ins = dve.scalar_tensor_tensor(nb.q2[hd][HD:P, :], bank(6, 2)[rows_of(hd)], HD ** -0.5,
                                                   nb.q2[hd][0:HD, :].bitcast(F32), ALU.mult, ALU.subtract)
                ins.then_inc(b_lo, 1)
                dve.wait_ge(b_hi, it * 2 + 2)
                for hd in range(2):
                    for half in range(2):
                        ins = dve.tensor_tensor(nb_k2b[hd][rows_of(half), :], layer_a.flat(3)[rows_of(hd)],
                                                nb_k2a[hd][0:HD, :].bitcast(F32), ALU.subtract)
                ins.then_inc(b_lo, 1)
                dve.wait_ge(b_stored, 16 * KT)
                dve.wait_ge(b_loaded, it * 32 + 32)
                for hd in range(2):
                    rows = nb_bias[:, hd, :].rearrange("p (r c) -> p r c", c=GRID_W)
                    dve.tensor_tensor(rows, rows, consts[:, K_COL:K_COL + GRID_W].unsqueeze(1)
                                      .broadcast_to([P, 14, GRID_W]), ALU.add)
                    dve.memset(nb_mid[:, hd, 0:C], 0.0)
                dve.drain()
                for hd in range(2):
                    rows = nb_bias[:, hd, :].rearrange("p (r c) -> p r c", c=GRID_W)[:, 2:11, :]
                    dve.tensor_tensor(nb_mid[:, hd, C:].rearrange("p (r c) -> p r c", c=GRID_W), rows,
                                      consts[:, K_ROW:K_ROW + 9].unsqueeze(2).broadcast_to([P, 9, GRID_W]), ALU.add)
                dve.drain()
                dve.wait_ge(b_vt, it + 1)

                def masks(u):
                    blk, hd = nb.blocks[u // 2], u % 2
                    dve.memset(nb.mark[:, u:u + 1], 0.0)
                    if 2 <= blk["b"] <= 5:
                        return [(0, blk["width"], nb_mid[:, hd, :])]
                    c0 = (blk["first_row"] + 6) * GRID_W
                    return [(0, C, nb_mid[:, hd, 0:C]), (C, CH, nb_bias[:, hd, c0:c0 + CH])]

                nb.dve(dve, it, lambda nm: dve.memset(nm, 3e38), masks)
                nb.finish_dve(dve, it)

        b_stored = sem("b_stored")
        out_stored = sem("out_stored")

        def store_a(act):
            for k in range(KT):
                act.wait_ge(layer_a.normed, k + 1)
                act.dma_start(h_dram[k, :, 0:T], layer_a.h[:, k, 0:T]).then_inc(b_stored, 16)

        def store_b(act):
            for k in range(KT):
                act.wait_ge(layer_b.normed, KT + k + 1)
                nc.scalar.activation(layer_b.h[:, k, :], layer_b.h[:, k, :], ACT.Identity,
                                     bias=vecs[:, V_LNB + KT + k:V_LNB + KT + k + 1])
                act.drain()
                act.dma_start(a["out"][k], layer_b.h[:, k, :]).then_inc(out_stored, 16)
            act.wait_ge(out_stored, 16 * KT)

        block = ctx.enter_context(nc.Block())

        @block.sync
        def _(sp):
            for i in range(4):
                sp.dma_start(x_sb[:, 2 * i:2 * i + 2, :], a["x_t"][:, 2 * i:2 * i + 2, :]).then_inc(x_loaded[i], 16)
            stream_loads(sp)
            sp.dma_start(vecs[:], a["vecs"]).then_inc(loaded, 16)
            sp.dma_start(consts[:], a["consts"]).then_inc(loaded, 16)
            stream_loads_to(sp, 2, U_OUT + 2)
            load_hgrn_parts(sp)
            stream_loads_to(sp, U_OUT + 2, U_A_OUT + 2)
            layer_a.load_parts(sp, wa)
            stream_loads_to(sp, U_A_OUT + 2, U_B_OUT + 2)
            layer_b.load_parts(sp, nb)
            stream_loads_to(sp, U_B_OUT + 2, UNITS)

        @block.gpsimd
        def _(pool):
            stream_splits(pool)

        @block.scalar
        def _(act):
            norm1_act(act)
            hgrn_act(act)
            fz_act_part(act)
            fox_act(act)
            out1_act(act)
            ple_act(act)
            norm4_act(act)
            load_tables(act)
            mod_a.act(act, 0)
            mod_a.act(act, 1)
            store_h3(act)
            wa_act(act)
            layer_a.act(act, wa)
            mod_b.act(act, 0)
            store_a(act)
            mod_b.act(act, 1)
            nb_act(act)
            layer_b.act(act, nb)
            store_b(act)

        @block.tensor
        def _(pe):
            norm1_pe(pe)
            hgrn_pe(pe)
            fz_pe(pe)
            fox_pe(pe)
            out1_pe(pe)
            ple_pe(pe)
            gate_pe(pe)
            norm4_pe(pe)
            wa_pe(pe)
            layer_a.pe(pe, wa)
            nb_pe(pe)
            layer_b.pe(pe, nb)

        @block.vector
        def _(dve):
            norm1_dve(dve)
            hgrn_dve(dve)
            fz_dve(dve)
            fox_dve(dve)
            ada_dve(dve)
            out1_dve(dve)
            ple_dve(dve)
            norm4_dve(dve)
            mod_a.dve(dve, 0)
            dve.wait_ge(ctx_loaded, 16)
            mod_a.dve(dve, 1)
            scale_h3(dve)
            wa_dve(dve)
            layer_a.dve(dve)
            mod_b.dve(dve, 0)
            layer_a.scale(dve)
            mod_b.dve(dve, 1)
            nb_dve(dve)
            layer_b.dve(dve)
            layer_b.scale(dve)


def _tiles(v):
    return v.reshape(-1, P).T


def _unit(w, c0, width=P):
    cols = w[:, c0:c0 + width]
    if cols.shape[1] < width:
        cols = np.concatenate([cols, np.zeros((w.shape[0], width - cols.shape[1]), w.dtype)], 1)
    return cols.reshape(-1, P, width).transpose(1, 0, 2).reshape(P, -1)


def lay_out(x, p, norm_w, w_in, fox_fb, hgrn_gn, hgrn_lb_logits, w_out, w_ple, w_ple_gate, final_norm_w,
            c_2, ctx_2, c_ctx_2, w_ada_2, b_ada_2, ln_g_2, ln_b_2, a_w_in_2, a_w_out_2, a_sink_2,
            b_w_in_2, b_w_out_2, b_rel_bias_2):
    w1, wo, wp, wg = w_in[0], w_out[0], w_ple[0], w_ple_gate[0]
    wa, wao, wb, wbo = a_w_in_2[0], a_w_out_2[0], b_w_in_2[0], b_w_out_2[0]
    units = []
    for h in range(HG):
        units += [_unit(w1, j * D + h * P) for j in (1, 0, 2, 3)]
    units += [_unit(w1, 8 * D)] * 2
    for h in range(PAIRS):
        units += [_unit(w1, (4 + j) * D + h * P) for j in range(4)]
    for half in range(2):
        for rows in (wo[:D], wo[D:]):
            units += [_unit(rows, (4 * half + m) * P) for m in range(4)]
    for half in range(2):
        units.append(np.concatenate([_unit(wp, (4 * half + m) * P) for m in range(4)], 1))
    units += [_unit(wg, m * P) for m in range(KT)]
    for j in range(2):
        units += [_unit(wa, D + j * P), _unit(wa, D + 256 + j * P)]
        for g in range(4):
            units += [_unit(wa, (4 * j + g) * P), _unit(wa, D + 512 + (4 * j + g) * P)]
    units += [_unit(wao, m * P) for m in range(KT)]
    for h in range(PAIRS):
        units += [_unit(wb, j * D + h * P) for j in range(4)]
    units += [_unit(wbo, m * P) for m in range(KT)]
    assert len(units) == UNITS

    s = np.arange(P)
    levels = []
    for lv in range(LEVELS):
        H = 1 << lv
        t = s[s % (2 * H) >= H]
        levels.append((s[:, None] // (2 * H) == t[None] // (2 * H)) & (s[:, None] % (2 * H) < H))
    levels = np.concatenate(levels + [np.eye(P, dtype=bool)], 1)
    consts = np.zeros((P, K_END), np.float32)
    consts[:, K_ID:K_ID + P] = np.eye(P)
    masks = np.zeros((P, 2, T), np.float32)
    masks[:, 0, :levels.shape[1]] = levels
    masks[:, 1] = (np.arange(T) % HGRN_CHUNK != 0)
    consts[:, K_TRI:K_TRI + P] = np.where(s[None] > s[:, None], BIG, 0.0)

    win = consts[:, K_WIN:K_WIN + 640]
    win[:, 0:P] = np.where(s[None] < s[:, None], BIG, 0.0)
    win[:, 2 * P:3 * P] = np.where(s[None] > s[:, None], BIG, 0.0)
    qc, kc, second = s % GRID_W, np.arange(GRID_W), s // GRID_W
    first = np.clip(qc - 8, 0, GRID_W - 16)
    consts[:, K_COL:K_COL + GRID_W] = np.where((kc[None] >= first[:, None]) & (kc[None] < first[:, None] + 16), 0.0, BIG)
    consts[:, K_ROW + 8] = np.where(second == 0, BIG, 0.0)
    consts[:, K_ROW] = np.where(second == 1, BIG, 0.0)
    rows = np.arange(-6, 8)[None, :, None] - second[:, None, None] + 7
    rel_bias = b_rel_bias_2[0][:, rows, np.clip(kc[None, None] - qc[:, None, None] + 15, 0, 30)].reshape(16, P, -1)

    t = np.arange(T)
    inv = (np.float32(10000.0) ** (-np.arange(16, dtype=np.float32) / np.float32(16))).astype(np.float32)
    angles = [(pos.astype(np.float32)[None] * inv[:, None]).astype(np.float32) for pos in (t // GRID_W, t % GRID_W)]
    rope = np.zeros((P, 2, T), np.float32)
    for part in range(4):
        ang = angles[part % 2]
        for b, sign in ((0, -1.0), (1, 1.0)):
            r = slice(32 * part + 16 * b, 32 * part + 16 * b + 16)
            rope[r, 0] = np.cos(ang)
            rope[r, 1] = sign * np.sin(ang)

    vecs = np.concatenate([_tiles(norm_w[0]), _tiles(hgrn_gn[0]), _tiles(final_norm_w),
                           _tiles(ln_g_2.reshape(-1)), _tiles(ln_b_2.reshape(-1)), _tiles(b_ada_2.reshape(-1)),
                           _tiles(hgrn_lb_logits[0])], 1)
    lay = lambda v: np.ascontiguousarray(v)
    return {
        "w_stream": lay(np.stack(units)),
        "vecs": lay(vecs),
        "consts": consts,
        "hgrn_masks": masks,
        "fox_fb": lay(fox_fb[0][:, None]),
        "cond": lay(np.concatenate([c_2, c_ctx_2[None]])),
        "w_ada": lay(w_ada_2.reshape(2, D, 24, P).transpose(0, 2, 3, 1).reshape(ADA_UNITS, P, D)),
        "p_t": lay(p[0, 0].T.reshape(2, P, T).transpose(1, 0, 2)),
        "ctx_t": lay(ctx_2[0].T.reshape(KT, P, C).transpose(1, 0, 2)),
        "rope": rope,
        "rel_bias": lay(rel_bias),
        "a_sink": lay(a_sink_2[0][None]),
        "x_t": lay(x[0].T.reshape(KT, P, T).transpose(1, 0, 2)),
    }


def kernel(**inputs):
    from concourse import bacc
    from concourse.bass_utils import run_bass_kernel_spmd

    arrays = {f"in_{k}": v for k, v in lay_out(**{k: np.asarray(v) for k, v in inputs.items()}).items()}
    nc = bacc.Bacc("TRN2", target_bir_lowering=False, num_devices=1)
    tensors = {k[3:]: nc.dram_tensor(k, v.shape, mybir.dt.from_np(v.dtype), kind="ExternalInput").ap()
               for k, v in arrays.items()}
    tensors["out"] = nc.dram_tensor("out_t", (KT, P, T), F32, kind="ExternalOutput").ap()
    build_program(nc, tensors)
    out = run_bass_kernel_spmd(nc, [arrays], core_ids=[0]).results[0]["out_t"]
    return np.ascontiguousarray(out.reshape(1, D, T).transpose(0, 2, 1))
```
